# Optimizing a Trainium2 kernel written in Bass

```python
import math
import jax, jax.numpy as jnp
from jax import lax
import numpy as np

D_MODEL = 1024
BATCH = 1
SEQ = 512
DEPTH = 1

NSA_HEADS = 8
NSA_KV_GROUPS = 2
NSA_HPG = NSA_HEADS // NSA_KV_GROUPS
NSA_HEAD_DIM = 64
CMP_BLOCK = 32
CMP_STRIDE = 16
CMP_HIDDEN = 256
SLC_BLOCK = 64
SLC_COUNT = 16
WINDOW = 512
Q_BLOCK = 128
ROPE_THETA = 500000.0
ROPE_DIM = NSA_HEAD_DIM // 4
RET_HEADS = 4
RET_HEAD_DIM = 128
RET_CHUNK = 128
RET_ROT_BASE = 10000.0
MLP_HIDDEN = 4 * D_MODEL
NORM_EPS = 1e-6
NEG = -1e30
BIG = 1e30

NSA_Q_W = NSA_HEADS * NSA_HEAD_DIM
NSA_KV_W = NSA_KV_GROUPS * NSA_HEAD_DIM
RET_W = RET_HEADS * RET_HEAD_DIM
IN_SIZES = (NSA_Q_W, NSA_KV_W, NSA_KV_W, NSA_KV_W, NSA_KV_W, NSA_KV_W, NSA_KV_W, 3 * NSA_HEADS,
            RET_W, RET_W, RET_W, RET_W, D_MODEL, D_MODEL)
IN_WIDTH = sum(IN_SIZES)


def rmsnorm(x, g):
    xf = x.astype(jnp.float32)
    y = xf * lax.rsqrt(jnp.mean(xf * xf, axis=-1, keepdims=True) + NORM_EPS) * g.astype(jnp.float32)
    return y.astype(x.dtype)

def rotary(x, pos, rot_dim, base):
    half = rot_dim // 2
    inv = jnp.exp(-math.log(base) * jnp.arange(half, dtype=jnp.float32) * 2.0 / rot_dim)
    ang = pos.astype(jnp.float32)[..., None] * inv
    cos, sin = jnp.cos(ang)[:, :, None, :], jnp.sin(ang)[:, :, None, :]
    xf = x.astype(jnp.float32)
    x1, x2 = xf[..., :half], xf[..., half:rot_dim]
    out = jnp.concatenate([x1 * cos - x2 * sin, x1 * sin + x2 * cos, xf[..., rot_dim:]], axis=-1)
    return out.astype(x.dtype)

def nsa_mixer(q, kc, vc, ks, vs, kw, vw, gates, pe_k, pe_v, ck_w1, ck_w2, cv_w1, cv_w2):
    S = q.shape[0]
    dt = q.dtype
    G, HPG, dh = NSA_KV_GROUPS, NSA_HPG, NSA_HEAD_DIM
    n_cmp = (S - CMP_BLOCK) // CMP_STRIDE + 1
    n_slc = S // SLC_BLOCK
    n_sel = min(SLC_COUNT, n_slc)
    n_qb = S // Q_BLOCK
    scale = dh ** -0.5

    cmp_idx = jnp.arange(n_cmp)[:, None] * CMP_STRIDE + jnp.arange(CMP_BLOCK)[None, :]

    def compress(k, pe, w1, w2):
        blk = k[cmp_idx] + pe[None, :, None, :]
        blk = blk.transpose(0, 2, 1, 3).reshape(n_cmp, G, CMP_BLOCK * dh)
        return jax.nn.silu(blk @ w1) @ w2

    k_cmp = compress(kc, pe_k, ck_w1, ck_w2)
    v_cmp = compress(vc, pe_v, cv_w1, cv_w2)
    cmp_start = cmp_idx[:, 0]
    cmp_end = cmp_idx[:, -1]
    slc_start = jnp.arange(n_slc) * SLC_BLOCK
    overlap = jnp.clip(jnp.minimum(cmp_start[:, None] + CMP_BLOCK, slc_start[None, :] + SLC_BLOCK)
                       - jnp.maximum(cmp_start[:, None], slc_start[None, :]), 0, None)
    overlap = overlap.astype(jnp.float32) / CMP_BLOCK

    ks_b = ks.reshape(n_slc, SLC_BLOCK, G, dh).transpose(2, 0, 1, 3)
    vs_b = vs.reshape(n_slc, SLC_BLOCK, G, dh).transpose(2, 0, 1, 3)
    kw_pad = jnp.pad(kw, ((WINDOW, 0), (0, 0), (0, 0)))
    vw_pad = jnp.pad(vw, ((WINDOW, 0), (0, 0), (0, 0)))

    qg = q.reshape(S, G, HPG, dh)
    gg = jax.nn.sigmoid(gates.astype(jnp.float32)).reshape(S, G, HPG, 3)
    g_idx = jnp.arange(G)[:, None, None]
    blk_j = jnp.arange(n_slc)

    def block(b):
        s0 = b * Q_BLOCK
        qi = lax.dynamic_slice_in_dim(qg, s0, Q_BLOCK, 0)
        gi = lax.dynamic_slice_in_dim(gg, s0, Q_BLOCK, 0)
        t = s0 + jnp.arange(Q_BLOCK)

        sc = jnp.einsum('qghd,cgd->gqhc', qi, k_cmp).astype(jnp.float32) * scale
        valid = cmp_end[None, :] <= t[:, None]
        p_c = jax.nn.softmax(jnp.where(valid[None, :, None, :], sc, NEG), axis=-1)
        p_c = p_c * jnp.any(valid, axis=-1)[None, :, None, None].astype(jnp.float32)
        o_c = jnp.einsum('gqhc,cgd->qghd', p_c.astype(dt), v_cmp)

        imp = jnp.einsum('gqhc,cj->gqj', p_c, overlap)
        cur = t // SLC_BLOCK
        forced = (blk_j[None] == 0) | (blk_j[None] == cur[:, None]) | (blk_j[None] == cur[:, None] - 1)
        future = blk_j[None] > cur[:, None]
        imp = jnp.where(forced[None], BIG, jnp.where(future[None], NEG, imp))
        _, sel = lax.top_k(imp, n_sel)

        k_sel = ks_b[g_idx, sel].reshape(G, Q_BLOCK, n_sel * SLC_BLOCK, dh)
        v_sel = vs_b[g_idx, sel].reshape(G, Q_BLOCK, n_sel * SLC_BLOCK, dh)
        k_pos = (sel[..., None] * SLC_BLOCK + jnp.arange(SLC_BLOCK)).reshape(G, Q_BLOCK, n_sel * SLC_BLOCK)
        ss = jnp.einsum('qghd,gqkd->gqhk', qi, k_sel).astype(jnp.float32) * scale
        smask = (k_pos <= t[None, :, None])[:, :, None, :]
        p_s = jax.nn.softmax(jnp.where(smask, ss, NEG), axis=-1)
        o_s = jnp.einsum('gqhk,gqkd->qghd', p_s.astype(dt), v_sel)

        k_win = lax.dynamic_slice_in_dim(kw_pad, s0, WINDOW + Q_BLOCK, 0)
        v_win = lax.dynamic_slice_in_dim(vw_pad, s0, WINDOW + Q_BLOCK, 0)
        w_pos = s0 - WINDOW + jnp.arange(WINDOW + Q_BLOCK)
        wmask = (w_pos[None] <= t[:, None]) & (w_pos[None] > t[:, None] - WINDOW) & (w_pos[None] >= 0)
        sw = jnp.einsum('qghd,kgd->gqhk', qi, k_win).astype(jnp.float32) * scale
        p_w = jax.nn.softmax(jnp.where(wmask[None, :, None, :], sw, NEG), axis=-1)
        o_w = jnp.einsum('gqhk,kgd->qghd', p_w.astype(dt), v_win)

        o = gi[..., 0:1] * o_c + gi[..., 1:2] * o_s + gi[..., 2:3] * o_w
        return o.reshape(Q_BLOCK, NSA_HEADS * dh).astype(dt)

    out = lax.map(block, jnp.arange(n_qb))
    return out.reshape(S, NSA_HEADS * dh)

def retention(q, k, v, pos):
    B, S = q.shape[0], q.shape[1]
    H, d, C = RET_HEADS, RET_HEAD_DIM, RET_CHUNK
    q = rotary(q, pos, d, RET_ROT_BASE).astype(jnp.float32)
    k = rotary(k, pos, d, RET_ROT_BASE).astype(jnp.float32) * (d ** -0.5)
    v = v.astype(jnp.float32)
    n_c = S // C

    def chunks(a):
        return a.reshape(B, n_c, C, H, d).transpose(1, 0, 3, 2, 4)

    log_g = jnp.log(1.0 - jnp.exp2(-5.0 - jnp.arange(H, dtype=jnp.float32)))
    n = jnp.arange(C, dtype=jnp.float32)
    rel = n[:, None] - n[None, :]
    dmat = jnp.where(rel >= 0, jnp.exp(log_g[:, None, None] * jnp.maximum(rel, 0.0)), 0.0)
    xi = jnp.exp(log_g[:, None] * (n + 1.0))
    zeta = jnp.exp(log_g[:, None] * (C - 1.0 - n))
    chunk_decay = jnp.exp(log_g * C)

    def step(state, inp):
        qc, kc, vc = inp
        inner = jnp.einsum('bhnm,bhme->bhne', jnp.einsum('bhnd,bhmd->bhnm', qc, kc) * dmat, vc)
        cross = jnp.einsum('bhnd,bhde->bhne', qc, state) * xi[None, :, :, None]
        state = chunk_decay[None, :, None, None] * state + jnp.einsum(
            'bhmd,bhme->bhde', kc * zeta[None, :, :, None], vc)
        return state, inner + cross

    state0 = jnp.zeros((B, H, d, d), jnp.float32)
    _, o = lax.scan(step, state0, (chunks(q), chunks(k), chunks(v)))
    o = o.transpose(1, 0, 3, 2, 4).reshape(B, S, H, d)
    return o * lax.rsqrt(jnp.mean(o * o, axis=-1, keepdims=True) + NORM_EPS)

def first_inputs(seed: int = 0) -> dict:
    key = jax.random.key(seed)
    ks = jax.random.split(key, 20)
    f32 = jnp.float32
    nrm = lambda k, shape, s: jax.random.normal(k, shape, f32) * s
    L = DEPTH
    x = jax.random.normal(ks[0], (BATCH, SEQ, D_MODEL), f32)
    offset = jax.random.randint(ks[1], (BATCH, 1), 0, 4096, dtype=jnp.int32)
    positions = (offset + jnp.arange(SEQ, dtype=jnp.int32)[None, :]).astype(jnp.int32)
    return {
        "x": x,
        "positions": positions,
        "norm_mix": 1.0 + nrm(ks[2], (L, D_MODEL), 0.02),
        "w_in": nrm(ks[3], (L, D_MODEL, IN_WIDTH), D_MODEL ** -0.5),
        "cmp_pos_k": nrm(ks[4], (L, CMP_BLOCK, NSA_HEAD_DIM), 0.1),
        "cmp_pos_v": nrm(ks[5], (L, CMP_BLOCK, NSA_HEAD_DIM), 0.1),
        "cmp_k_w1": nrm(ks[6], (L, CMP_BLOCK * NSA_HEAD_DIM, CMP_HIDDEN), (CMP_BLOCK * NSA_HEAD_DIM) ** -0.5),
        "cmp_k_w2": nrm(ks[7], (L, CMP_HIDDEN, NSA_HEAD_DIM), CMP_HIDDEN ** -0.5),
        "cmp_v_w1": nrm(ks[8], (L, CMP_BLOCK * NSA_HEAD_DIM, CMP_HIDDEN), (CMP_BLOCK * NSA_HEAD_DIM) ** -0.5),
        "cmp_v_w2": nrm(ks[9], (L, CMP_HIDDEN, NSA_HEAD_DIM), CMP_HIDDEN ** -0.5),
        "w_proj_a": nrm(ks[10], (L, NSA_Q_W, D_MODEL), NSA_Q_W ** -0.5),
        "w_proj_b": nrm(ks[11], (L, RET_W, D_MODEL), RET_W ** -0.5),
        "w_out": nrm(ks[12], (L, D_MODEL, D_MODEL), D_MODEL ** -0.5),
        "norm_mlp": 1.0 + nrm(ks[13], (L, D_MODEL), 0.02),
        "w_up": nrm(ks[14], (L, D_MODEL, MLP_HIDDEN), D_MODEL ** -0.5),
        "w_down": nrm(ks[15], (L, MLP_HIDDEN, D_MODEL), MLP_HIDDEN ** -0.5),
        "norm_final": 1.0 + nrm(ks[16], (D_MODEL,), 0.02),
    }

def first_block(x, positions, norm_mix, w_in, cmp_pos_k, cmp_pos_v, cmp_k_w1, cmp_k_w2, cmp_v_w1, cmp_v_w2,
              w_proj_a, w_proj_b, w_out, norm_mlp, w_up, w_down, norm_final):
    B, S, _ = x.shape
    offsets = np.cumsum(IN_SIZES)[:-1].tolist()
    nsa_batched = jax.vmap(nsa_mixer, in_axes=(0,) * 8 + (None,) * 6)
    for layer in range(DEPTH):
        h = rmsnorm(x, norm_mix[layer])
        (q, kc, vc, ks, vs, kw, vw, nsa_g, rq, rk, rv, rg, gate_a, gate_b) = jnp.split(
            h @ w_in[layer], offsets, axis=-1)
        heads = lambda a, n_h, d: a.reshape(B, S, n_h, d)
        q = rotary(heads(q, NSA_HEADS, NSA_HEAD_DIM), positions, ROPE_DIM, ROPE_THETA)
        kc = rotary(heads(kc, NSA_KV_GROUPS, NSA_HEAD_DIM), positions, ROPE_DIM, ROPE_THETA)
        ks = rotary(heads(ks, NSA_KV_GROUPS, NSA_HEAD_DIM), positions, ROPE_DIM, ROPE_THETA)
        kw = rotary(heads(kw, NSA_KV_GROUPS, NSA_HEAD_DIM), positions, ROPE_DIM, ROPE_THETA)
        vc = heads(vc, NSA_KV_GROUPS, NSA_HEAD_DIM)
        vs = heads(vs, NSA_KV_GROUPS, NSA_HEAD_DIM)
        vw = heads(vw, NSA_KV_GROUPS, NSA_HEAD_DIM)
        nsa_out = nsa_batched(q, kc, vc, ks, vs, kw, vw, nsa_g.reshape(B, S, NSA_HEADS, 3),
                              cmp_pos_k[layer], cmp_pos_v[layer], cmp_k_w1[layer], cmp_k_w2[layer],
                              cmp_v_w1[layer], cmp_v_w2[layer])
        ret = retention(heads(rq, RET_HEADS, RET_HEAD_DIM), heads(rk, RET_HEADS, RET_HEAD_DIM),
                        heads(rv, RET_HEADS, RET_HEAD_DIM), positions)
        ret_out = (jax.nn.silu(rg.astype(jnp.float32)) * ret.reshape(B, S, RET_W)).astype(x.dtype)
        mix = (jax.nn.sigmoid(gate_a) * (nsa_out @ w_proj_a[layer])
               + jax.nn.sigmoid(gate_b) * (ret_out @ w_proj_b[layer]))
        x = x + mix @ w_out[layer]
        h = rmsnorm(x, norm_mlp[layer])
        x = x + jnp.square(jax.nn.relu(h @ w_up[layer])) @ w_down[layer]
    return rmsnorm(x, norm_final)


DEPTH_2 = 2

N_A_LAYERS = DEPTH_2 // 2
N_B_LAYERS = DEPTH_2 - N_A_LAYERS
MLSTM_HEADS = 8
MLSTM_QK_DIM = D_MODEL // 2 // MLSTM_HEADS
MLSTM_V_DIM = D_MODEL // MLSTM_HEADS
MLSTM_CHUNK = 64
MLSTM_SPLITS = [MLSTM_HEADS * MLSTM_QK_DIM, MLSTM_HEADS * MLSTM_QK_DIM, MLSTM_HEADS * MLSTM_V_DIM,
                MLSTM_HEADS * MLSTM_V_DIM, MLSTM_HEADS, MLSTM_HEADS]
MLSTM_IN = sum(MLSTM_SPLITS)
FOX_HEADS = 16
FOX_HEAD_DIM = D_MODEL // FOX_HEADS
FOX_BLOCK = 128
D_FF = 2816
CONV_WIDTH = 3
EPS = 1e-6


def rmsnorm_2(x, w):
    xf = x.astype(jnp.float32)
    y = xf * lax.rsqrt(jnp.mean(xf * xf, axis=-1, keepdims=True) + EPS)
    return (y * w.astype(jnp.float32)).astype(x.dtype)

def mlstm_mixer(h, w_in, b_gate, w_head_norm, w_out):
    B, S, _ = h.shape
    H, DK, DV, L = MLSTM_HEADS, MLSTM_QK_DIM, MLSTM_V_DIM, MLSTM_CHUNK
    NC = S // L
    proj = h @ w_in
    idx = list(np.cumsum(MLSTM_SPLITS)[:-1])
    q, k, v, o, ig, fg = jnp.split(proj, idx, axis=-1)
    f32 = jnp.float32
    ig = ig.astype(f32) + b_gate[:H].astype(f32)
    lf = jax.nn.log_sigmoid(fg.astype(f32) + b_gate[H:].astype(f32))

    def to_chunks(t, d):
        return t.astype(f32).reshape(B, NC, L, H, d).transpose(1, 0, 3, 2, 4)

    qc = to_chunks(q, DK) * (DK ** -0.5)
    kc = to_chunks(k, DK)
    vc = to_chunks(v, DV)
    ic = ig.reshape(B, NC, L, H).transpose(1, 0, 3, 2)
    fc = lf.reshape(B, NC, L, H).transpose(1, 0, 3, 2)
    causal = jnp.tril(jnp.ones((L, L), dtype=bool))

    def step(carry, inp):
        C, n, m = carry
        qt, kt, vt, it, ft = inp
        b = jnp.cumsum(ft, axis=-1)
        dmat = jnp.where(causal, b[..., :, None] - b[..., None, :] + it[..., None, :], -jnp.inf)
        m_inter = b + m[..., None]
        m_t = jnp.maximum(m_inter, jnp.max(dmat, axis=-1))
        s = jnp.einsum('bhtd,bhsd->bhts', qt, kt) * jnp.exp(dmat - m_t[..., None])
        w_inter = jnp.exp(m_inter - m_t)
        num = jnp.einsum('bhts,bhse->bhte', s, vt) + w_inter[..., None] * jnp.einsum('bhtd,bhde->bhte', qt, C)
        den = jnp.sum(s, axis=-1) + w_inter * jnp.einsum('bhtd,bhd->bht', qt, n)
        ht = num / jnp.maximum(jnp.abs(den), jnp.exp(-m_t))[..., None]
        b_last = b[..., -1]
        g = b_last[..., None] - b + it
        m_new = jnp.maximum(b_last + m, jnp.max(g, axis=-1))
        decay = jnp.exp(b_last + m - m_new)
        wk = jnp.exp(g - m_new[..., None])
        C_new = decay[..., None, None] * C + jnp.einsum('bhs,bhsd,bhse->bhde', wk, kt, vt)
        n_new = decay[..., None] * n + jnp.einsum('bhs,bhsd->bhd', wk, kt)
        return (C_new, n_new, m_new), ht

    init = (jnp.zeros((B, H, DK, DV), f32), jnp.zeros((B, H, DK), f32), jnp.zeros((B, H), f32))
    _, hs = lax.scan(step, init, (qc, kc, vc, ic, fc))
    hs = hs.transpose(1, 0, 3, 2, 4).reshape(B, S, H, DV)
    hs = hs * lax.rsqrt(jnp.mean(hs * hs, axis=-1, keepdims=True) + EPS)
    hs = hs.reshape(B, S, H * DV) * w_head_norm.astype(f32)
    hs = hs * jax.nn.sigmoid(o.astype(f32))
    return hs.astype(h.dtype) @ w_out

def shared_kv(x, kv_norm, kv_w, kv_b_f):
    B, S, _ = x.shape
    h = rmsnorm_2(x, kv_norm)
    proj = h @ kv_w
    k, v, f = jnp.split(proj, [D_MODEL, 2 * D_MODEL], axis=-1)
    k = k.reshape(B, S, FOX_HEADS, FOX_HEAD_DIM)
    v = v.reshape(B, S, FOX_HEADS, FOX_HEAD_DIM)
    log_f = jax.nn.log_sigmoid(f.astype(jnp.float32) + kv_b_f.astype(jnp.float32))
    c = jnp.cumsum(log_f, axis=1).transpose(0, 2, 1)
    return k, v, c

def fox_mixer(h, w_qg, w_out, k, v, c):
    B, S, _ = h.shape
    H, DH, BLK = FOX_HEADS, FOX_HEAD_DIM, FOX_BLOCK
    NQ = S // BLK
    proj = h @ w_qg
    q, g = jnp.split(proj, [D_MODEL], axis=-1)
    q = q.reshape(B, S, H, DH) * (DH ** -0.5)
    qb = q.reshape(B, NQ, BLK, H, DH).transpose(1, 0, 2, 3, 4)
    cb = c.reshape(B, H, NQ, BLK).transpose(2, 0, 1, 3)
    starts = jnp.arange(NQ) * BLK
    key_pos = jnp.arange(S)

    def block(args):
        qi, ci, st = args
        logits = jnp.einsum('bqhd,bkhd->bhqk', qi, k).astype(jnp.float32)
        logits = logits + (ci[..., :, None] - c[..., None, :])
        qpos = st + jnp.arange(BLK)
        mask = key_pos[None, :] <= qpos[:, None]
        logits = jnp.where(mask, logits, -jnp.inf)
        p = jax.nn.softmax(logits, axis=-1)
        return jnp.einsum('bhqk,bkhd->bqhd', p.astype(v.dtype), v)

    o = lax.map(block, (qb, cb, starts))
    o = o.transpose(1, 0, 2, 3, 4).reshape(B, S, D_MODEL)
    o = o * jax.nn.sigmoid(g)
    return o @ w_out

def conv_ffn(h, w_up, conv_w, conv_b, w_down):
    S = h.shape[1]
    u = h @ w_up
    up = jnp.pad(u, ((0, 0), (CONV_WIDTH - 1, 0), (0, 0)))
    y = conv_b
    for j in range(CONV_WIDTH):
        y = y + conv_w[j] * up[:, j:j + S]
    gate, val = jnp.split(y, 2, axis=-1)
    return (jax.nn.gelu(gate, approximate=True) * val) @ w_down

def second_inputs(seed: int = 0) -> dict:
    key = jax.random.key(seed)
    ks = jax.random.split(key, 24)
    D, H = D_MODEL, MLSTM_HEADS
    f32 = jnp.float32

    def nrm(k, shape, scale):
        return jax.random.normal(k, shape, f32) * scale

    def gain(k, shape):
        return 1.0 + 0.05 * jax.random.normal(k, shape, f32)

    x = jax.random.normal(ks[0], (BATCH, SEQ, D), f32)
    norm_mix_pre = gain(ks[1], (DEPTH_2, D))
    norm_mix_post = gain(ks[2], (DEPTH_2, D))
    norm_ffn_pre = gain(ks[3], (DEPTH_2, D))
    norm_ffn_post = gain(ks[4], (DEPTH_2, D))
    mlstm_w_in = nrm(ks[5], (N_A_LAYERS, D, MLSTM_IN), D ** -0.5)
    mlstm_b_gate = jnp.concatenate([
        nrm(ks[6], (N_A_LAYERS, H), 0.1),
        jax.random.uniform(ks[7], (N_A_LAYERS, H), f32, minval=3.0, maxval=6.0)], axis=-1)
    mlstm_norm = gain(ks[8], (N_A_LAYERS, H * MLSTM_V_DIM))
    mlstm_w_out = nrm(ks[9], (N_A_LAYERS, H * MLSTM_V_DIM, D), (H * MLSTM_V_DIM) ** -0.5)
    kv_norm = gain(ks[10], (D,))
    kv_w = nrm(ks[11], (D, 2 * D + FOX_HEADS), D ** -0.5)
    kv_b_f = jax.random.uniform(ks[12], (FOX_HEADS,), f32, minval=1.0, maxval=6.0)
    fox_w_qg = nrm(ks[13], (N_B_LAYERS, D, 2 * D), D ** -0.5)
    fox_w_out = nrm(ks[14], (N_B_LAYERS, D, D), D ** -0.5)
    ffn_w_up = nrm(ks[15], (DEPTH_2, D, 2 * D_FF), D ** -0.5)
    ffn_conv_w = nrm(ks[16], (DEPTH_2, CONV_WIDTH, 2 * D_FF), CONV_WIDTH ** -0.5)
    ffn_conv_b = nrm(ks[17], (DEPTH_2, 2 * D_FF), 0.02)
    ffn_w_down = nrm(ks[18], (DEPTH_2, D_FF, D), D_FF ** -0.5)
    return {'x': x, 'norm_mix_pre': norm_mix_pre, 'norm_mix_post': norm_mix_post,
            'norm_ffn_pre': norm_ffn_pre, 'norm_ffn_post': norm_ffn_post,
            'mlstm_w_in': mlstm_w_in, 'mlstm_b_gate': mlstm_b_gate, 'mlstm_norm': mlstm_norm,
            'mlstm_w_out': mlstm_w_out, 'kv_norm': kv_norm, 'kv_w': kv_w, 'kv_b_f': kv_b_f,
            'fox_w_qg': fox_w_qg, 'fox_w_out': fox_w_out, 'ffn_w_up': ffn_w_up,
            'ffn_conv_w': ffn_conv_w, 'ffn_conv_b': ffn_conv_b, 'ffn_w_down': ffn_w_down}

def second_block(x, norm_mix_pre, norm_mix_post, norm_ffn_pre, norm_ffn_post, mlstm_w_in, mlstm_b_gate,
              mlstm_norm, mlstm_w_out, kv_norm, kv_w, kv_b_f, fox_w_qg, fox_w_out, ffn_w_up,
              ffn_conv_w, ffn_conv_b, ffn_w_down):
    k_sh = v_sh = c_sh = None
    for layer in range(DEPTH_2):
        h = rmsnorm_2(x, norm_mix_pre[layer])
        if layer < N_A_LAYERS:
            y = mlstm_mixer(h, mlstm_w_in[layer], mlstm_b_gate[layer], mlstm_norm[layer], mlstm_w_out[layer])
        else:
            j = layer - N_A_LAYERS
            y = fox_mixer(h, fox_w_qg[j], fox_w_out[j], k_sh, v_sh, c_sh)
        x = x + rmsnorm_2(y, norm_mix_post[layer])
        h = rmsnorm_2(x, norm_ffn_pre[layer])
        y = conv_ffn(h, ffn_w_up[layer], ffn_conv_w[layer], ffn_conv_b[layer], ffn_w_down[layer])
        x = x + rmsnorm_2(y, norm_ffn_post[layer])
        if layer == N_A_LAYERS - 1:
            k_sh, v_sh, c_sh = shared_kv(x, kv_norm, kv_w, kv_b_f)
    return x


def setup_inputs(seed=0):
    out = dict(first_inputs(seed))
    for name, value in second_inputs(seed + 1).items():
        if name != "x":
            out[name + "_2"] = value
    return out


def reference(
    x, positions, norm_mix, w_in, cmp_pos_k, cmp_pos_v, cmp_k_w1, cmp_k_w2, cmp_v_w1, cmp_v_w2,
    w_proj_a, w_proj_b, w_out, norm_mlp, w_up, w_down, norm_final, norm_mix_pre_2,
    norm_mix_post_2, norm_ffn_pre_2, norm_ffn_post_2, mlstm_w_in_2, mlstm_b_gate_2,
    mlstm_norm_2, mlstm_w_out_2, kv_norm_2, kv_w_2, kv_b_f_2, fox_w_qg_2, fox_w_out_2,
    ffn_w_up_2, ffn_conv_w_2, ffn_conv_b_2, ffn_w_down_2,
):
    x = first_block(
        x, positions, norm_mix, w_in, cmp_pos_k, cmp_pos_v, cmp_k_w1, cmp_k_w2, cmp_v_w1,
        cmp_v_w2, w_proj_a, w_proj_b, w_out, norm_mlp, w_up, w_down, norm_final,
    )
    return second_block(
        x, norm_mix_pre_2, norm_mix_post_2, norm_ffn_pre_2, norm_ffn_post_2, mlstm_w_in_2,
        mlstm_b_gate_2, mlstm_norm_2, mlstm_w_out_2, kv_norm_2, kv_w_2, kv_b_f_2, fox_w_qg_2,
        fox_w_out_2, ffn_w_up_2, ffn_conv_w_2, ffn_conv_b_2, ffn_w_down_2,
    )


_drawn_inputs = setup_inputs


def setup_inputs(seed=0):
    import zlib

    import numpy as np

    out = dict(_drawn_inputs(seed))
    spreads = {}
    factors = {'cmp_pos_k': 8.0}
    for name, (base, spread) in spreads.items():
        noise = np.random.default_rng([zlib.crc32(name.encode()), seed]).standard_normal(out[name].shape)
        drawn = base * np.exp(spread * noise) if base else spread * noise
        out[name] = __import__('jax').numpy.asarray(drawn.astype(out[name].dtype))
    for name, factor in factors.items():
        out[name] = (out[name] * factor).astype(out[name].dtype)
    return out
```

```python
from contextlib import ExitStack

import numpy as np

import concourse.bass as bass
from concourse import mybir

F32, F32R = mybir.dt.float32, mybir.dt.float32r
BF16, I32 = mybir.dt.bfloat16, mybir.dt.int32
ACT = mybir.ActivationFunctionType
ALU = mybir.AluOpType
AX_X = mybir.AxisListType.X

P = 128
S = 512
D = 1024
KT = D // P
TT = S // P
SLOT = KT * 256
EPS = 1e-6
NEG = -1e30

HD, HQ, KV = 64, 8, 2
RH, RD = 4, 128
CB, CS, CH = 32, 16, 256
NC = (S - CB) // CS + 1
MLP_H = 4 * D
COLS = np.cumsum([0, HQ * HD] + [KV * HD] * 6 + [3 * HQ] + [RH * RD] * 4 + [D, D]).tolist()
(C_Q, C_KC, C_VC, C_KS, C_VS, C_KW, C_VW, C_G, C_RQ, C_RK, C_RV, C_RG, C_GA, C_GB) = COLS[:14]
GATES = 3 * HQ
MH, MK, MV = 8, 64, 128
FH, FD = 16, 64
FF = 2816
FT = FF // P

PI = float(np.pi)
TWO_PI_HI = 6.28125
TWO_PI_LO = 2 * np.pi - TWO_PI_HI
ROUND = 12582912.0
SIN_MAX = 3.1415925

VECS = ["norm_mix", "norm_mlp", "norm_final", "norm_mix_pre_2", "norm_mix_post_2",
        "norm_ffn_pre_2", "norm_ffn_post_2", "kv_norm_2"]


class Tally:

    def __init__(self, sem):
        self.sem = sem
        self.n = 0


def shape_constants():
    p = np.arange(P)
    c = {}
    c["ident"] = np.eye(P)
    c["causal_bias"] = np.where(p[None, :] <= p[:, None], 0.0, NEG)
    c["causal_keep"] = np.where(p[:, None] <= p[None, :], 1.0, 0.0)
    half, rot = 8, 16
    d = p % HD
    partner = np.where(d < half, p + half, np.where(d < rot, p - half, p))
    c["swap_nsa"] = (p[:, None] == partner[None, :])
    c["swap_ret"] = (p[:, None] == ((p + RD // 2) % RD)[None, :])
    inv = np.exp(np.float32(-np.log(500000.0)) * np.arange(half, dtype=np.float32) * np.float32(2.0) / np.float32(rot))
    invr = np.exp(np.float32(-np.log(10000.0)) * np.arange(RD // 2, dtype=np.float32) * np.float32(2.0) / np.float32(RD))
    angles = np.zeros((P, 4))
    angles[:, 0] = np.where(d < rot, inv[d % half], 0.0)
    angles[:, 1] = np.where(d < half, -1.0, 1.0)
    angles[:, 2] = invr[p % (RD // 2)]
    angles[:, 3] = np.where(p < RD // 2, -1.0, 1.0)
    c["angles"] = angles
    t = p[:, None] + P * np.arange(TT)[None, :]
    end = CS * np.arange(CB) + CB - 1
    ok = (end[None, None, :] <= t[:, :, None]) & (np.arange(CB) < NC)[None, None, :]
    c["cmp_bias"] = np.where(ok, 0.0, NEG).reshape(P, TT * CB)
    c["cmp_any"] = ok.any(-1)
    packed = np.concatenate([np.asarray(v, np.float32) for v in c.values()], 1)
    at, off = {}, 0
    for k, v in c.items():
        at[k] = (off, off + v.shape[1])
        off += v.shape[1]
    log_g = np.log(1.0 - np.exp2(-5.0 - np.arange(RH)))
    rel = np.arange(S)[None, :] - p[:, None]
    decay = np.where(rel[:, None, :] >= 0, np.exp(log_g[None, :, None] * np.maximum(rel, 0)[:, None, :]), 0.0)
    return packed, at, np.ascontiguousarray(decay.astype(np.float32))


class Weights:

    def __init__(self, blocks, forms):
        self.blocks = blocks
        self.forms = forms

    def form(self, b):
        return self.forms[b % len(self.forms)]


def build(nc, io, at):
    top = ExitStack()
    with top:
        def sb(ctx, name, shape, dt=F32):
            return ctx.enter_context(nc.sbuf_tensor(name, shape, dt))

        def tally(name):
            return Tally(top.enter_context(nc.semaphore(name)))

        raw = [sb(top, f"w_raw{r}", [P, SLOT]) for r in range(2)]
        w_hi = [sb(top, f"w_hi{r}", [P, SLOT], F32R) for r in range(2)]
        w_lo = [sb(top, f"w_lo{r}", [P, SLOT], F32R) for r in range(2)]
        xT = sb(top, "xT", [P, KT, S])
        a_hi = sb(top, "a_hi", [P, KT, S], F32R)
        a_lo = sb(top, "a_lo", [P, KT, S], F32R)
        width = io["const"].shape[1]
        const = sb(top, "const_sb", [P, width])
        ident_b = sb(top, "ident_b", [P, P], BF16)
        bias_b = sb(top, "bias_b", [P, P], BF16)
        cmpb_b = sb(top, "cmpb_b", [P, TT * CB], BF16)
        ones = sb(top, "ones", [P, P])
        gains = sb(top, "gains", [P, 96])
        conv = sb(top, "conv", [P, 4, 88])
        bank = [top.enter_context(nc.psum_tensor(f"bank{i}", [P, 512], F32)) for i in range(8)]

        def cst(name):
            return const[:, at[name][0]:at[name][1]]

        ident = cst("ident")

        raw_loaded = [tally(f"raw_loaded{r}") for r in range(2)]
        hi_ready, lo_ready = tally("hi_ready"), tally("lo_ready")
        products_done, evacuated = tally("products_done"), tally("evacuated")
        rows_done, rows_out = tally("rows_done"), tally("rows_out")
        part_ready, part_used = tally("part_ready"), tally("part_used")
        gelu_ready = tally("gelu_ready")
        hid_ready = tally("hid_ready")
        inputs_in = [tally(f"inputs_in{i}") for i in range(4)]
        sq_ready, sum_ready, mean_ready, root_ready = (tally(n) for n in ("sq_ready", "sum_ready", "mean_ready", "root_ready"))
        scaled, split_hi_done, split_lo_done = tally("scaled"), tally("split_hi_done"), tally("split_lo_done")
        turned, turned_out, turned_hi = tally("turned"), tally("turned_out"), tally("turned_hi")
        keys_staged = tally("keys_staged")
        staged, scores_ready, max_ready, probs_ready = (tally(n) for n in ("staged", "scores_ready", "max_ready", "probs_ready"))
        probs_turned, probs_copied, out_ready, out_done = (tally(n) for n in ("probs_turned", "probs_copied", "out_ready", "out_done"))
        bias_row_in = [tally(f"bias_row_in{r}") for r in range(2)]
        bias_row_used = tally("bias_row_used")
        logits_ready = tally("logits_ready")
        gap_ready, decay_ready, kept, weighted = (tally(n) for n in ("gap_ready", "decay_ready", "kept", "weighted"))
        act_step, dve_step, pe_step, pool_step = (tally(n) for n in ("act_step", "dve_step", "pe_step", "pool_step"))
        rows_stored = tally("rows_stored")
        stored = tally("stored")
        LEAD = 8
        led = [products_done, evacuated, rows_done, rows_out, part_ready, part_used, hi_ready, lo_ready, scores_ready,
               max_ready, probs_ready, probs_turned, probs_copied, out_ready, out_done, staged, keys_staged, bias_row_used,
               logits_ready, gap_ready, decay_ready, kept, weighted, gelu_ready, hid_ready]

        stream = {"slot": 0}

        def slot_view(ring, r, form):
            tiles, width, _ = form
            return ring[r][:, 0:tiles * width].rearrange("p (t n) -> p t n", t=tiles)

        def load(eng, spec, b, slot, q):
            dst = slot_view(raw, slot, spec.forms[q])
            for col, ncol, src in spec.forms[q][2]:
                eng.dma_start(dst[:, :, col:col + ncol], src(b)).then_inc(raw_loaded[slot].sem, 16)

        def prefetch(eng, spec):
            for b in range(min(2, spec.blocks)):
                slot = (stream["slot"] + b) % 2
                load(eng, spec, b, slot, b % len(spec.forms))

        def loads(eng, spec, nxt, m):
            def one(b, q):
                eng.wait_ge(lo_ready.sem, m["lo"] + b - 1)
                load(eng, spec, b, (m["slot"] + q) % 2, q % len(spec.forms))
            if spec.blocks > 4:
                with eng.Fori(1, spec.blocks // 2) as i:
                    one(i * 2, 0)
                    one(i * 2 + 1, 1)
            else:
                for b in range(2, spec.blocks):
                    one(b, b % 2)
            if nxt is not None:
                for b in range(min(2, nxt.blocks)):
                    e = spec.blocks + b
                    if e >= 2:
                        eng.wait_ge(lo_ready.sem, m["lo"] + e - 1)
                    load(eng, nxt, b, (m["slot"] + e) % 2, b % len(nxt.forms))

        def hi_part(act, spec, b, q, m):
            slot, form = (m["slot"] + q) % 2, spec.forms[q % len(spec.forms)]
            n = form[0] * form[1]
            act.wait_ge(raw_loaded[slot].sem, m["raw"][slot] + 16 * len(form[2]) * (b // 2 + 1 if isinstance(b, int) else m["i"] + (1 if m["ahead"] == 0 else 2)))
            act.wait_ge(products_done.sem, m["prod"] + b - 1)
            act.activation(w_hi[slot][:, 0:n], raw[slot][:, 0:n], ACT.Copy).then_inc(hi_ready.sem, 1)

        def lo_part(dve, spec, b, q, m):
            slot, form = (m["slot"] + q) % 2, spec.forms[q % len(spec.forms)]
            n = form[0] * form[1]
            dve.wait_ge(hi_ready.sem, m["hi"] + b + 1)
            dve.tensor_tensor(w_lo[slot][:, 0:n], raw[slot][:, 0:n], w_hi[slot][:, 0:n].bitcast(F32),
                              ALU.subtract).then_inc(lo_ready.sem, 1)

        def marks(spec):
            return {"slot": stream["slot"], "raw": [t.n for t in raw_loaded], "hi": hi_ready.n, "lo": lo_ready.n,
                    "prod": products_done.n, "evac": evacuated.n, "rows": rows_done.n, "rowsout": rows_out.n,
                    "part": part_ready.n, "pused": part_used.n, "gelu": gelu_ready.n, "hid": hid_ready.n, "i": 0, "ahead": 0}

        def finish(spec):
            for b in range(spec.blocks):
                slot = (stream["slot"] + b) % 2
                raw_loaded[slot].n += 16 * len(spec.form(b)[2])
            stream["slot"] = (stream["slot"] + spec.blocks) % 2
            for t in (hi_ready, lo_ready, products_done):
                t.n += spec.blocks

        def split_ahead(eng, spec, m, part, use):
            n = spec.blocks // 2
            m["ahead"] = 0
            part(eng, spec, 0, 0, m)
            if spec.blocks == 1:
                use(0, 0)
                return
            if n > 1:
                with eng.Fori(0, n - 1) as i:
                    m["i"], m["ahead"] = i, 0
                    part(eng, spec, i * 2 + 1, 1, m)
                    use(i * 2, 0)
                    m["ahead"] = 1
                    part(eng, spec, i * 2 + 2, 0, m)
                    use(i * 2 + 1, 1)
            part(eng, spec, spec.blocks - 1, 1, m)
            use(spec.blocks - 2, 0)
            use(spec.blocks - 1, 1)

        def pairs(eng, spec, use):
            if spec.blocks == 1:
                use(0, 0)
            elif spec.blocks == 2:
                use(0, 0)
                use(1, 1)
            else:
                with eng.Fori(0, spec.blocks // 2) as i:
                    use(i * 2, 0)
                    use(i * 2 + 1, 1)

        def three_products(pe, out, w, x, first, last):
            pe.matmul(out, w[0], x[0], start=first, stop=False)
            pe.matmul(out, w[0], x[1], start=False, stop=False)
            return pe.matmul(out, w[1], x[0], start=False, stop=last)

        def dense(spec, nxt, chunks, evac_dve, evac_act=None, evac_pool=None, evac_waits=1):
            m = marks(spec)

            with nc.Block() as block:
                @block.sync
                def _(sp):
                    loads(sp, spec, nxt, m)

                @block.scalar
                def _(act):
                    split_ahead(act, spec, m, hi_part,
                                lambda b, q: evac_act(act, b, (m["slot"] + q) % 2, m) if evac_act else None)

                @block.vector
                def _(dve):
                    split_ahead(dve, spec, m, lo_part, lambda b, q: evac_dve(dve, b, (m["slot"] + q) % 2, m))

                if evac_pool is not None:
                    @block.gpsimd
                    def _(pool):
                        pairs(pool, spec, lambda b, q: evac_pool(pool, b, (m["slot"] + q) % 2, m))

                @block.tensor
                def _(pe):
                    def use(b, q):
                        slot = (m["slot"] + q) % 2
                        pe.wait_ge(lo_ready.sem, m["lo"] + b + 1)
                        pe.wait_ge(evacuated.sem, m["evac"] + b - 1)
                        for c, terms in enumerate(chunks[q % len(chunks)]):
                            for k, (col, x) in enumerate(terms):
                                w = [ring[slot][:, col:col + P] for ring in (w_hi, w_lo)]
                                last = three_products(pe, bank[2 * slot + c][:, :], w, x, k == 0, k == len(terms) - 1)
                        last.then_inc(products_done.sem, 1)
                    pairs(pe, spec, use)
            finish(spec)
            evacuated.n += spec.blocks

        def dense_rows(spec, nxt, evac_dve=None, evac_act=None):
            m = marks(spec)
            tiles, width, _ = spec.forms[0]

            with nc.Block() as block:
                @block.sync
                def _(sp):
                    loads(sp, spec, nxt, m)

                def rows(eng, fn):
                    def use(b, q):
                        if q == 1 and fn is not None:
                            g = (b - 1) // 2 if isinstance(b, int) else m["i"]
                            for t in range(TT):
                                eng.wait_ge(rows_done.sem, m["rows"] + g * TT + (t + 1))
                                fn(eng, g, t).then_inc(rows_out.sem, 1)
                    return use

                @block.scalar
                def _(act):
                    split_ahead(act, spec, m, hi_part, rows(act, evac_act))

                @block.vector
                def _(dve):
                    split_ahead(dve, spec, m, lo_part, rows(dve, evac_dve))

                @block.tensor
                def _(pe):
                    def use(b, q):
                        slot = (m["slot"] + q) % 2
                        pe.wait_ge(lo_ready.sem, m["lo"] + b + 1)
                        g = b // 2 if isinstance(b, int) else m["i"]
                        for t in range(TT):
                            if q == 0:
                                pe.wait_ge(rows_out.sem, m["rowsout"] + g * TT + (t + 1 - TT))
                            for k in range(tiles):
                                x = [a[:, q * tiles + k, t * P:(t + 1) * P] for a in (a_hi, a_lo)]
                                w = [ring[slot][:, k * width:(k + 1) * width] for ring in (w_hi, w_lo)]
                                last = three_products(pe, bank[t][:, 0:width], x, w, q == 0 and k == 0,
                                                      q == 1 and k == tiles - 1)
                            if q == 1:
                                last.then_inc(rows_done.sem, 1)
                        pe.drain().then_inc(products_done.sem, 1)
                    if spec.blocks == 2:
                        use(0, 0)
                        use(1, 1)
                    else:
                        with pe.Fori(0, spec.blocks // 2) as i:
                            m["i"] = i
                            use(i * 2, 0)
                            use(i * 2 + 1, 1)
            finish(spec)
            rows_done.n += TT * spec.blocks // 2
            rows_out.n += TT * spec.blocks // 2

        def view(w):
            return w.rearrange("(t p) n -> p t n", p=P)

        def cols(w, start, n=256, step=256, t0=0, t1=None):
            v = view(w)[:, t0:t1, :]
            return lambda b: v[:, :, bass.ds(b * step + start, n)]

        def plain(w, start, blocks, t0=0, tiles=KT):
            return Weights(blocks, [(tiles, 256, [(0, 256, cols(w, start, t0=t0, t1=t0 + tiles))])])

        def row_blocks(w, start, groups):
            forms = []
            for q in range(2):
                v = view(w)[:, q * KT // 2:(q + 1) * KT // 2, :]
                forms.append((KT // 2, 512, [(0, 512, (lambda v, q: lambda b: v[:, :, bass.ds((b - q) * 256 + start, 512)])(v, q))]))
            return Weights(2 * groups, forms)

        a_tiles = [(a_hi[:, k, :], a_lo[:, k, :]) for k in range(KT)]

        def two_chunks(xs):
            return [[[(k * 256 + c * P, x) for k, x in enumerate(xs)] for c in range(2)]]

        W_IN, W_IN2, KV_W = io["w_in"][0], io["mlstm_w_in_2"][0], io["kv_w_2"]
        v_in = view(W_IN)
        q_pieces = [(128 * j + 64 * g, 64, (lambda j, g: lambda b: v_in[:, :, bass.ds(b * 128 + (C_Q + 256 * g + 64 * j), 64)])(j, g))
                    for j in range(2) for g in range(2)]
        half = [v_in[:, q * 4:(q + 1) * 4, :] for q in range(2)]
        specs = {}
        specs["q"] = Weights(2, [(KT, 256, q_pieces)])
        specs["kcvc"] = Weights(2, [(KT, 256, [(0, 256, lambda b: v_in[:, :, C_KC:C_KC + 256])]),
                                    (KT, 256, [(0, 128, lambda b: v_in[:, :, C_KS:C_KS + 128]),
                                               (128, 128, lambda b: v_in[:, :, C_KW:C_KW + 128])])])
        specs["vg"] = Weights(2, [(4, 280, [(0, 128, (lambda q: lambda b: half[q][:, :, C_VS:C_VS + 128])(q)),
                                            (128, 152, (lambda q: lambda b: half[q][:, :, C_VW:C_VW + 152])(q))])
                                  for q in range(2)])
        specs["rqk"] = plain(W_IN, C_RQ, 4)
        specs["rvg"] = row_blocks(W_IN, C_RV, 2)
        specs["mix"] = Weights(16, [
            (KT, 256, [(0, 128, lambda b: v_in[:, :, bass.ds(b * 64 + C_GA, 128)]),
                       (128, 128, lambda b: v_in[:, :, bass.ds(b * 64 + C_GB, 128)])]),
            (4, 256, [(0, 128, lambda b: view(io["w_proj_a"][0])[:, :, bass.ds(b * 64 - 64, 128)]),
                      (128, 128, lambda b: view(io["w_proj_b"][0])[:, :, bass.ds(b * 64 - 64, 128)])])])
        specs["out1"] = plain(io["w_out"][0], 0, 4)
        order = ["q", "kcvc", "vg", "rqk", "rvg", "mix", "out1"]
        for g in range(4):
            specs[f"up{g}"] = plain(io["w_up"][0], g * D, 4)
            specs[f"down{g}"] = plain(io["w_down"][0], 0, 4, t0=g * KT)
            order += [f"up{g}", f"down{g}"]
        specs["mqk"] = plain(W_IN2, 0, 4)
        specs["mv"] = row_blocks(W_IN2, 1024, 2)
        specs["mo"] = row_blocks(W_IN2, 2048, 2)
        v_in2, v_kv = view(W_IN2), view(KV_W)
        specs["mg"] = Weights(1, [(KT, 128, [(0, 8, lambda b: v_in2[:, :, 3072:3080]), (8, 24, lambda b: v_in2[:, :, 0:24]),
                                             (32, 8, lambda b: v_in2[:, :, 3080:3088]), (40, 88, lambda b: v_in2[:, :, 24:112])])])
        specs["mout"] = plain(io["mlstm_w_out_2"][0], 0, 4)
        order += ["mqk", "mv", "mo", "mg", "mout"]
        FG = [(0, 8), (8, 8), (16, 6)]

        def ffn_specs(l):
            wu, wd = view(io["ffn_w_up_2"][l]), io["ffn_w_down_2"][l]
            for g, (f0, n) in enumerate(FG):
                specs[f"fu{l}{g}"] = Weights(n, [(KT, 256, [
                    (0, 128, (lambda f0: lambda b: wu[:, :, bass.ds(b * P + f0 * P, P)])(f0)),
                    (128, 128, (lambda f0: lambda b: wu[:, :, bass.ds(b * P + (FF + f0 * P), P)])(f0))])])
                specs[f"fd{l}{g}"] = plain(wd, 0, 4, t0=f0, tiles=n)
                order.extend([f"fu{l}{g}", f"fd{l}{g}"])

        ffn_specs(0)
        specs["fk"] = plain(KV_W, 0, 4)
        specs["fv"] = row_blocks(KV_W, D, 2)
        specs["ff"] = Weights(1, [(KT, 128, [(0, 16, lambda b: v_kv[:, :, 2048:2064]), (16, 112, lambda b: v_kv[:, :, 0:112])])])
        specs["fq"] = plain(io["fox_w_qg_2"][0], 0, 4)
        specs["fg"] = row_blocks(io["fox_w_qg_2"][0], D, 2)
        specs["fout"] = plain(io["fox_w_out_2"][0], 0, 4)
        order += ["fk", "fv", "ff", "fq", "fg", "fout"]
        ffn_specs(1)

        def after(name):
            i = order.index(name)
            return specs[order[i + 1]] if i + 1 < len(order) else None

        def setup():
            with ExitStack() as ctx:
                x_rows = sb(ctx, "x_rows", [P, TT, D])
                gain_rows = sb(ctx, "gain_rows", [96, P])
                conv_rows = sb(ctx, "conv_rows", [88, 4, P])
                with nc.Block() as block:
                    @block.sync
                    def _(sp):
                        sp.dma_start(x_rows[:, :, :], io["x"][0].rearrange("(t p) d -> p t d", p=P)).then_inc(inputs_in[0].sem, 16)
                        prefetch(sp, specs["q"])

                    @block.scalar
                    def _(act):
                        act.dma_start(const[:, :], io["const"]).then_inc(inputs_in[1].sem, 16)
                        row = 0
                        for name in VECS:
                            v = io[name]
                            n = v.shape[0] if len(v.shape) == 2 else 1
                            src = v.rearrange("l (t p) -> (l t) p", p=P) if len(v.shape) == 2 else v.rearrange("(t p) -> t p", p=P)
                            act.dma_start(gain_rows[row:row + n * KT, :], src).then_inc(inputs_in[2].sem, 16)
                            row += n * KT
                        for l in range(2):
                            w = io["ffn_conv_w_2"][l].rearrange("k (t p) -> (k t) p", p=P)
                            act.dma_start(conv_rows[:, 2 * l, :], w[0:88, :]).then_inc(inputs_in[3].sem, 16)
                            act.dma_start(conv_rows[0:44, 2 * l + 1, :], w[88:132, :]).then_inc(inputs_in[3].sem, 16)
                            act.dma_start(conv_rows[44:88, 2 * l + 1, :],
                                          io["ffn_conv_b_2"][l].rearrange("(t p) -> t p", p=P)).then_inc(inputs_in[3].sem, 16)

                    @block.gpsimd
                    def _(pool):
                        for t in led:
                            pool.sem_inc(t.sem, LEAD)
                        pool.memset(ones[:, :], 1.0).then_inc(pool_step.sem, 1)

                    @block.tensor
                    def _(pe):
                        pe.wait_ge(inputs_in[0].sem, 16)
                        pe.wait_ge(inputs_in[1].sem, 16)
                        for k in range(KT):
                            if k >= 4:
                                pe.wait_ge(turned_out.sem, k - 3)
                            for t in range(TT):
                                last = pe.transpose(bank[k % 4][:, t * P:(t + 1) * P], x_rows[:, t, k * P:(k + 1) * P], ident)
                            last.then_inc(turned.sem, 1)
                        pe.wait_ge(inputs_in[2].sem, 16 * len(VECS))
                        pe.transpose(bank[4][:, 0:96], gain_rows[:, :], ident[0:96, 0:96]).then_inc(turned.sem, 1)
                        pe.wait_ge(inputs_in[3].sem, 16 * 6)
                        for j in range(4):
                            last = pe.transpose(bank[5][:, j * 88:(j + 1) * 88], conv_rows[:, j, :], ident[0:88, 0:88])
                        last.then_inc(turned.sem, 1)

                    @block.vector
                    def _(dve):
                        dve.wait_ge(inputs_in[1].sem, 16)
                        dve.tensor_copy(ident_b[:, :], ident)
                        dve.tensor_copy(bias_b[:, :], cst("causal_bias"))
                        dve.tensor_copy(cmpb_b[:, :], cst("cmp_bias"))
                        for k in range(KT):
                            dve.wait_ge(turned.sem, k + 1)
                            dve.tensor_copy(xT[:, k, :], bank[k % 4][:, :]).then_inc(turned_out.sem, 1)
                        dve.wait_ge(turned.sem, KT + 1)
                        dve.tensor_copy(gains[:, :], bank[4][:, 0:96])
                        dve.wait_ge(turned.sem, KT + 2)
                        dve.tensor_copy(conv[:, :, :], bank[5][:, 0:352].rearrange("p (a b) -> p a b", a=4))
            turned.n += KT + 2
            turned_out.n += KT
            pool_step.n += 1
            for t, n in zip(inputs_in, (1, 1, len(VECS), 6)):
                t.n += 16 * n
            for t in led:
                t.n = LEAD

        def norm(name, vec, mode, src=None):
            src = xT if src is None else src
            with ExitStack() as ctx:
                sq = [sb(ctx, f"{name}_sq{r}", [P, S]) for r in range(2)]
                total = sb(ctx, f"{name}_total", [P, S])
                root = sb(ctx, f"{name}_root", [P, S])
                inv = sb(ctx, f"{name}_inv", [P, S])
                y = [sb(ctx, f"{name}_y{r}", [P, S]) for r in range(2)]
                b_sq, b_sum, b_mean, b_root = sq_ready.n, sum_ready.n, mean_ready.n, root_ready.n
                b_sc, b_hi, b_lo = scaled.n, split_hi_done.n, split_lo_done.n
                with nc.Block() as block:
                    @block.scalar
                    def _(act):
                        for k in range(KT):
                            if k >= 2:
                                act.wait_ge(sum_ready.sem, b_sum + k - 1)
                            act.activation(sq[k % 2][:, :], src[:, k, :], ACT.Square).then_inc(sq_ready.sem, 1)
                        act.wait_ge(mean_ready.sem, b_mean + 1)
                        act.activation(root[:, :], bank[0][:, :], ACT.Sqrt, scale=1.0 / D, bias=EPS).then_inc(root_ready.sem, 1)
                        if mode == "parts":
                            for k in range(KT):
                                act.wait_ge(scaled.sem, b_sc + k + 1)
                                act.activation(a_hi[:, k, :], y[k % 2][:, :], ACT.Copy).then_inc(split_hi_done.sem, 1)

                    @block.tensor
                    def _(pe):
                        pe.wait_ge(sum_ready.sem, b_sum + KT)
                        pe.matmul(bank[0][:, :], ones[:, :], total[:, :], start=True, stop=True).then_inc(mean_ready.sem, 1)

                    @block.vector
                    def _(dve):
                        for k in range(KT):
                            dve.wait_ge(sq_ready.sem, b_sq + k + 1)
                            if k == 0:
                                dve.tensor_copy(total[:, :], sq[0][:, :]).then_inc(sum_ready.sem, 1)
                            else:
                                dve.wait_ge(sum_ready.sem, b_sum + k)
                                dve.tensor_tensor(total[:, :], total[:, :], sq[k % 2][:, :], ALU.add).then_inc(sum_ready.sem, 1)
                        dve.wait_ge(root_ready.sem, b_root + 1)
                        dve.reciprocal(inv[:, :], root[:, :])
                        dve.drain()

                        def lo(k):
                            dve.wait_ge(split_hi_done.sem, b_hi + k + 1)
                            dve.tensor_tensor(a_lo[:, k, :], y[k % 2][:, :], a_hi[:, k, :].bitcast(F32),
                                              ALU.subtract).then_inc(split_lo_done.sem, 1)
                        for k in range(KT):
                            g = gains[:, vec * KT + k:vec * KT + k + 1]
                            dst = xT[:, k, :] if mode == "x" else y[k % 2][:, :]
                            if mode == "parts" and k >= 2:
                                lo(k - 2)
                                dve.wait_ge(split_lo_done.sem, b_lo + k - 1)
                            dve.scalar_tensor_tensor(dst, src[:, k, :], g, inv[:, :], ALU.mult, ALU.mult).then_inc(scaled.sem, 1)
                            if mode == "add":
                                dve.wait_ge(scaled.sem, b_sc + k + 1)
                                dve.tensor_tensor(xT[:, k, :], xT[:, k, :], dst, ALU.add)
                        if mode == "parts":
                            lo(KT - 2)
                            lo(KT - 1)
                sq_ready.n += KT
                sum_ready.n += KT
                mean_ready.n += 1
                root_ready.n += 1
                scaled.n += KT
                if mode == "parts":
                    split_hi_done.n += KT
                    split_lo_done.n += KT

        def copy_to(dst, per=2):
            def evac(dve, b, slot, m):
                dve.wait_ge(products_done.sem, m["prod"] + b + 1)
                for c in range(per):
                    ins = dve.tensor_copy(dst[:, bass.ds(b * 2 + c, 1), :], bank[2 * slot + c][:, :])
                ins.then_inc(evacuated.sem, 1)
            return evac

        def add_to(dst):
            def evac(dve, b, slot, m):
                dve.wait_ge(products_done.sem, m["prod"] + b + 1)
                for c in range(2):
                    y = dst[:, bass.ds(b * 2 + c, 1), :]
                    ins = dve.tensor_tensor(y, bank[2 * slot + c][:, None, :], y, ALU.add)
                ins.then_inc(evacuated.sem, 1)
            return evac

        def to_features(src, tiles, hi, lo, first=0):
            b_t, b_h, b_o = turned.n, turned_hi.n, turned_out.n
            with nc.Block() as block:
                @block.tensor
                def _(pe):
                    for k in range(tiles):
                        if k >= 4:
                            pe.wait_ge(turned_out.sem, b_o + k - 3)
                        for t in range(TT):
                            last = pe.transpose(bank[k % 4][:, t * P:(t + 1) * P], src[:, t, k * P:(k + 1) * P], ident)
                        last.then_inc(turned.sem, 1)

                @block.scalar
                def _(act):
                    for k in range(tiles):
                        act.wait_ge(turned.sem, b_t + k + 1)
                        act.activation(hi[:, first + k, :], bank[k % 4][:, :], ACT.Copy).then_inc(turned_hi.sem, 1)

                @block.vector
                def _(dve):
                    for k in range(tiles):
                        dve.wait_ge(turned_hi.sem, b_h + k + 1)
                        dve.tensor_tensor(lo[:, first + k, :], bank[k % 4][:, :], hi[:, first + k, :].bitcast(F32),
                                          ALU.subtract).then_inc(turned_out.sem, 1)
            turned.n += tiles
            turned_hi.n += tiles
            turned_out.n += tiles

        def rope_tables(ctx, name, freq, cos, sin):
            pos_i = sb(ctx, f"{name}_pos_i", [P, S], I32)
            ang = sb(ctx, f"{name}_ang", [P, S])
            turns = sb(ctx, f"{name}_turns", [P, S])
            rest = sb(ctx, f"{name}_rest", [P, S])
            a0 = at["angles"][0]
            b_in, b_a, b_d = inputs_in[0].n, act_step.n, dve_step.n
            with nc.Block() as block:
                @block.sync
                def _(sp):
                    sp.dma_start(pos_i[:, :], io["positions"][0:1, :].broadcast_to([P, S])).then_inc(inputs_in[0].sem, 16)

                @block.vector
                def _(dve):
                    dve.wait_ge(inputs_in[0].sem, b_in + 16)
                    dve.tensor_copy(ang[:, :], pos_i[:, :])
                    dve.drain()
                    dve.tensor_scalar(ang[:, :], ang[:, :], const[:, a0 + freq:a0 + freq + 1], None, ALU.mult)
                    dve.drain()
                    dve.tensor_scalar(turns[:, :], ang[:, :], 1.0 / (2 * PI), ROUND, ALU.mult, ALU.add)
                    dve.drain()
                    dve.tensor_scalar(turns[:, :], turns[:, :], ROUND, None, ALU.subtract)
                    dve.drain()
                    dve.scalar_tensor_tensor(rest[:, :], turns[:, :], -TWO_PI_HI, ang[:, :], ALU.mult, ALU.add)
                    dve.drain()
                    dve.scalar_tensor_tensor(rest[:, :], turns[:, :], -TWO_PI_LO, rest[:, :], ALU.mult, ALU.add)
                    dve.drain()
                    dve.tensor_scalar(rest[:, :], rest[:, :], SIN_MAX, -SIN_MAX, ALU.min, ALU.max).then_inc(dve_step.sem, 1)
                    dve.wait_ge(dve_step.sem, b_d + 1)
                    dve.scalar_tensor_tensor(turns[:, :], rest[:, :], -1.0, rest[:, :], ALU.mult, ALU.min)
                    dve.drain()
                    dve.tensor_scalar(turns[:, :], turns[:, :], PI / 2, None, ALU.add).then_inc(dve_step.sem, 1)
                    dve.wait_ge(act_step.sem, b_a + 1)
                    dve.tensor_scalar(sin[:, :], sin[:, :], const[:, a0 + freq + 1:a0 + freq + 2], None, ALU.mult)

                @block.scalar
                def _(act):
                    act.wait_ge(dve_step.sem, b_d + 1)
                    act.activation(sin[:, :], rest[:, :], ACT.Sin).then_inc(act_step.sem, 1)
                    act.wait_ge(dve_step.sem, b_d + 2)
                    act.activation(cos[:, :], turns[:, :], ACT.Sin)
            inputs_in[0].n += 16
            act_step.n += 1
            dve_step.n += 2

        def rotate(ctx, name, x, lo, hi, swap, cos, sin):
            along = [sb(ctx, f"{name}_along{r}", [P, S]) for r in range(2)]
            across = [sb(ctx, f"{name}_across{r}", [P, S]) for r in range(2)]
            b_p, b_d = pe_step.n, dve_step.n
            with nc.Block() as block:
                @block.tensor
                def _(pe):
                    for i, k in enumerate(range(lo, hi)):
                        if i >= 2:
                            pe.wait_ge(dve_step.sem, b_d + i - 1)
                        pe.matmul(bank[i % 2][:, :], swap, x[:, k, :], start=True, stop=True).then_inc(pe_step.sem, 1)

                @block.vector
                def _(dve):
                    for i, k in enumerate(range(lo, hi)):
                        dve.tensor_tensor(along[i % 2][:, :], x[:, k, :], cos[:, :], ALU.mult)
                        dve.wait_ge(pe_step.sem, b_p + i + 1)
                        dve.tensor_tensor(across[i % 2][:, :], bank[i % 2][:, :], sin[:, :], ALU.mult).then_inc(dve_step.sem, 1)
                        dve.drain()
                        dve.tensor_tensor(x[:, k, :], along[i % 2][:, :], across[i % 2][:, :], ALU.add)
            pe_step.n += hi - lo
            dve_step.n += hi - lo

        def attention(name, pairs_n, q, k, k_static, v_of, finish_unit, bias_rows=None):
            U = 2 * TT
            with ExitStack() as ctx:
                q_st = sb(ctx, f"{name}_q_st", [P, S])
                k_st = None if k_static else sb(ctx, f"{name}_k_st", [P, S])
                probs = [sb(ctx, f"{name}_probs{r}", [P, S]) for r in range(2)]
                probs_t = [sb(ctx, f"{name}_probs_t{r}", [P, TT, P]) for r in range(2)]
                neg_max = [sb(ctx, f"{name}_neg_max{r}", [P, 1]) for r in range(2)]
                row_sum = [sb(ctx, f"{name}_row_sum{r}", [P, 1]) for r in range(4)]
                inv = [sb(ctx, f"{name}_inv{r}", [P, 1]) for r in range(2)]
                rows = [sb(ctx, f"{name}_bias{r}", [P, S]) for r in range(2)] if bias_rows is not None else None
                logits = [sb(ctx, f"{name}_logits{r}", [P, S]) for r in range(2)] if bias_rows is not None else None
                b_st, b_s, b_m, b_p = staged.n, scores_ready.n, max_ready.n, probs_ready.n
                b_ks = keys_staged.n
                b_t, b_c, b_o, b_d = probs_turned.n, probs_copied.n, out_ready.n, out_done.n
                b_r, b_ru = [t.n for t in bias_row_in], bias_row_used.n
                keys = k if k_static else k_st
                with nc.Block() as block:
                    if not k_static:
                        @block.gpsimd
                        def _(pool):
                            with pool.Fori(0, pairs_n) as c:
                                pool.wait_ge(scores_ready.sem, b_s + c * U)
                                pool.tensor_copy(k_st[:, None, :], k[:, bass.ds(c, 1), :]).then_inc(keys_staged.sem, 1)

                    if bias_rows is not None:
                        @block.sync
                        def _(sp):
                            with sp.Fori(0, pairs_n) as c:
                                for e in range(2):
                                    sp.wait_ge(bias_row_used.sem, b_ru + c * U + (e * TT - TT))
                                    sp.dma_start(rows[e][:, :], bias_rows[bass.ds(c * 2 + e, 1), :].broadcast_to([P, S]))\
                                        .then_inc(bias_row_in[e].sem, 16)

                    @block.tensor
                    def _(pe):
                        with pe.Fori(0, pairs_n) as c:
                            pe.wait_ge(staged.sem, b_st + c + 1)
                            if not k_static:
                                pe.wait_ge(keys_staged.sem, b_ks + c + 1)

                            def score(u):
                                e, i = u // TT, u % TT
                                n = (i + 1) * P
                                pe.wait_ge(probs_ready.sem, b_p + c * U + (u - 1))
                                out = bank[u % 2]
                                if bias_rows is not None:
                                    pe.wait_ge(bias_row_used.sem, b_ru + c * U + (u - 1))
                                pe.matmul(out[:, 0:n], q_st[64 * e:64 * e + 64, i * P:n], keys[64 * e:64 * e + 64, 0:n],
                                          start=True, stop=False)
                                pe.matmul(out[:, i * P:n], ident_b[:, :], bias_b[:, :], start=False,
                                          stop=True).then_inc(scores_ready.sem, 1)

                            def turn(u):
                                i = u % TT
                                pe.wait_ge(probs_ready.sem, b_p + c * U + (u + 1))
                                pe.wait_ge(probs_copied.sem, b_c + c * U + (u - 1))
                                for j in range(i + 1):
                                    last = pe.transpose(bank[2 + u % 2][:, j * P:(j + 1) * P], probs[u % 2][:, j * P:(j + 1) * P], ident)
                                last.then_inc(probs_turned.sem, 1)

                            def values(u):
                                e, i = u // TT, u % TT
                                pe.wait_ge(probs_copied.sem, b_c + c * U + (u + 1))
                                pe.wait_ge(out_done.sem, b_d + c * U + (u - 1))
                                for j in range(i + 1):
                                    last = pe.matmul(bank[4 + u % 2][:, 0:HD], probs_t[u % 2][:, j, :], v_of(c, e, j),
                                                     start=j == 0, stop=j == i)
                                last.then_inc(out_ready.sem, 1)
                            for step in range(U + 2):
                                if step < U:
                                    score(step)
                                if 1 <= step <= U:
                                    turn(step - 1)
                                if step >= 2:
                                    values(step - 2)

                    @block.vector
                    def _(dve):
                        with dve.Fori(0, pairs_n) as c:
                            def maximum(u):
                                e, n = u // TT, (u % TT + 1) * P
                                dve.wait_ge(scores_ready.sem, b_s + c * U + (u + 1))
                                dve.wait_ge(probs_ready.sem, b_p + c * U + (u - 1))
                                x = bank[u % 2]
                                if bias_rows is not None:
                                    if u % TT == 0:
                                        dve.wait_ge(bias_row_in[e].sem, b_r[e] + (c + 1) * 16)
                                    dve.tensor_tensor(logits[u % 2][:, 0:n], x[:, 0:n], rows[e][:, 0:n], ALU.add).then_inc(bias_row_used.sem, 1)
                                    dve.wait_ge(bias_row_used.sem, b_ru + c * U + (u + 1))
                                    x = logits[u % 2]
                                dve.tensor_reduce(neg_max[u % 2][:, :], x[:, 0:n], AX_X, ALU.max, negate=True).then_inc(max_ready.sem, 1)

                            def take(u):
                                e, i = u // TT, u % TT
                                dve.wait_ge(out_ready.sem, b_o + c * U + (u + 1))
                                dve.reciprocal(inv[u % 2][:, :], row_sum[u % 4][:, :])
                                dve.drain()
                                finish_unit(dve, c, e, i, bank[4 + u % 2][:, 0:HD], inv[u % 2][:, :]).then_inc(out_done.sem, 1)
                            for step in range(U + 2):
                                if step < U:
                                    maximum(step)
                                if step >= 2:
                                    take(step - 2)

                    @block.scalar
                    def _(act):
                        with act.Fori(0, pairs_n) as c:
                            act.wait_ge(scores_ready.sem, b_s + c * U)
                            act.activation(q_st[:, None, :], q[:, bass.ds(c, 1), :], ACT.Copy, scale=float(HD) ** -0.5).then_inc(staged.sem, 1)

                            def exponential(u):
                                n = (u % TT + 1) * P
                                act.wait_ge(max_ready.sem, b_m + c * U + (u + 1))
                                act.wait_ge(probs_turned.sem, b_t + c * U + (u - 1))
                                act.wait_ge(out_done.sem, b_d + c * U + (u - 3))
                                x = bank[u % 2] if bias_rows is None else logits[u % 2]
                                act.activation(probs[u % 2][:, 0:n], x[:, 0:n], ACT.Exp, bias=neg_max[u % 2][:, :],
                                               accum_out=row_sum[u % 4][:, :]).then_inc(probs_ready.sem, 1)

                            def copy(u):
                                i = u % TT
                                act.wait_ge(probs_turned.sem, b_t + c * U + (u + 1))
                                act.wait_ge(out_ready.sem, b_o + c * U + (u - 1))
                                act.activation(probs_t[u % 2][:, 0:i + 1, :],
                                               bank[2 + u % 2][:, 0:(i + 1) * P].rearrange("p (j t) -> p j t", t=P),
                                               ACT.Copy).then_inc(probs_copied.sem, 1)
                            for step in range(U + 1):
                                if step < U:
                                    exponential(step)
                                if step >= 1:
                                    copy(step - 1)
                staged.n += pairs_n
                keys_staged.n += 0 if k_static else pairs_n
                for t in (scores_ready, max_ready, probs_ready, probs_turned, probs_copied, out_ready, out_done):
                    t.n += pairs_n * U
                if bias_rows is not None:
                    bias_row_used.n += pairs_n * U
                    for t in bias_row_in:
                        t.n += 16 * pairs_n

        def linear_attention(name, heads, dk, q, k, v, dv, scale, take, decay_of=None, gates=None):
            turns_n = heads // 2
            per = P // dk
            with ExitStack() as ctx:
                k_st = [sb(ctx, f"{name}_k_st{e}", [P, S]) for e in range(2)]
                q_st = [sb(ctx, f"{name}_q_st{e}", [P, S]) for e in range(2)]
                wts = [sb(ctx, f"{name}_wts{e}", [P, TT, S]) for e in range(2)]
                dec = sb(ctx, f"{name}_dec", [P, TT, S]) if gates else None
                m_row = [sb(ctx, f"{name}_m_row{e}", [P, S]) for e in range(2)] if gates else None
                b_st, b_s, b_w, b_o, b_d = staged.n, scores_ready.n, weighted.n, out_ready.n, out_done.n
                b_g, b_e, b_k = gap_ready.n, decay_ready.n, kept.n
                b_r = [t.n for t in bias_row_in]
                U = 2 * TT
                n_st = 2 if per == 2 else 4
                with nc.Block() as block:
                    if gates:
                        @block.sync
                        def _(sp):
                            with sp.Fori(0, turns_n) as c:
                                for e in range(2):
                                    sp.wait_ge(gap_ready.sem, b_g + c * U + (e * TT - TT))
                                    sp.dma_start(m_row[e][:, :], gates[0][bass.ds(c * 2 + e, 1), :].broadcast_to([P, S]))\
                                        .then_inc(bias_row_in[e].sem, 16)

                        @block.scalar
                        def _(act):
                            with act.Fori(0, turns_n) as c:
                                for u in range(U):
                                    j = u % TT
                                    act.wait_ge(gap_ready.sem, b_g + c * U + (u + 1))
                                    act.activation(dec[:, j, j * P:S], dec[:, j, j * P:S], ACT.Exp).then_inc(decay_ready.sem, 1)

                    @block.gpsimd
                    def _(pool):
                        with pool.Fori(0, turns_n) as c:
                            pool.wait_ge(scores_ready.sem, b_s + c * U)
                            for e in range(n_st // 2):
                                x = c if per == 2 else c * 2 + e
                                pool.tensor_copy(k_st[e][:, None, :], k[:, bass.ds(x, 1), :]).then_inc(staged.sem, 1)
                                pool.tensor_copy(q_st[e][:, None, :], q[:, bass.ds(x, 1), :]).then_inc(staged.sem, 1)
                            if gates:
                                for u in range(U):
                                    j = u % TT
                                    pool.wait_ge(decay_ready.sem, b_e + c * U + (u + 1))
                                    pool.tensor_tensor(dec[:, j, j * P:(j + 1) * P], dec[:, j, j * P:(j + 1) * P],
                                                       cst("causal_keep"), ALU.mult).then_inc(kept.sem, 1)

                    @block.tensor
                    def _(pe):
                        with pe.Fori(0, turns_n) as c:
                            pe.wait_ge(staged.sem, b_st + (c + 1) * n_st)
                            for u in range(U):
                                e, j = u // TT, u % TT
                                pe.wait_ge(weighted.sem, b_w + c * U + (u - 3))
                                if per == 2:
                                    kk, qq = k_st[0][64 * e:64 * e + 64, :], q_st[0][64 * e:64 * e + 64, :]
                                else:
                                    kk, qq = k_st[e][:, :], q_st[e][:, :]
                                pe.matmul(bank[j][:, j * P:S], kk[:, j * P:(j + 1) * P], qq[:, j * P:S],
                                          start=True, stop=True).then_inc(scores_ready.sem, 1)
                            for u in range(U):
                                e, i = u // TT, u % TT
                                pe.wait_ge(weighted.sem, b_w + c * U + (e * TT + i + 1))
                                pe.wait_ge(out_done.sem, b_d + c * U + (u - 1))
                                for j in range(i + 1):
                                    last = pe.matmul(bank[4 + u % 2][:, 0:dv], wts[e][:, j, i * P:(i + 1) * P], v(c, e, j),
                                                     start=j == 0, stop=j == i)
                                last.then_inc(out_ready.sem, 1)

                    @block.vector
                    def _(dve):
                        with dve.Fori(0, turns_n) as c:
                            def gap(u):
                                e, j = u // TT, u % TT
                                if j == 0:
                                    dve.wait_ge(bias_row_in[e].sem, b_r[e] + (c + 1) * 16)
                                dve.wait_ge(weighted.sem, b_w + c * U + (u - 3))
                                dve.tensor_scalar(dec[:, j, j * P:S], m_row[e][:, j * P:S], gates[1][:, j, bass.ds(c * 2 + e, 1)],
                                                  0.0, ALU.add, ALU.min).then_inc(gap_ready.sem, 1)

                            def weigh(u):
                                e, j = u // TT, u % TT
                                n = S - j * P
                                dve.wait_ge(scores_ready.sem, b_s + c * U + (u + 1))
                                if gates:
                                    dve.wait_ge(kept.sem, b_k + c * U + (u + 1))
                                    d = dec[:, j, j * P:S]
                                else:
                                    d = decay_of(c * 2 + e)[:, :, 0:n]
                                if j == 0:
                                    dve.wait_ge(out_ready.sem, b_o + c * U + (e * TT - TT))
                                o, s = wts[e][:, j, j * P:S], bank[j][:, j * P:S]
                                if not gates:
                                    o, s = o[:, None, :], s[:, None, :]
                                dve.scalar_tensor_tensor(o, s, scale, d, ALU.mult, ALU.mult).then_inc(weighted.sem, 1)

                            if gates:
                                for u in range(TT):
                                    gap(u)
                            for u in range(U):
                                weigh(u)
                                if gates and u + TT < U:
                                    gap(u + TT)
                            for u in range(U):
                                e, i = u // TT, u % TT
                                dve.wait_ge(out_ready.sem, b_o + c * U + (u + 1))
                                take(dve, c, e, i, bank[4 + u % 2][:, 0:dv]).then_inc(out_done.sem, 1)
                staged.n += turns_n * n_st
                for t in (scores_ready, weighted, out_ready, out_done):
                    t.n += turns_n * U
                if gates:
                    for t in (gap_ready, decay_ready, kept):
                        t.n += turns_n * U
                    for t in bias_row_in:
                        t.n += 16 * turns_n

        def head_norm(name, h, heads, gate, extra=None):
            with ExitStack() as ctx:
                sq = sb(ctx, f"{name}_hsq", [P, TT, heads * P])
                ss = sb(ctx, f"{name}_hss", [P, TT * heads])
                b_a, b_d = act_step.n, dve_step.n
                flat = lambda x: x[:, :, :].rearrange("p t (h d) -> p (t h) d", d=P)
                with nc.Block() as block:
                    @block.scalar
                    def _(act):
                        act.activation(sq[:, :, :], h[:, :, :], ACT.Square).then_inc(act_step.sem, 1)
                        act.wait_ge(dve_step.sem, b_d + 1)
                        act.activation(ss[:, :], ss[:, :], ACT.Sqrt, scale=1.0 / P, bias=EPS).then_inc(act_step.sem, 1)

                    @block.vector
                    def _(dve):
                        dve.wait_ge(act_step.sem, b_a + 1)
                        dve.tensor_reduce(ss[:, :], flat(sq), AX_X, ALU.add).then_inc(dve_step.sem, 1)
                        dve.tensor_tensor(h[:, :, :], h[:, :, :], gate[:, :, :], ALU.mult)
                        dve.drain()
                        if extra is not None:
                            dve.tensor_tensor(h[:, :, :], h[:, :, :], extra[:, None, :].broadcast_to([P, TT, heads * P]), ALU.mult)
                            dve.drain()
                        dve.wait_ge(act_step.sem, b_a + 2)
                        dve.reciprocal(ss[:, :], ss[:, :])
                        dve.drain()
                        dve.tensor_tensor(flat(h), flat(h), ss[:, :, None].broadcast_to([P, TT * heads, P]), ALU.mult)
                act_step.n += 2
                dve_step.n += 1

        def compressed(ctx, kv, k_cmp, v_cmp):
            pe_rows = sb(ctx, "pe_rows", [CB, 2, 2, HD])
            pe_t = sb(ctx, "pe_t", [P, 2, CB])
            w1 = sb(ctx, "cmp_w1", [P, CB, CH])
            w2 = sb(ctx, "cmp_w2", [P, 2, 2, HD])
            blk = sb(ctx, "cmp_blk", [P, CB, NC + 1])
            hid = sb(ctx, "cmp_hid", [P, 2, 2, NC + 1])
            b_in = [t.n for t in inputs_in]
            b_p, b_d, b_a = pe_step.n, dve_step.n, act_step.n
            with nc.Block() as block:
                @block.sync
                def _(sp):
                    for s, n in enumerate(("cmp_pos_k", "cmp_pos_v")):
                        for g in range(KV):
                            sp.dma_start(pe_rows[:, s, g, :], io[n][0]).then_inc(inputs_in[0].sem, 16)
                    for s, n in enumerate(("cmp_k_w2", "cmp_v_w2")):
                        sp.dma_start(w2[:, s, :, :], io[n][0].rearrange("(t p) d -> p t d", p=P)).then_inc(inputs_in[3].sem, 16)
                    for s, n in enumerate(("cmp_k_w1", "cmp_v_w1")):
                        w = io[n][0].rearrange("(l d) n -> d l n", d=HD)
                        if s == 1:
                            sp.wait_ge(pe_step.sem, b_p + 4)
                        for g in range(KV):
                            sp.dma_start(w1[64 * g:64 * g + 64, :, :], w).then_inc(inputs_in[1 + s].sem, 16)

                @block.tensor
                def _(pe):
                    pe.wait_ge(inputs_in[0].sem, b_in[0] + 64)
                    for s in range(2):
                        last = pe.transpose(bank[0][:, s * CB:(s + 1) * CB], pe_rows[:, s, :, :].rearrange("l g d -> l (g d)"), ident[0:CB, 0:CB])
                    last.then_inc(pe_step.sem, 1)
                    for s in range(2):
                        pe.wait_ge(inputs_in[1 + s].sem, b_in[1 + s] + 32)
                        pe.wait_ge(dve_step.sem, b_d + s + 2)
                        if s == 1:
                            pe.wait_ge(act_step.sem, b_a + 2)
                        for g in range(KV):
                            for t in range(2):
                                out = bank[2 + 2 * g + t][:, 0:NC]
                                for l in range(CB):
                                    last = pe.matmul(out, w1[64 * g:64 * g + 64, l, t * P:(t + 1) * P], blk[64 * g:64 * g + 64, l, 0:NC],
                                                     start=l == 0, stop=l == CB - 1)
                            last.then_inc(pe_step.sem, 1)
                        pe.wait_ge(inputs_in[3].sem, b_in[3] + 32)
                        for g in range(KV):
                            pe.wait_ge(act_step.sem, b_a + 2 * s + g + 1)
                            for t in range(2):
                                if s == 0:
                                    last = pe.matmul(bank[6][64 * g:64 * g + 64, 0:NC], w2[:, s, t, :], hid[:, g, t, 0:NC], start=t == 0, stop=t == 1)
                                else:
                                    last = pe.matmul(bank[7][0:NC, g * HD:(g + 1) * HD], hid[:, g, t, 0:NC], w2[:, s, t, :], start=t == 0, stop=t == 1)
                        last.then_inc(pe_step.sem, 1)

                @block.scalar
                def _(act):
                    for s in range(2):
                        for g in range(KV):
                            act.wait_ge(pe_step.sem, b_p + 1 + 3 * s + g + 1)
                            if s == 1 and g == 0:
                                act.wait_ge(pe_step.sem, b_p + 4)
                            for t in range(2):
                                ins = act.activation(hid[:, g, t, 0:NC], bank[2 + 2 * g + t][:, 0:NC], ACT.Silu)
                            ins.then_inc(act_step.sem, 1)

                @block.vector
                def _(dve):
                    dve.wait_ge(pe_step.sem, b_p + 1)
                    dve.tensor_copy(pe_t[:, :, :], bank[0][:, 0:2 * CB].rearrange("p (s l) -> p s l", s=2)).then_inc(dve_step.sem, 1)
                    dve.wait_ge(dve_step.sem, b_d + 1)
                    for s in range(2):
                        if s == 1:
                            dve.wait_ge(pe_step.sem, b_p + 3)
                        for r in range(2):
                            src = kv[:, s, 16 * r:16 * r + 16 * NC].rearrange("p (c l) -> p l c", l=16)
                            ins = dve.tensor_tensor(blk[:, 16 * r:16 * r + 16, 0:NC], src,
                                                    pe_t[:, s, 16 * r:16 * r + 16, None].broadcast_to([P, 16, NC]), ALU.add)
                        ins.then_inc(dve_step.sem, 1)
                    dve.wait_ge(pe_step.sem, b_p + 4)
                    dve.tensor_copy(k_cmp[:, 0:NC], bank[6][:, 0:NC])
                    dve.wait_ge(pe_step.sem, b_p + 7)
                    dve.tensor_copy(v_cmp[0:NC, :], bank[7][0:NC, 0:P])
            inputs_in[0].n += 64
            for s in range(3):
                inputs_in[1 + s].n += 32
            pe_step.n += 7
            dve_step.n += 3
            act_step.n += 4

        def compressed_attention(ctx, q, k_cmp, v_cmp, gates, o):
            probs = [sb(ctx, f"cmp_probs{r}", [P, 2 * TT, CB]) for r in range(2)]
            q_st = [sb(ctx, f"cmp_q_st{r}", [P, S]) for r in range(1)]
            probs_t = sb(ctx, "cmp_probs_t", [CB, 2 * TT, P])
            neg_max = sb(ctx, "cmp_neg_max", [P, 2 * TT])
            row_sum = sb(ctx, "cmp_row_sum", [P, 2 * TT])
            coef = sb(ctx, "cmp_coef", [P, 2 * TT])
            U = 2 * TT
            any_ok = cst("cmp_any")
            b_st, b_s, b_m, b_p = staged.n, scores_ready.n, max_ready.n, probs_ready.n
            b_t, b_c, b_o, b_d = probs_turned.n, probs_copied.n, out_ready.n, out_done.n
            with nc.Block() as block:
                @block.tensor
                def _(pe):
                    with pe.Fori(0, HQ // 2) as c:
                        pe.wait_ge(staged.sem, b_st + c + 1)
                        pe.wait_ge(probs_ready.sem, b_p + c)
                        for u in range(U):
                            e, i = u // TT, u % TT
                            out = bank[e][:, i * CB:i * CB + NC]
                            pe.matmul(out, q_st[0][64 * e:64 * e + 64, i * P:(i + 1) * P], k_cmp[64 * e:64 * e + 64, 0:NC], start=True, stop=False)
                            last = pe.matmul(out, ident_b[:, :], cmpb_b[:, i * CB:i * CB + NC], start=False, stop=True)
                        last.then_inc(scores_ready.sem, 1)
                        pe.wait_ge(probs_ready.sem, b_p + c + 1)
                        pe.wait_ge(probs_copied.sem, b_c + c)
                        for u in range(U):
                            last = pe.transpose(bank[2 + u // TT][0:NC, (u % TT) * P:(u % TT + 1) * P], probs[0][:, u, 0:NC], ident)
                        last.then_inc(probs_turned.sem, 1)
                        pe.wait_ge(probs_copied.sem, b_c + c + 1)
                        pe.wait_ge(out_done.sem, b_d + c)
                        for u in range(U):
                            e = u // TT
                            last = pe.matmul(bank[4][:, u * HD:(u + 1) * HD], probs_t[0:NC, u, :], v_cmp[0:NC, e * HD:(e + 1) * HD], start=True, stop=True)
                        last.then_inc(out_ready.sem, 1)

                @block.vector
                def _(dve):
                    with dve.Fori(0, HQ // 2) as c:
                        dve.wait_ge(scores_ready.sem, b_s + c + 1)
                        for e in range(2):
                            ins = dve.tensor_reduce(neg_max[:, e * TT:(e + 1) * TT],
                                                    bank[e][:, 0:TT * CB].rearrange("p (i c) -> p i c", c=CB)[:, :, 0:NC], AX_X, ALU.max, negate=True)
                        ins.then_inc(max_ready.sem, 1)
                        dve.wait_ge(probs_ready.sem, b_p + c + 1)
                        dve.reciprocal(row_sum[:, :], row_sum[:, :])
                        dve.drain()
                        for e in range(2):
                            g = gates[:, :, :].rearrange("p i (e c b) -> p i e c b", e=2, b=3)[:, :, e, bass.ds(c, 1), 0:1]
                            dve.tensor_tensor(coef[:, e * TT:(e + 1) * TT, None, None], row_sum[:, e * TT:(e + 1) * TT, None, None], g, ALU.mult)
                        dve.drain()
                        for e in range(2):
                            dve.tensor_tensor(coef[:, e * TT:(e + 1) * TT], coef[:, e * TT:(e + 1) * TT], any_ok, ALU.mult)
                        dve.drain()
                        dve.wait_ge(probs_turned.sem, b_t + c + 1)
                        for e in range(2):
                            ins = dve.tensor_copy(probs_t[0:NC, e * TT:(e + 1) * TT, :], bank[2 + e][0:NC, :].rearrange("c (i t) -> c i t", t=P))
                        ins.then_inc(probs_copied.sem, 1)
                        dve.wait_ge(out_ready.sem, b_o + c + 1)
                        for u in range(U):
                            e, i = u // TT, u % TT
                            dst = o[:, i, :].rearrange("p (e c d) -> p e c d", e=2, d=HD)[:, e, bass.ds(c, 1), :]
                            ins = dve.tensor_scalar(dst, bank[4][:, None, u * HD:(u + 1) * HD], coef[:, u:u + 1], None, ALU.mult)
                        ins.then_inc(out_done.sem, 1)

                @block.scalar
                def _(act):
                    with act.Fori(0, HQ // 2) as c:
                        act.wait_ge(scores_ready.sem, b_s + c)
                        act.activation(q_st[0][:, None, :], q[:, bass.ds(c, 1), :], ACT.Copy, scale=float(HD) ** -0.5).then_inc(staged.sem, 1)
                        act.wait_ge(max_ready.sem, b_m + c + 1)
                        act.wait_ge(out_done.sem, b_d + c)
                        for u in range(U):
                            e, i = u // TT, u % TT
                            ins = act.activation(probs[0][:, u, 0:NC], bank[e][:, i * CB:i * CB + NC], ACT.Exp, bias=neg_max[:, u:u + 1],
                                                 accum_out=row_sum[:, u:u + 1])
                        ins.then_inc(probs_ready.sem, 1)
            for t in (staged, scores_ready, max_ready, probs_ready, probs_turned, probs_copied, out_ready, out_done):
                t.n += HQ // 2

        def nsa(h_hi, h_lo):
            with ExitStack() as ctx:
                qk = sb(ctx, "nsa_qk", [P, 8, S])
                vg = sb(ctx, "nsa_vg", [P, TT, 280])
                o = sb(ctx, "nsa_o", [P, TT, HQ * HD])
                cos, sin = sb(ctx, "nsa_cos", [P, S]), sb(ctx, "nsa_sin", [P, S])
                gate = sb(ctx, "nsa_gate", [P, TT, GATES])
                k_cmp, v_cmp = sb(ctx, "k_cmp", [P, CB]), sb(ctx, "v_cmp", [CB, P])
                with ExitStack() as inner:
                    rope_tables(inner, "nsa", 0, cos, sin)
                dense(specs["q"], after("q"), two_chunks(a_tiles), copy_to(qk))
                dense(specs["kcvc"], after("kcvc"), two_chunks(a_tiles), copy_to(qk[:, 4:8, :]))

                def take_rows(dve, g, t):
                    return dve.tensor_copy(vg[:, t, :], bank[t][:, 0:280])
                dense_rows(specs["vg"], after("vg"), evac_dve=take_rows)
                with ExitStack() as inner:
                    rotate(inner, "nsa_a", qk, 0, 5, cst("swap_nsa"), cos, sin)
                with ExitStack() as inner:
                    rotate(inner, "nsa_b", qk, 6, 8, cst("swap_nsa"), cos, sin)
                with nc.Block() as block:
                    @block.scalar
                    def _(act):
                        act.activation(gate[:, :, :], vg[:, :, 256:280], ACT.Sigmoid)
                with ExitStack() as inner:
                    compressed(inner, qk[:, 4:6, :], k_cmp, v_cmp)
                with ExitStack() as inner:
                    compressed_attention(inner, qk, k_cmp, v_cmp, gate, o)
                coef = sb(ctx, "nsa_coef", [P, 1])

                def branch(b):
                    def finish_unit(dve, c, e, i, out, inv):
                        g = gate[:, i, :].rearrange("p (e c b) -> p e c b", e=2, b=3)[:, e, bass.ds(c, 1), b:b + 1]
                        dve.tensor_tensor(coef[:, :, None], inv[:, :, None], g, ALU.mult)
                        dve.drain()
                        dst = o[:, i, :].rearrange("p (e c d) -> p e c d", e=2, d=HD)[:, e, bass.ds(c, 1), :]
                        return dve.scalar_tensor_tensor(dst, out[:, None, :], coef[:, :], dst, ALU.mult, ALU.add)
                    return finish_unit
                attention("slc", HQ // 2, qk, qk[:, 6, :], True, lambda c, e, j: vg[:, j, e * HD:(e + 1) * HD], branch(1))
                attention("win", HQ // 2, qk, qk[:, 7, :], True, lambda c, e, j: vg[:, j, P + e * HD:P + (e + 1) * HD], branch(2))
                to_features(o, 4, h_hi, h_lo, 0)

        def retention(h_hi, h_lo):
            with ExitStack() as ctx:
                qk = sb(ctx, "ret_qk", [P, 8, S])
                vg = sb(ctx, "ret_vg", [P, TT, 2, RH * RD])
                h = sb(ctx, "ret_h", [P, TT, RH * RD])
                dense(specs["rqk"], after("rqk"), two_chunks(a_tiles), copy_to(qk))

                def take_rows(dve, g, t):
                    return dve.tensor_copy(vg[:, t, bass.ds(g, 1), :], bank[t][:, None, :])
                dense_rows(specs["rvg"], after("rvg"), evac_dve=take_rows)
                with ExitStack() as inner:
                    cos, sin = sb(inner, "ret_cos", [P, S]), sb(inner, "ret_sin", [P, S])
                    rope_tables(inner, "ret", 2, cos, sin)
                    rotate(inner, "ret", qk, 0, 8, cst("swap_ret"), cos, sin)
                with ExitStack() as inner:
                    decay = sb(inner, "ret_decay", [P, RH, S])
                    b_in = inputs_in[0].n
                    with nc.Block() as block:
                        @block.sync
                        def _(sp):
                            sp.dma_start(decay[:, :, :], io["decay"]).then_inc(inputs_in[0].sem, 16)
                            sp.wait_ge(inputs_in[0].sem, b_in + 16)

                        @block.scalar
                        def _(act):
                            act.activation(vg[:, :, 1, :], vg[:, :, 1, :], ACT.Silu)
                    inputs_in[0].n += 16

                    def take(dve, c, e, i, out):
                        return dve.tensor_copy(h[:, i, bass.ds(c * 256 + e * P, P)], out)
                    linear_attention("ret", RH, RD, qk[:, 0:4, :], qk[:, 4:8, :],
                                     lambda c, e, j: vg[:, j, 0, bass.ds(c * 256 + e * P, P)], RD, float(RD) ** -0.5,
                                     take, decay_of=lambda x: decay[:, bass.ds(x, 1), :])
                head_norm("ret", h, RH, vg[:, :, 1, :])
                to_features(h, 4, h_hi, h_lo, 4)

        def first_block():
            norm("n1", 0, "parts")
            with ExitStack() as ctx:
                h_hi = sb(ctx, "mix_hi", [P, KT, S], F32R)
                h_lo = sb(ctx, "mix_lo", [P, KT, S], F32R)
                nsa(h_hi, h_lo)
                retention(h_hi, h_lo)
                mix = sb(ctx, "mix", [P, KT, S])
                sig = sb(ctx, "mix_sig", [P, 2, S])
                half_mix = sb(ctx, "half_mix", [P, 2, S])
                h_tiles = [(h_hi[:, k, :], h_lo[:, k, :]) for k in range(KT)]
                chunks = [two_chunks(a_tiles)[0], [[(k * 256 + c * P, h_tiles[4 * c + k]) for k in range(4)] for c in range(2)]]
                even = (stream["slot"]) % 2

                def evac_act(act, b, slot, m):
                    if slot != even:
                        return
                    act.wait_ge(products_done.sem, m["prod"] + b + 1)
                    act.wait_ge(evacuated.sem, m["evac"] + b)
                    for c in range(2):
                        ins = act.activation(sig[:, c, :], bank[2 * slot + c][:, :], ACT.Sigmoid)
                    ins.then_inc(evacuated.sem, 1)

                def evac_dve(dve, b, slot, m):
                    if slot == even:
                        return
                    dve.wait_ge(products_done.sem, m["prod"] + b + 1)
                    dve.wait_ge(evacuated.sem, m["evac"] + b)
                    for c in range(2):
                        dve.tensor_tensor(half_mix[:, c, :], bank[2 * slot + c][:, :], sig[:, c, :], ALU.mult)
                    dve.drain()
                    ch = (b - 1) // 2 if isinstance(b, int) else m["i"]
                    dve.tensor_tensor(mix[:, bass.ds(ch, 1), :], half_mix[:, 0:1, :], half_mix[:, 1:2, :], ALU.add).then_inc(evacuated.sem, 1)
                dense(specs["mix"], after("mix"), chunks, evac_dve, evac_act)
                split_parts(mix, a_hi, a_lo)
            dense(specs["out1"], after("out1"), two_chunks(a_tiles), add_to(xT))
            norm("n2", 1, "parts")
            with ExitStack() as ctx:
                h_hi = sb(ctx, "mlp_hi", [P, KT, S], F32R)
                h_lo = sb(ctx, "mlp_lo", [P, KT, S], F32R)
                pos = [sb(ctx, f"mlp_pos{r}", [P, 2, S]) for r in range(2)]
                h_tiles = [(h_hi[:, k, :], h_lo[:, k, :]) for k in range(KT)]

                def up_dve(dve, b, slot, m):
                    dve.wait_ge(products_done.sem, m["prod"] + b + 1)
                    for c in range(2):
                        ins = dve.tensor_scalar(pos[slot][:, c, :], bank[2 * slot + c][:, :], 0.0, None, ALU.max)
                    ins.then_inc(evacuated.sem, 1)
                    dve.wait_ge(part_ready.sem, m["part"] + b + 1)
                    dve.tensor_tensor(h_lo[:, bass.ds(b * 2, 2), :], pos[slot][:, :, :], h_hi[:, bass.ds(b * 2, 2), :].bitcast(F32),
                                      ALU.subtract).then_inc(hid_ready.sem, 1)

                def up_act(act, b, slot, m):
                    act.wait_ge(evacuated.sem, m["evac"] + b + 1)
                    act.activation(pos[slot][:, :, :], pos[slot][:, :, :], ACT.Square)
                    act.drain()
                    act.activation(h_hi[:, bass.ds(b * 2, 2), :], pos[slot][:, :, :], ACT.Copy).then_inc(part_ready.sem, 1)

                for g in range(4):
                    dense(specs[f"up{g}"], after(f"up{g}"), two_chunks(a_tiles), up_dve, up_act)
                    part_ready.n += 4
                    hid_ready.n += 4
                    dense(specs[f"down{g}"], after(f"down{g}"), two_chunks(h_tiles), add_to(xT))
            norm("n3", 2, "x")

        def split_parts(src, hi, lo):
            b_h = split_hi_done.n
            with nc.Block() as block:
                @block.scalar
                def _(act):
                    for k in range(KT):
                        act.activation(hi[:, k, :], src[:, k, :], ACT.Copy).then_inc(split_hi_done.sem, 1)

                @block.vector
                def _(dve):
                    for k in range(KT):
                        dve.wait_ge(split_hi_done.sem, b_h + k + 1)
                        dve.tensor_tensor(lo[:, k, :], src[:, k, :], hi[:, k, :].bitcast(F32), ALU.subtract)
            split_hi_done.n += KT

        def log_sigmoid(act, dve, x, t1, t2, b_a, b_d, part):
            if part == "dve":
                dve.scalar_tensor_tensor(t1, x, -1.0, x, ALU.mult, ALU.min).then_inc(dve_step.sem, 1)
                dve.tensor_scalar(t2, x, 0.0, None, ALU.min)
                dve.drain()
                dve.wait_ge(act_step.sem, b_a + 1)
                dve.tensor_tensor(x, t2, t1, ALU.subtract)
                dve.drain()
            else:
                act.wait_ge(dve_step.sem, b_d + 1)
                act.activation(t1, t1, ACT.Exp)
                act.drain()
                act.activation(t1, t1, ACT.Ln, bias=1.0).then_inc(act_step.sem, 1)

        def mlstm():
            with ExitStack() as ctx:
                h = sb(ctx, "ml_h", [P, TT, MH * MV])
                with ExitStack() as inner:
                    qk = sb(inner, "ml_qk", [P, 8, S])
                    v = sb(inner, "ml_v", [P, TT, MH, MV + 1])
                    og = sb(inner, "ml_og", [P, TT, MH * MV])
                    a_col = sb(inner, "ml_a_col", [P, TT, MH])
                    e_col = sb(inner, "ml_e_col", [P, TT, MH])
                    dense(specs["mqk"], after("mqk"), two_chunks(a_tiles), copy_to(qk))

                    def v_rows(dve, g, t):
                        return dve.tensor_copy(v[:, t, bass.ds(g * 4, 4), 0:MV], bank[t][:, :].rearrange("p (h d) -> p h d", d=MV))
                    dense_rows(specs["mv"], after("mv"), evac_dve=v_rows)

                    def o_rows(act, g, t):
                        return act.activation(og[:, t, bass.ds(g * 512, 512)], bank[t][:, :], ACT.Sigmoid)
                    dense_rows(specs["mo"], after("mo"), evac_act=o_rows)
                    with ExitStack() as tmp:
                        bias = sb(tmp, "ml_bias", [MH, 2])
                        lf, ig, t1, t2 = (sb(tmp, f"ml_{n}", [MH, S]) for n in ("lf", "ig", "t1", "t2"))
                        fsum, mrun, one = (sb(tmp, f"ml_{n}", [MH, S]) for n in ("fsum", "mrun", "one"))
                        gate_bank = 2 * stream["slot"]

                        def gate_rows(dve, b, slot, m):
                            dve.wait_ge(products_done.sem, m["prod"] + b + 1)
                            dve.tensor_copy(ig[:, :], bank[2 * slot][0:MH, :])
                            dve.tensor_copy(lf[:, :], bank[2 * slot][32:32 + MH, :]).then_inc(evacuated.sem, 1)
                        dense(specs["mg"], after("mg"), [[[(k * P, a_tiles[k]) for k in range(KT)]]], gate_rows)
                        b_in, b_a, b_d, b_p, b_st = inputs_in[0].n, act_step.n, dve_step.n, pe_step.n, rows_stored.n
                        with nc.Block() as block:
                            @block.sync
                            def _(sp):
                                sp.dma_start(bias[:, 0:1], io["mlstm_b_gate_2"][0, 0:MH].rearrange("(h a) -> h a", a=1)).then_inc(inputs_in[0].sem, 16)
                                sp.dma_start(bias[:, 1:2], io["mlstm_b_gate_2"][0, MH:2 * MH].rearrange("(h a) -> h a", a=1)).then_inc(inputs_in[0].sem, 16)
                                sp.wait_ge(dve_step.sem, b_d + 2)
                                sp.dma_start(io["row_scratch"][0:MH, :], t2[:, :]).then_inc(rows_stored.sem, 16)
                                sp.wait_ge(rows_stored.sem, b_st + 16)

                            @block.gpsimd
                            def _(pool):
                                pool.memset(v[:, :, :, MV:MV + 1], 1.0)

                            @block.vector
                            def _(dve):
                                dve.memset(one[:, :], 1.0)
                                dve.wait_ge(inputs_in[0].sem, b_in + 32)
                                dve.tensor_scalar(ig[:, :], ig[:, :], bias[:, 0:1], None, ALU.add)
                                dve.tensor_scalar(lf[:, :], lf[:, :], bias[:, 1:2], None, ALU.add)
                                dve.drain()
                                log_sigmoid(None, dve, lf[:, :], t1[:, :], t2[:, :], b_a, b_d, "dve")
                                dve.tensor_tensor_scan(fsum[:, :], one[:, :], lf[:, :], 0.0, ALU.mult, ALU.add)
                                dve.drain()
                                dve.tensor_tensor(ig[:, :], ig[:, :], fsum[:, :], ALU.subtract)
                                dve.drain()
                                dve.tensor_tensor_scan(mrun[:, :], one[:, :], ig[:, :], 0.0, ALU.mult, ALU.max)
                                dve.drain()
                                dve.tensor_scalar(t2[:, :], mrun[:, :], -1.0, None, ALU.mult)
                                dve.tensor_tensor(t1[:, :], fsum[:, :], mrun[:, :], ALU.add)
                                dve.drain()
                                dve.engine_nop().then_inc(dve_step.sem, 1)
                                dve.wait_ge(pe_step.sem, b_p + 1)
                                dve.tensor_copy(a_col[:, :, :], bank[4][:, 0:TT * MH].rearrange("p (t h) -> p t h", h=MH))
                                dve.wait_ge(pe_step.sem, b_p + 2)
                                dve.tensor_copy(e_col[:, :, :], bank[5][:, 0:TT * MH].rearrange("p (t h) -> p t h", h=MH))

                            @block.scalar
                            def _(act):
                                log_sigmoid(act, None, lf[:, :], t1[:, :], t2[:, :], b_a, b_d, "act")
                                act.wait_ge(dve_step.sem, b_d + 2)
                                act.activation(t1[:, :], t1[:, :], ACT.Exp, scale=-1.0).then_inc(act_step.sem, 1)

                            @block.tensor
                            def _(pe):
                                pe.wait_ge(dve_step.sem, b_d + 2)
                                for t in range(TT):
                                    last = pe.transpose(bank[4][:, t * MH:(t + 1) * MH], ig[:, t * P:(t + 1) * P], ident[0:MH, 0:MH])
                                last.then_inc(pe_step.sem, 1)
                                pe.wait_ge(act_step.sem, b_a + 2)
                                for t in range(TT):
                                    last = pe.transpose(bank[5][:, t * MH:(t + 1) * MH], t1[:, t * P:(t + 1) * P], ident[0:MH, 0:MH])
                                last.then_inc(pe_step.sem, 1)
                        inputs_in[0].n += 32
                        act_step.n += 2
                        dve_step.n += 2
                        pe_step.n += 2
                        rows_stored.n += 16
                    with ExitStack() as tmp:
                        dens = [sb(tmp, f"ml_den{r}", [P, 1]) for r in range(2)]

                        def take(dve, c, e, i, out):
                            den = dens[i % 2]
                            dve.scalar_tensor_tensor(den[:, :], out[:, MV:MV + 1], -1.0, e_col[:, i, bass.ds(c * 2 + e, 1)], ALU.mult, ALU.max)
                            dve.drain()
                            dve.tensor_tensor(den[:, :], out[:, MV:MV + 1], den[:, :], ALU.max)
                            dve.drain()
                            dve.reciprocal(den[:, :], den[:, :])
                            dve.drain()
                            return dve.tensor_scalar(h[:, i, bass.ds(c * 256 + e * P, P)], out[:, 0:MV], den[:, :], None, ALU.mult)
                        linear_attention("ml", MH, MK, qk[:, 0:4, :], qk[:, 4:8, :],
                                         lambda c, e, j: v[:, j, bass.ds(c * 2 + e, 1), :], MV + 1, float(MK) ** -0.5, take,
                                         gates=(io["row_scratch"], a_col))
                    with ExitStack() as tmp:
                        wrow = sb(tmp, "ml_norm", [P, MH * MV])
                        b_in = inputs_in[0].n
                        with nc.Block() as block:
                            @block.sync
                            def _(sp):
                                sp.dma_start(wrow[:, :], io["mlstm_norm_2"][0:1, :].broadcast_to([P, MH * MV])).then_inc(inputs_in[0].sem, 16)
                                sp.wait_ge(inputs_in[0].sem, b_in + 16)
                        inputs_in[0].n += 16
                        head_norm("ml", h, MH, og, wrow)
                to_features(h, KT, a_hi, a_lo)
            post_norm_dense("mout", 5, a_tiles)

        def post_norm_dense(spec, vec, xs):
            with ExitStack() as ctx:
                y = sb(ctx, f"{spec}_y", [P, KT, S])
                dense(specs[spec], after(spec), two_chunks(xs), copy_to(y))
                norm(f"{spec}_n", vec, "add", src=y)

        def ffn(l):
            norm(f"ffn{l}", 7 + l, "parts")
            with ExitStack() as ctx:
                y = sb(ctx, f"ffn{l}_y", [P, KT, S])
                with ExitStack() as inner:
                    h_hi = sb(inner, f"ffn{l}_hi", [P, KT, S], F32R)
                    h_lo = sb(inner, f"ffn{l}_lo", [P, KT, S], F32R)
                    u = [sb(inner, f"ffn{l}_u{r}", [P, 2, S + 2]) for r in range(2)]
                    z = [sb(inner, f"ffn{l}_z{r}", [P, 2, S]) for r in range(2)]
                    h_tiles = [(h_hi[:, k, :], h_lo[:, k, :]) for k in range(KT)]
                    with nc.Block() as block:
                        @block.gpsimd
                        def _(pool):
                            for r in range(2):
                                pool.memset(u[r][:, :, 0:2], 0.0)

                    for g, (f0, n) in enumerate(FG):
                        def tap(j, b, c, f0=f0):
                            return conv[:, 2 * l + j // 2, bass.ds(b + (44 * (j % 2) + FT * c + f0), 1)]

                        def up_act(act, b, slot, m):
                            act.wait_ge(products_done.sem, m["prod"] + b + 1)
                            act.wait_ge(part_used.sem, m["pused"] + 2 * b - 2)
                            for c in range(2):
                                ins = act.activation(u[slot][:, c, 2:S + 2], bank[2 * slot + c][:, :], ACT.Copy)
                            ins.then_inc(evacuated.sem, 1)
                            act.wait_ge(part_used.sem, m["pused"] + 2 * b + 1)
                            act.activation(z[slot][:, 0, :], z[slot][:, 0, :], ACT.Gelu_apprx_tanh).then_inc(gelu_ready.sem, 1)
                            act.wait_ge(hid_ready.sem, m["hid"] + 2 * b + 1)
                            act.activation(h_hi[:, bass.ds(b, 1), :], z[slot][:, 0:1, :], ACT.Copy).then_inc(part_ready.sem, 1)

                        def up_dve(dve, b, slot, m):
                            dve.wait_ge(evacuated.sem, m["evac"] + b + 1)
                            for c in range(2):
                                dve.tensor_scalar(z[slot][:, c, :], u[slot][:, c, 2:S + 2], tap(2, b, c), tap(3, b, c), ALU.mult, ALU.add)
                                dve.drain()
                                dve.scalar_tensor_tensor(z[slot][:, c, :], u[slot][:, c, 1:S + 1], tap(1, b, c), z[slot][:, c, :], ALU.mult, ALU.add)
                                dve.drain()
                                dve.scalar_tensor_tensor(z[slot][:, c, :], u[slot][:, c, 0:S], tap(0, b, c), z[slot][:, c, :],
                                                         ALU.mult, ALU.add).then_inc(part_used.sem, 1)
                            dve.wait_ge(part_used.sem, m["pused"] + 2 * b + 2)
                            dve.wait_ge(gelu_ready.sem, m["gelu"] + b + 1)
                            dve.tensor_tensor(z[slot][:, 0, :], z[slot][:, 0, :], z[slot][:, 1, :], ALU.mult).then_inc(hid_ready.sem, 1)
                            dve.wait_ge(hid_ready.sem, m["hid"] + 2 * b + 1)
                            dve.wait_ge(part_ready.sem, m["part"] + b + 1)
                            dve.tensor_tensor(h_lo[:, bass.ds(b, 1), :], z[slot][:, 0:1, :], h_hi[:, bass.ds(b, 1), :].bitcast(F32),
                                              ALU.subtract).then_inc(hid_ready.sem, 1)
                        dense(specs[f"fu{l}{g}"], after(f"fu{l}{g}"), two_chunks(a_tiles), up_dve, up_act)
                        part_used.n += 2 * n
                        hid_ready.n += 2 * n
                        part_ready.n += n
                        gelu_ready.n += n
                        dense(specs[f"fd{l}{g}"], after(f"fd{l}{g}"), two_chunks(h_tiles[:n]), copy_to(y) if g == 0 else add_to(y))
                norm(f"ffn{l}_n", 9 + l, "add", src=y)

        def fox():
            with ExitStack() as ctx:
                g = sb(ctx, "fx_g", [P, TT, FH * FD])
                with ExitStack() as inner:
                    kT = sb(inner, "fx_k", [P, 8, S])
                    v = sb(inner, "fx_v", [P, TT, FH * FD])
                    norm("kv", 11, "parts")
                    dense(specs["fk"], after("fk"), two_chunks(a_tiles), copy_to(kT))

                    def v_rows(dve, grp, t):
                        return dve.tensor_copy(v[:, t, bass.ds(grp * 512, 512)], bank[t][:, :])
                    dense_rows(specs["fv"], after("fv"), evac_dve=v_rows)
                    with ExitStack() as tmp:
                        bias = sb(tmp, "fx_bias", [FH, 1])
                        lf, t1, t2, one = (sb(tmp, f"fx_{n}", [FH, S]) for n in ("lf", "t1", "t2", "one"))

                        def f_rows(dve, b, slot, m):
                            dve.wait_ge(products_done.sem, m["prod"] + b + 1)
                            dve.tensor_copy(lf[:, :], bank[2 * slot][0:FH, :]).then_inc(evacuated.sem, 1)
                        dense(specs["ff"], after("ff"), [[[(k * P, a_tiles[k]) for k in range(KT)]]], f_rows)
                        b_in, b_a, b_d, b_st = inputs_in[0].n, act_step.n, dve_step.n, rows_stored.n
                        with nc.Block() as block:
                            @block.sync
                            def _(sp):
                                sp.dma_start(bias[:, :], io["kv_b_f_2"].rearrange("(h a) -> h a", a=1)).then_inc(inputs_in[0].sem, 16)
                                sp.wait_ge(dve_step.sem, b_d + 2)
                                sp.dma_start(io["row_scratch"][:, :], t1[:, :]).then_inc(rows_stored.sem, 16)
                                sp.wait_ge(rows_stored.sem, b_st + 16)

                            @block.vector
                            def _(dve):
                                dve.memset(one[:, :], -1.0)
                                dve.wait_ge(inputs_in[0].sem, b_in + 16)
                                dve.tensor_scalar(lf[:, :], lf[:, :], bias[:, 0:1], None, ALU.add)
                                dve.drain()
                                log_sigmoid(None, dve, lf[:, :], t1[:, :], t2[:, :], b_a, b_d, "dve")
                                dve.tensor_scalar(one[:, :], one[:, :], -1.0, None, ALU.mult)
                                dve.drain()
                                dve.tensor_tensor_scan(t2[:, :], one[:, :], lf[:, :], 0.0, ALU.mult, ALU.add)
                                dve.drain()
                                dve.tensor_scalar(t1[:, :], t2[:, :], -1.0, None, ALU.mult).then_inc(dve_step.sem, 1)

                            @block.scalar
                            def _(act):
                                log_sigmoid(act, None, lf[:, :], t1[:, :], t2[:, :], b_a, b_d, "act")
                        inputs_in[0].n += 16
                        act_step.n += 1
                        dve_step.n += 2
                        rows_stored.n += 16
                    norm("fx", 4, "parts")
                    qT = sb(inner, "fx_q", [P, 8, S])
                    dense(specs["fq"], after("fq"), two_chunks(a_tiles), copy_to(qT))

                    def g_rows(act, grp, t):
                        return act.activation(g[:, t, bass.ds(grp * 512, 512)], bank[t][:, :], ACT.Sigmoid)
                    dense_rows(specs["fg"], after("fg"), evac_act=g_rows)

                    def finish_unit(dve, c, e, i, out, inv):
                        dst = g[:, i, bass.ds(c * P + e * FD, FD)]
                        return dve.scalar_tensor_tensor(dst, out, inv, dst, ALU.mult, ALU.mult)
                    attention("fox", FH // 2, qT, kT, False, lambda c, e, j: v[:, j, bass.ds(c * P + e * FD, FD)],
                              finish_unit, bias_rows=io["row_scratch"])
                to_features(g, KT, a_hi, a_lo)
            post_norm_dense("fout", 6, a_tiles)

        def store():
            with ExitStack() as ctx:
                rows = sb(ctx, "out_rows", [P, TT, D])
                b_t, b_o = turned.n, turned_out.n
                with nc.Block() as block:
                    @block.tensor
                    def _(pe):
                        for t in range(TT):
                            for h in range(2):
                                n = 2 * t + h
                                if n >= 4:
                                    pe.wait_ge(turned_out.sem, b_o + n - 3)
                                for k in range(4):
                                    last = pe.transpose(bank[n % 4][:, k * P:(k + 1) * P], xT[:, 4 * h + k, t * P:(t + 1) * P], ident)
                                last.then_inc(turned.sem, 1)

                    @block.vector
                    def _(dve):
                        for n in range(2 * TT):
                            dve.wait_ge(turned.sem, b_t + n + 1)
                            dve.tensor_copy(rows[:, n // 2, (n % 2) * 512:(n % 2 + 1) * 512], bank[n % 4][:, :]).then_inc(turned_out.sem, 1)

                    @block.sync
                    def _(sp):
                        for t in range(TT):
                            sp.wait_ge(turned_out.sem, b_o + 2 * t + 2)
                            sp.dma_start(io["out"][0, t * P:(t + 1) * P, :], rows[:, t, :]).then_inc(stored.sem, 16)
                        sp.wait_ge(stored.sem, 16 * TT)

        setup()
        first_block()
        norm("m1", 3, "parts")
        mlstm()
        ffn(0)
        fox()
        ffn(1)
        store()


_INS = ["x", "positions", "norm_mix", "w_in", "cmp_pos_k", "cmp_pos_v", "cmp_k_w1", "cmp_k_w2", "cmp_v_w1", "cmp_v_w2",
        "w_proj_a", "w_proj_b", "w_out", "norm_mlp", "w_up", "w_down", "norm_final", "norm_mix_pre_2", "norm_mix_post_2",
        "norm_ffn_pre_2", "norm_ffn_post_2", "mlstm_w_in_2", "mlstm_b_gate_2", "mlstm_norm_2", "mlstm_w_out_2", "kv_norm_2",
        "kv_w_2", "kv_b_f_2", "fox_w_qg_2", "fox_w_out_2", "ffn_w_up_2", "ffn_conv_w_2", "ffn_conv_b_2", "ffn_w_down_2"]


def kernel(**inputs):
    import concourse.bacc as _bacc
    from concourse.bass_utils import run_bass_kernel_spmd as _run

    nc = _bacc.Bacc("TRN2", target_bir_lowering=False, num_devices=1)
    packed, at, decay = shape_constants()
    arrays, io = {}, {}

    def give(name, a):
        arrays[f"in_{name}"] = a
        io[name] = nc.dram_tensor(f"in_{name}", a.shape, mybir.dt.from_np(a.dtype), kind="ExternalInput").ap()

    for name in _INS:
        give(name, np.ascontiguousarray(inputs[name]))
    give("const", packed)
    give("decay", decay)
    io["row_scratch"] = nc.dram_tensor("row_scratch", (FH, S), F32, kind="Internal").ap()
    io["out"] = nc.dram_tensor("out_x", (1, S, D), F32, kind="ExternalOutput").ap()
    build(nc, io, at)
    r = _run(nc, [arrays], core_ids=[0])
    return r.results[0]["out_x"]
```

```python
from contextlib import ExitStack

import numpy as np

import concourse.bass as bass
from concourse import mybir

F32, F32R = mybir.dt.float32, mybir.dt.float32r
BF16, I32 = mybir.dt.bfloat16, mybir.dt.int32
ACT = mybir.ActivationFunctionType
ALU = mybir.AluOpType
AX_X = mybir.AxisListType.X

P = 128
S = 512
D = 1024
KT = D // P
TT = S // P
SLOT = KT * 256
EPS = 1e-6
NEG = -1e30

HD, HQ, KV = 64, 8, 2
RH, RD = 4, 128
CB, CS, CH = 32, 16, 256
NC = (S - CB) // CS + 1
MLP_H = 4 * D
COLS = np.cumsum([0, HQ * HD] + [KV * HD] * 6 + [3 * HQ] + [RH * RD] * 4 + [D, D]).tolist()
(C_Q, C_KC, C_VC, C_KS, C_VS, C_KW, C_VW, C_G, C_RQ, C_RK, C_RV, C_RG, C_GA, C_GB) = COLS[:14]
GATES = 3 * HQ
MH, MK, MV = 8, 64, 128
FH, FD = 16, 64
FF = 2816
FT = FF // P

PI = float(np.pi)
TWO_PI_HI = 6.28125
TWO_PI_LO = 2 * np.pi - TWO_PI_HI
ROUND = 12582912.0
SIN_MAX = 3.1415925

VECS = ["norm_mix", "norm_mlp", "norm_final", "norm_mix_pre_2", "norm_mix_post_2",
        "norm_ffn_pre_2", "norm_ffn_post_2", "kv_norm_2", "mlstm_norm_2"]

GAINS = 13 * KT


class Tally:

    def __init__(self, sem):
        self.sem = sem
        self.n = 0


def shape_constants():
    p = np.arange(P)
    c = {}
    c["ident"] = np.eye(P)
    c["causal_bias"] = np.where(p[None, :] <= p[:, None], 0.0, NEG)
    c["causal_keep"] = np.where(p[:, None] <= p[None, :], 1.0, 0.0)
    half, rot = 8, 16
    d = p % HD
    partner = np.where(d < half, p + half, np.where(d < rot, p - half, p))
    c["swap_nsa"] = (p[:, None] == partner[None, :])
    c["swap_ret"] = (p[:, None] == ((p + RD // 2) % RD)[None, :])
    inv = np.exp(np.float32(-np.log(500000.0)) * np.arange(half, dtype=np.float32) * np.float32(2.0) / np.float32(rot))
    invr = np.exp(np.float32(-np.log(10000.0)) * np.arange(RD // 2, dtype=np.float32) * np.float32(2.0) / np.float32(RD))
    angles = np.zeros((P, 4))
    angles[:, 0] = np.where(d < rot, inv[d % half], 0.0)
    angles[:, 1] = np.where(d < half, -1.0, 1.0)
    angles[:, 2] = invr[p % (RD // 2)]
    angles[:, 3] = np.where(p < RD // 2, -1.0, 1.0)
    c["angles"] = angles
    t = p[:, None] + P * np.arange(TT)[None, :]
    end = CS * np.arange(CB) + CB - 1
    ok = (end[None, None, :] <= t[:, :, None]) & (np.arange(CB) < NC)[None, None, :]
    c["cmp_bias"] = np.where(ok, 0.0, NEG).reshape(P, TT * CB)
    c["cmp_any"] = ok.any(-1)
    packed = np.concatenate([np.asarray(v, np.float32) for v in c.values()], 1)
    at, off = {}, 0
    for k, v in c.items():
        at[k] = (off, off + v.shape[1])
        off += v.shape[1]
    log_g = np.log(1.0 - np.exp2(-5.0 - np.arange(RH)))
    rel = np.arange(S)[None, :] - p[:, None]
    decay = np.where(rel[:, None, :] >= 0, np.exp(log_g[None, :, None] * np.maximum(rel, 0)[:, None, :]), 0.0)
    return packed, at, np.ascontiguousarray(decay.astype(np.float32))


class Weights:

    def __init__(self, blocks, forms):
        self.blocks = blocks
        self.forms = forms

    def form(self, b):
        return self.forms[b % len(self.forms)]


def build(nc, io, at):
    top = ExitStack()
    with top:
        def sb(ctx, name, shape, dt=F32):
            return ctx.enter_context(nc.sbuf_tensor(name, shape, dt))

        def tally(name):
            return Tally(top.enter_context(nc.semaphore(name)))

        raw = [sb(top, f"w_raw{r}", [P, SLOT]) for r in range(2)]
        w_hi = [sb(top, f"w_hi{r}", [P, SLOT], F32R) for r in range(2)]
        w_lo = [sb(top, f"w_lo{r}", [P, SLOT], F32R) for r in range(2)]
        xT = sb(top, "xT", [P, KT, S])
        a_hi = sb(top, "a_hi", [P, KT, S], F32R)
        a_lo = sb(top, "a_lo", [P, KT, S], F32R)
        width = io["const"].shape[1]
        const = sb(top, "const_sb", [P, width])
        ident_b = sb(top, "ident_b", [P, P], BF16)
        bias_b = sb(top, "bias_b", [P, P], BF16)
        mean_of = sb(top, "mean_of", [P, 1])
        inv_col = sb(top, "inv_col", [P, TT])
        sq = [sb(top, f"sq{r}", [P, S]) for r in range(2)]
        total = sb(top, "total", [P, S])
        inv = sb(top, "inv", [P, S])
        y_part = [sb(top, f"y_part{r}", [P, S]) for r in range(2)]
        gains = sb(top, "gains", [P, GAINS])
        conv = sb(top, "conv", [P, 4, 88])
        bank = [top.enter_context(nc.psum_tensor(f"bank{i}", [P, 512], F32)) for i in range(8)]

        def cst(name):
            return const[:, at[name][0]:at[name][1]]

        ident = cst("ident")

        raw_loaded = [tally(f"raw_loaded{r}") for r in range(2)]
        hi_ready, lo_ready = tally("hi_ready"), tally("lo_ready")
        products_done, evacuated = tally("products_done"), tally("evacuated")
        rows_done, rows_out = tally("rows_done"), tally("rows_out")
        part_ready, part_used = tally("part_ready"), tally("part_used")
        gelu_ready = tally("gelu_ready")
        hid_ready = tally("hid_ready")
        inputs_in = [tally(f"inputs_in{i}") for i in range(4)]
        squared, summed, mean_ready, mixed = (tally(n) for n in ("squared", "summed", "mean_ready", "mixed"))
        positions_in, high_staged, probs_high = (tally(n) for n in ("positions_in", "high_staged", "probs_high"))
        scaled, split_hi_done, split_lo_done = tally("scaled"), tally("split_hi_done"), tally("split_lo_done")
        turned, turned_out, turned_hi = tally("turned"), tally("turned_out"), tally("turned_hi")
        keys_staged = tally("keys_staged")
        staged, scores_ready, max_ready, probs_ready = (tally(n) for n in ("staged", "scores_ready", "max_ready", "probs_ready"))
        probs_turned, probs_copied, out_ready, out_done = (tally(n) for n in ("probs_turned", "probs_copied", "out_ready", "out_done"))
        bias_row_in = [tally(f"bias_row_in{r}") for r in range(2)]
        bias_row_used = tally("bias_row_used")
        logits_ready = tally("logits_ready")
        gap_ready, decay_ready, kept, weighted = (tally(n) for n in ("gap_ready", "decay_ready", "kept", "weighted"))
        act_step, dve_step, pe_step, pool_step = (tally(n) for n in ("act_step", "dve_step", "pe_step", "pool_step"))
        rows_stored = tally("rows_stored")
        stored = tally("stored")
        LEAD = 32
        led = [products_done, evacuated, rows_done, rows_out, part_ready, part_used, hi_ready, lo_ready, scores_ready,
               max_ready, probs_ready, probs_turned, probs_copied, out_ready, out_done, staged, keys_staged, bias_row_used,
               logits_ready, gap_ready, decay_ready, kept, weighted, gelu_ready, hid_ready,
               squared, summed, mixed, high_staged, probs_high]

        stream = {"slot": 0}

        def slot_view(ring, r, form):
            tiles, width, _ = form
            return ring[r][:, 0:tiles * width].rearrange("p (t n) -> p t n", t=tiles)

        def load(eng, spec, b, slot, q):
            dst = slot_view(raw, slot, spec.forms[q])
            for col, ncol, src in spec.forms[q][2]:
                eng.dma_start(dst[:, :, col:col + ncol], src(b)).then_inc(raw_loaded[slot].sem, 16)

        def prefetch(eng, spec):
            for b in range(min(2, spec.blocks)):
                slot = (stream["slot"] + b) % 2
                load(eng, spec, b, slot, b % len(spec.forms))

        def loads(eng, spec, nxt, m):
            def one(b, q):
                eng.wait_ge(lo_ready.sem, m["lo"] + b - 1)
                load(eng, spec, b, (m["slot"] + q) % 2, q % len(spec.forms))
            if spec.blocks > 4:
                with eng.Fori(1, spec.blocks // 2) as i:
                    one(i * 2, 0)
                    one(i * 2 + 1, 1)
            else:
                for b in range(2, spec.blocks):
                    one(b, b % 2)
            if nxt is not None:
                for b in range(min(2, nxt.blocks)):
                    e = spec.blocks + b
                    eng.wait_ge(lo_ready.sem, m["lo"] + e - 1)
                    load(eng, nxt, b, (m["slot"] + e) % 2, b % len(nxt.forms))

        def hi_part(act, spec, nxt, b, q, m):
            beyond = isinstance(b, int) and b == spec.blocks
            if beyond and nxt is None:
                return
            slot, form = (m["slot"] + q) % 2, (nxt.forms[0] if beyond else spec.forms[q % len(spec.forms)])
            n = form[0] * form[1]
            before = m["raw"][slot]
            if beyond:
                before += sum(16 * len(spec.form(x)[2]) for x in range(q, spec.blocks, 2))
                turn = 1
            else:
                turn = b // 2 + 1 if isinstance(b, int) else m["i"] + 2
            act.wait_ge(raw_loaded[slot].sem, before + 16 * len(form[2]) * turn)
            act.wait_ge(products_done.sem, m["prod"] + b - 1)
            act.activation(w_hi[slot][:, 0:n], raw[slot][:, 0:n], ACT.Copy).then_inc(hi_ready.sem, 1)

        def lo_part(dve, spec, nxt, b, q, m):
            beyond = isinstance(b, int) and b == spec.blocks
            if beyond and nxt is None:
                return
            slot, form = (m["slot"] + q) % 2, (nxt.forms[0] if beyond else spec.forms[q % len(spec.forms)])
            n = form[0] * form[1]
            dve.wait_ge(hi_ready.sem, m["hi"] + b + 1)
            dve.tensor_tensor(w_lo[slot][:, 0:n], raw[slot][:, 0:n], w_hi[slot][:, 0:n].bitcast(F32),
                              ALU.subtract).then_inc(lo_ready.sem, 1)

        def marks():
            return {"slot": stream["slot"], "raw": [t.n for t in raw_loaded], "hi": hi_ready.n, "lo": lo_ready.n,
                    "prod": products_done.n, "evac": evacuated.n, "rows": rows_done.n, "rowsout": rows_out.n,
                    "part": part_ready.n, "pused": part_used.n, "gelu": gelu_ready.n, "hid": hid_ready.n,
                    "sq": squared.n, "sum": summed.n, "mixed": mixed.n, "i": 0}

        def finish(spec):
            for b in range(spec.blocks):
                slot = (stream["slot"] + b) % 2
                raw_loaded[slot].n += 16 * len(spec.form(b)[2])
            stream["slot"] = (stream["slot"] + spec.blocks) % 2
            for t in (hi_ready, lo_ready, products_done):
                t.n += spec.blocks

        def none(eng, b, slot, m):
            pass

        def split_between(eng, spec, nxt, m, part, early, late):
            part(eng, spec, nxt, 1, 1, m)
            n, first = spec.blocks, 0
            slot = lambda q: (m["slot"] + q) % 2
            if n > 4:
                with eng.Fori(0, n // 2 - 1) as i:
                    m["i"] = i
                    for q in range(2):
                        early(eng, i * 2 + q, slot(q), m)
                        part(eng, spec, nxt, i * 2 + (q + 2), q, m)
                        late(eng, i * 2 + q, slot(q), m)
                first = n - 2
            for b in range(first, n):
                early(eng, b, slot(b % 2), m)
                if n > 1 and b + 2 <= n:
                    part(eng, spec, nxt, b + 2, b % 2, m)
                late(eng, b, slot(b % 2), m)

        def three_products(pe, out, w, x, first, last):
            pe.matmul(out, w[0], x[0], start=first, stop=False)
            pe.matmul(out, w[0], x[1], start=False, stop=False)
            return pe.matmul(out, w[1], x[0], start=False, stop=last)

        def run(*stages):
            uses = {e for s in stages for e in s}
            with nc.Block(no_gpsimd_drain="gpsimd" not in uses) as block:
                if "sync" in uses:
                    @block.sync
                    def _(sp):
                        for s in stages:
                            if "sync" in s:
                                s["sync"](sp)

                if "scalar" in uses:
                    @block.scalar
                    def _(act):
                        for s in stages:
                            if "scalar" in s:
                                s["scalar"](act)

                if "vector" in uses:
                    @block.vector
                    def _(dve):
                        for s in stages:
                            if "vector" in s:
                                s["vector"](dve)

                if "gpsimd" in uses:
                    @block.gpsimd
                    def _(pool):
                        for s in stages:
                            if "gpsimd" in s:
                                s["gpsimd"](pool)

                if "tensor" in uses:
                    @block.tensor
                    def _(pe):
                        for s in stages:
                            if "tensor" in s:
                                s["tensor"](pe)

        def dense(name, chunks, early_dve=none, late_dve=none, early_act=none, late_act=none, tile_ready=None):
            spec, nxt, m = specs[name], after(name), marks()

            def sync(sp):
                loads(sp, spec, nxt, m)

            def scalar(act):
                split_between(act, spec, nxt, m, hi_part, early_act, late_act)

            def vector(dve):
                split_between(dve, spec, nxt, m, lo_part, early_dve, late_dve)

            def tensor(pe):
                def use(b, q):
                    slot = (m["slot"] + q) % 2
                    pe.wait_ge(lo_ready.sem, m["lo"] + b + 1)
                    pe.wait_ge(evacuated.sem, m["evac"] + b - 1)
                    sets = chunks[q % len(chunks)]
                    terms = [(c, k) for c in range(len(sets)) for k in range(len(sets[c]))]
                    if tile_ready is not None and q == 0:
                        terms = [(c, k) for k in range(len(sets[0])) for c in range(len(sets))]
                    for c, k in terms:
                        if tile_ready is not None and q == 0 and c == 0:
                            pe.wait_ge(*tile_ready(k))
                        col, x = sets[c][k]
                        w = [ring[slot][:, col:col + P] for ring in (w_hi, w_lo)]
                        last = three_products(pe, bank[2 * slot + c][:, :], w, x, k == 0, k == len(sets[c]) - 1)
                    last.then_inc(products_done.sem, 1)
                if spec.blocks <= 2:
                    for b in range(spec.blocks):
                        use(b, b)
                else:
                    with pe.Fori(0, spec.blocks // 2) as i:
                        use(i * 2, 0)
                        use(i * 2 + 1, 1)
            finish(spec)
            evacuated.n += spec.blocks
            return {"sync": sync, "scalar": scalar, "vector": vector, "tensor": tensor}

        def dense_rows(name, evac_dve=None, evac_act=None):
            spec, nxt, m = specs[name], after(name), marks()
            tiles, width, _ = spec.forms[0]
            b_dve = dve_step.n

            def rows(fn):
                def early(eng, b, slot, m):
                    if fn is None or slot == m["slot"]:
                        return
                    g = (b - 1) // 2 if isinstance(b, int) else m["i"]
                    for t in range(TT):
                        eng.wait_ge(rows_done.sem, m["rows"] + g * TT + (t + 1))
                        fn(eng, g, t).then_inc(rows_out.sem, 1)
                return early

            def sync(sp):
                loads(sp, spec, nxt, m)

            def scalar(act):
                split_between(act, spec, nxt, m, hi_part, rows(evac_act), none)

            def vector(dve):
                split_between(dve, spec, nxt, m, lo_part, rows(evac_dve), none)

            def tensor(pe):
                if b_dve:
                    pe.wait_ge(dve_step.sem, b_dve)
                m["i"] = 0

                def use(b, q):
                    slot = (m["slot"] + q) % 2
                    pe.wait_ge(lo_ready.sem, m["lo"] + b + 1)
                    g = b // 2 if isinstance(b, int) else m["i"]
                    for t in range(TT):
                        if q == 0:
                            pe.wait_ge(rows_out.sem, m["rowsout"] + g * TT + (t + 1 - TT))
                        for k in range(tiles):
                            x = [a[:, q * tiles + k, t * P:(t + 1) * P] for a in (a_hi, a_lo)]
                            w = [ring[slot][:, k * width:(k + 1) * width] for ring in (w_hi, w_lo)]
                            last = three_products(pe, bank[4 + t][:, 0:width], x, w, q == 0 and k == 0,
                                                  q == 1 and k == tiles - 1)
                        if q == 1:
                            last.then_inc(rows_done.sem, 1)
                    if q == 0:
                        last.then_inc(products_done.sem, 1)
                    else:
                        pe.drain().then_inc(products_done.sem, 1)
                if spec.blocks == 2:
                    use(0, 0)
                    use(1, 1)
                else:
                    with pe.Fori(0, spec.blocks // 2) as i:
                        m["i"] = i
                        use(i * 2, 0)
                        use(i * 2 + 1, 1)
            finish(spec)
            rows_done.n += TT * spec.blocks // 2
            rows_out.n += TT * spec.blocks // 2
            return {"sync": sync, "scalar": scalar, "vector": vector, "tensor": tensor}

        def view(w):
            return w.rearrange("(t p) n -> p t n", p=P)

        def cols(w, start, n=256, step=256, t0=0, t1=None):
            v = view(w)[:, t0:t1, :]
            return lambda b: v[:, :, bass.ds(b * step + start, n)]

        def plain(w, start, blocks, t0=0, tiles=KT):
            return Weights(blocks, [(tiles, 256, [(0, 256, cols(w, start, t0=t0, t1=t0 + tiles))])])

        def row_blocks(w, start, groups):
            forms = []
            for q in range(2):
                v = view(w)[:, q * KT // 2:(q + 1) * KT // 2, :]
                forms.append((KT // 2, 512, [(0, 512, (lambda v, q: lambda b: v[:, :, bass.ds((b - q) * 256 + start, 512)])(v, q))]))
            return Weights(2 * groups, forms)

        a_tiles = [(a_hi[:, k, :], a_lo[:, k, :]) for k in range(KT)]

        def two_chunks(xs):
            return [[[(k * 256 + c * P, x) for k, x in enumerate(xs)] for c in range(2)]]

        W_IN, W_IN2, KV_W = io["w_in"][0], io["mlstm_w_in_2"][0], io["kv_w_2"]
        v_in = view(W_IN)
        q_pieces = [(128 * j + 64 * g, 64, (lambda j, g: lambda b: v_in[:, :, bass.ds(b * 128 + (C_Q + 256 * g + 64 * j), 64)])(j, g))
                    for j in range(2) for g in range(2)]
        half = [v_in[:, q * 4:(q + 1) * 4, :] for q in range(2)]
        specs = {}
        specs["q"] = Weights(2, [(KT, 256, q_pieces)])
        specs["kcvc"] = Weights(2, [(KT, 256, [(0, 256, lambda b: v_in[:, :, C_KC:C_KC + 256])]),
                                    (KT, 256, [(0, 128, lambda b: v_in[:, :, C_KS:C_KS + 128]),
                                               (128, 128, lambda b: v_in[:, :, C_KW:C_KW + 128])])])
        specs["vg"] = Weights(2, [(4, 280, [(0, 128, (lambda q: lambda b: half[q][:, :, C_VS:C_VS + 128])(q)),
                                            (128, 152, (lambda q: lambda b: half[q][:, :, C_VW:C_VW + 152])(q))])
                                  for q in range(2)])
        specs["rqk"] = plain(W_IN, C_RQ, 4)
        specs["rvg"] = row_blocks(W_IN, C_RV, 2)
        specs["mix"] = Weights(16, [
            (KT, 256, [(0, 128, lambda b: v_in[:, :, bass.ds(b * 64 + C_GA, 128)]),
                       (128, 128, lambda b: v_in[:, :, bass.ds(b * 64 + C_GB, 128)])]),
            (4, 256, [(0, 128, lambda b: view(io["w_proj_a"][0])[:, :, bass.ds(b * 64 - 64, 128)]),
                      (128, 128, lambda b: view(io["w_proj_b"][0])[:, :, bass.ds(b * 64 - 64, 128)])])])
        specs["out1"] = plain(io["w_out"][0], 0, 4)
        order = ["q", "kcvc", "vg", "rqk", "rvg", "mix", "out1"]
        for g in range(4):
            specs[f"up{g}"] = plain(io["w_up"][0], g * D, 4)
            specs[f"down{g}"] = plain(io["w_down"][0], 0, 4, t0=g * KT)
            order += [f"up{g}", f"down{g}"]
        specs["mqk"] = plain(W_IN2, 0, 4)
        specs["mv"] = row_blocks(W_IN2, 1024, 2)
        specs["mo"] = row_blocks(W_IN2, 2048, 2)
        v_in2, v_kv = view(W_IN2), view(KV_W)
        specs["mg"] = Weights(1, [(KT, 128, [(0, 8, lambda b: v_in2[:, :, 3072:3080]), (8, 24, lambda b: v_in2[:, :, 0:24]),
                                             (32, 8, lambda b: v_in2[:, :, 3080:3088]), (40, 88, lambda b: v_in2[:, :, 24:112])])])
        specs["mout"] = plain(io["mlstm_w_out_2"][0], 0, 4)
        order += ["mg", "mqk", "mv", "mo", "mout"]
        FG = [(0, 8), (8, 8), (16, 6)]

        def ffn_specs(l):
            wu, wd = view(io["ffn_w_up_2"][l]), io["ffn_w_down_2"][l]
            for g, (f0, n) in enumerate(FG):
                specs[f"fu{l}{g}"] = Weights(n, [(KT, 256, [
                    (0, 128, (lambda f0: lambda b: wu[:, :, bass.ds(b * P + f0 * P, P)])(f0)),
                    (128, 128, (lambda f0: lambda b: wu[:, :, bass.ds(b * P + (FF + f0 * P), P)])(f0))])])
                specs[f"fd{l}{g}"] = plain(wd, 0, 4, t0=f0, tiles=n)
                order.extend([f"fu{l}{g}", f"fd{l}{g}"])

        ffn_specs(0)
        specs["fk"] = plain(KV_W, 0, 4)
        specs["fv"] = row_blocks(KV_W, D, 2)
        specs["ff"] = Weights(1, [(KT, 128, [(0, 16, lambda b: v_kv[:, :, 2048:2064]), (16, 112, lambda b: v_kv[:, :, 0:112])])])
        specs["fq"] = plain(io["fox_w_qg_2"][0], 0, 4)
        specs["fg"] = row_blocks(io["fox_w_qg_2"][0], D, 2)
        specs["fout"] = plain(io["fox_w_out_2"][0], 0, 4)
        order += ["ff", "fk", "fv", "fq", "fg", "fout"]
        ffn_specs(1)

        def after(name):
            i = order.index(name)
            return specs[order[i + 1]] if i + 1 < len(order) else None

        def setup():
            with ExitStack() as ctx:
                x_rows = sb(ctx, "x_rows", [P, TT, D])
                gain_rows = sb(ctx, "gain_rows", [GAINS, P])
                conv_rows = sb(ctx, "conv_rows", [88, 4, P])
                with nc.Block() as block:
                    @block.sync
                    def _(sp):
                        sp.dma_start(x_rows[:, :, :], io["x"][0].rearrange("(t p) d -> p t d", p=P)).then_inc(inputs_in[0].sem, 16)
                        prefetch(sp, specs["q"])

                    @block.scalar
                    def _(act):
                        act.dma_start(const[:, :], io["const"]).then_inc(inputs_in[1].sem, 16)
                        row = 0
                        for name in VECS:
                            v = io[name]
                            n = v.shape[0] if len(v.shape) == 2 else 1
                            src = v.rearrange("l (t p) -> (l t) p", p=P) if len(v.shape) == 2 else v.rearrange("(t p) -> t p", p=P)
                            act.dma_start(gain_rows[row:row + n * KT, :], src).then_inc(inputs_in[2].sem, 16)
                            row += n * KT
                        for l in range(2):
                            w = io["ffn_conv_w_2"][l].rearrange("k (t p) -> (k t) p", p=P)
                            act.dma_start(conv_rows[:, 2 * l, :], w[0:88, :]).then_inc(inputs_in[3].sem, 16)
                            act.dma_start(conv_rows[0:44, 2 * l + 1, :], w[88:132, :]).then_inc(inputs_in[3].sem, 16)
                            act.dma_start(conv_rows[44:88, 2 * l + 1, :],
                                          io["ffn_conv_b_2"][l].rearrange("(t p) -> t p", p=P)).then_inc(inputs_in[3].sem, 16)
                        act.wait_ge(raw_loaded[0].sem, 16 * len(specs["q"].forms[0][2]))
                        act.activation(w_hi[0][:, :], raw[0][:, :], ACT.Copy).then_inc(hi_ready.sem, 1)

                    @block.gpsimd
                    def _(pool):
                        for t in led:
                            pool.sem_inc(t.sem, LEAD)
                        pool.memset(mean_of[:, :], 1.0 / D).then_inc(pool_step.sem, 1)

                    @block.tensor
                    def _(pe):
                        pe.wait_ge(inputs_in[0].sem, 16)
                        pe.wait_ge(inputs_in[1].sem, 16)
                        for k in range(KT):
                            if k >= 4:
                                pe.wait_ge(turned_out.sem, k - 3)
                            for t in range(TT):
                                last = pe.transpose(bank[k % 4][:, t * P:(t + 1) * P], x_rows[:, t, k * P:(k + 1) * P], ident)
                            last.then_inc(turned.sem, 1)
                        pe.wait_ge(inputs_in[2].sem, 16 * len(VECS))
                        pe.transpose(bank[4][:, 0:GAINS], gain_rows[:, :], ident[0:GAINS, 0:GAINS]).then_inc(turned.sem, 1)
                        pe.wait_ge(inputs_in[3].sem, 16 * 6)
                        for j in range(4):
                            last = pe.transpose(bank[5][:, j * 88:(j + 1) * 88], conv_rows[:, j, :], ident[0:88, 0:88])
                        last.then_inc(turned.sem, 1)

                    @block.vector
                    def _(dve):
                        dve.wait_ge(inputs_in[1].sem, 16)
                        dve.tensor_copy(ident_b[:, :], ident)
                        dve.tensor_copy(bias_b[:, :], cst("causal_bias"))
                        for k in range(KT):
                            dve.wait_ge(turned.sem, k + 1)
                            dve.tensor_copy(xT[:, k, :], bank[k % 4][:, :]).then_inc(turned_out.sem, 1)
                        dve.wait_ge(turned.sem, KT + 1)
                        dve.tensor_copy(gains[:, :], bank[4][:, 0:GAINS])
                        dve.wait_ge(turned.sem, KT + 2)
                        dve.tensor_copy(conv[:, :, :], bank[5][:, 0:352].rearrange("p (a b) -> p a b", a=4))
                        dve.wait_ge(hi_ready.sem, LEAD + 1)
                        dve.tensor_tensor(w_lo[0][:, :], raw[0][:, :], w_hi[0][:, :].bitcast(F32), ALU.subtract).then_inc(lo_ready.sem, 1)
            turned.n += KT + 2
            turned_out.n += KT
            pool_step.n += 1
            for t, n in zip(inputs_in, (1, 1, len(VECS), 6)):
                t.n += 16 * n
            for t in led:
                t.n = LEAD

        def sums(src):
            b_sq, b_sum = squared.n, summed.n

            def scalar(act):
                for k in range(KT):
                    if k >= 2:
                        act.wait_ge(summed.sem, b_sum + k - 1)
                    act.activation(sq[k % 2][:, :], src[:, k, :], ACT.Square).then_inc(squared.sem, 1)

            def vector(dve):
                for k in range(KT):
                    add_square(dve, k, b_sq, b_sum)
            squared.n += KT
            summed.n += KT
            return {"scalar": scalar, "vector": vector}

        def add_square(dve, k, b_sq, b_sum):
            dve.wait_ge(squared.sem, b_sq + k + 1)
            if k == 0:
                dve.tensor_copy(total[:, :], sq[0][:, :]).then_inc(summed.sem, 1)
            else:
                dve.wait_ge(summed.sem, b_sum + k)
                dve.tensor_tensor(total[:, :], total[:, :], sq[k % 2][:, :], ALU.add).then_inc(summed.sem, 1)

        def sums_on_the_way(src):
            def late_act(act, b, slot, m):
                act.wait_ge(evacuated.sem, m["evac"] + b + 1)
                for c in range(2):
                    k = 2 * b + c
                    if k >= 2:
                        act.wait_ge(summed.sem, m["sum"] + k - 1)
                    act.activation(sq[c][:, :], src[:, k, :], ACT.Square).then_inc(squared.sem, 1)

            def late_dve(dve, b, slot, m):
                for c in range(2):
                    add_square(dve, 2 * b + c, m["sq"], m["sum"])
            return late_act, late_dve

        def inverse_root():
            b_sum, b_mean = summed.n, mean_ready.n

            def tensor(pe):
                pe.wait_ge(summed.sem, b_sum)
                for t in range(TT):
                    last = pe.matmul(bank[7][:, t:t + 1], total[:, t * P:(t + 1) * P], mean_of[:, :], start=True, stop=True)
                last.then_inc(mean_ready.sem, 1)
                pe.wait_ge(mean_ready.sem, b_mean + 3)
                for t in range(TT):
                    last = pe.matmul(bank[6][:, t * P:(t + 1) * P], inv_col[:, t:t + 1].broadcast_to([P, P]), ident, start=True, stop=True)
                last.then_inc(mean_ready.sem, 1)

            def scalar(act):
                act.wait_ge(mean_ready.sem, b_mean + 1)
                act.activation(inv_col[:, :], bank[7][:, 0:TT], ACT.Sqrt, bias=EPS).then_inc(mean_ready.sem, 1)

            def vector(dve):
                dve.wait_ge(mean_ready.sem, b_mean + 2)
                dve.reciprocal(inv_col[:, :], inv_col[:, :]).then_inc(mean_ready.sem, 1)
                dve.wait_ge(mean_ready.sem, b_mean + 4)
                dve.tensor_copy(inv[:, :], bank[6][:, :])
                dve.drain()
            mean_ready.n += 4
            return {"tensor": tensor, "scalar": scalar, "vector": vector}

        def gain(vec, k):
            return gains[:, vec * KT + k:vec * KT + k + 1]

        def normalise(vec):
            b_sc, b_hi, b_lo, b_pr = scaled.n, split_hi_done.n, split_lo_done.n, products_done.n

            def scalar(act):
                act.wait_ge(products_done.sem, b_pr)
                for k in range(KT):
                    act.wait_ge(scaled.sem, b_sc + k + 1)
                    act.activation(a_hi[:, k, :], y_part[k % 2][:, :], ACT.Copy).then_inc(split_hi_done.sem, 1)

            def vector(dve):
                def lo(k):
                    dve.wait_ge(split_hi_done.sem, b_hi + k + 1)
                    dve.tensor_tensor(a_lo[:, k, :], y_part[k % 2][:, :], a_hi[:, k, :].bitcast(F32),
                                      ALU.subtract).then_inc(split_lo_done.sem, 1)
                for k in range(KT):
                    if k >= 2:
                        dve.wait_ge(split_lo_done.sem, b_lo + k - 1)
                    dve.scalar_tensor_tensor(y_part[k % 2][:, :], xT[:, k, :], gain(vec, k), inv[:, :],
                                             ALU.mult, ALU.mult).then_inc(scaled.sem, 1)
                    if k >= 1:
                        lo(k - 1)
                lo(KT - 1)
            scaled.n += KT
            split_hi_done.n += KT
            split_lo_done.n += KT
            return {"scalar": scalar, "vector": vector}, lambda k: (split_lo_done.sem, b_lo + k + 1)

        def update(vec, src=None, with_sums=True):
            b_sc, b_sq, b_sum = scaled.n, squared.n, summed.n

            def scalar(act):
                if with_sums:
                    for k in range(KT):
                        act.wait_ge(scaled.sem, b_sc + k + 1)
                        if k >= 2:
                            act.wait_ge(summed.sem, b_sum + k - 1)
                        act.activation(sq[k % 2][:, :], xT[:, k, :], ACT.Square).then_inc(squared.sem, 1)

            def vector(dve):
                def scale(k):
                    dst = xT[:, k, :] if src is None else y_part[k % 2][:, :]
                    return dve.scalar_tensor_tensor(dst, (xT if src is None else src)[:, k, :], gain(vec, k), inv[:, :],
                                                    ALU.mult, ALU.mult)
                for k in range(KT):
                    if src is None:
                        scale(k).then_inc(scaled.sem, 1)
                    else:
                        scale(k)
                        dve.drain()
                        dve.tensor_tensor(xT[:, k, :], xT[:, k, :], y_part[k % 2][:, :], ALU.add).then_inc(scaled.sem, 1)
                    if with_sums and k >= 1:
                        add_square(dve, k - 1, b_sq, b_sum)
                if with_sums:
                    add_square(dve, KT - 1, b_sq, b_sum)
                dve.drain()
            scaled.n += KT
            if with_sums:
                squared.n += KT
                summed.n += KT
            return {"scalar": scalar, "vector": vector}

        def copy_to(dst, scale=None):
            def early(dve, b, slot, m):
                dve.wait_ge(products_done.sem, m["prod"] + b + 1)
                for c in range(2):
                    out, src = dst[:, bass.ds(b * 2 + c, 1), :], bank[2 * slot + c][:, None, :]
                    ins = dve.tensor_copy(out, src) if scale is None else dve.tensor_scalar(out, src, scale, None, ALU.mult)
                ins.then_inc(evacuated.sem, 1)
            return early

        def add_to(dst):
            def early(dve, b, slot, m):
                dve.wait_ge(products_done.sem, m["prod"] + b + 1)
                for c in range(2):
                    y = dst[:, bass.ds(b * 2 + c, 1), :]
                    ins = dve.tensor_tensor(y, bank[2 * slot + c][:, None, :], y, ALU.add)
                ins.then_inc(evacuated.sem, 1)
            return early

        def to_features(src, tiles, hi, lo, first=0, weight=None):
            b_t, b_h, b_o = turned.n, turned_hi.n, turned_out.n
            with nc.Block() as block:
                @block.tensor
                def _(pe):
                    for k in range(tiles):
                        if k >= 4:
                            pe.wait_ge(turned_out.sem, b_o + k - 3)
                        for t in range(TT):
                            last = pe.transpose(bank[k % 4][:, t * P:(t + 1) * P], src(t, k), ident)
                        last.then_inc(turned.sem, 1)

                @block.scalar
                def _(act):
                    for k in range(tiles):
                        act.wait_ge(turned.sem, b_t + k + 1)
                        act.activation(hi[:, first + k, :], bank[k % 4][:, :], ACT.Copy,
                                       scale=1.0 if weight is None else gain(weight, k)).then_inc(turned_hi.sem, 1)

                @block.vector
                def _(dve):
                    for k in range(tiles):
                        dve.wait_ge(turned_hi.sem, b_h + k + 1)
                        high = hi[:, first + k, :].bitcast(F32)
                        if weight is None:
                            ins = dve.tensor_tensor(lo[:, first + k, :], bank[k % 4][:, :], high, ALU.subtract)
                        else:
                            ins = dve.scalar_tensor_tensor(lo[:, first + k, :], bank[k % 4][:, :], gain(weight, k), high,
                                                           ALU.mult, ALU.subtract)
                        ins.then_inc(turned_out.sem, 1)
            turned.n += tiles
            turned_hi.n += tiles
            turned_out.n += tiles

        def positions_load(pos_i):
            def sync(sp):
                sp.dma_start(pos_i[:, :], io["positions"][0:1, :].broadcast_to([P, S])).then_inc(positions_in.sem, 16)
            return {"sync": sync}

        def rope_tables(work, pos_i, freq, cos, sin):
            ang, turns, rest = work
            a0 = at["angles"][0]
            b_a, b_d = act_step.n, dve_step.n

            def vector(dve):
                dve.wait_ge(positions_in.sem, 16)
                if b_a:
                    dve.wait_ge(act_step.sem, b_a)
                dve.tensor_copy(ang[:, :], pos_i[:, :])
                dve.drain()
                dve.tensor_scalar(ang[:, :], ang[:, :], const[:, a0 + freq:a0 + freq + 1], None, ALU.mult)
                dve.drain()
                dve.tensor_scalar(turns[:, :], ang[:, :], 1.0 / (2 * PI), ROUND, ALU.mult, ALU.add)
                dve.drain()
                dve.tensor_scalar(turns[:, :], turns[:, :], ROUND, None, ALU.subtract)
                dve.drain()
                dve.scalar_tensor_tensor(rest[:, :], turns[:, :], -TWO_PI_HI, ang[:, :], ALU.mult, ALU.add)
                dve.drain()
                dve.scalar_tensor_tensor(rest[:, :], turns[:, :], -TWO_PI_LO, rest[:, :], ALU.mult, ALU.add)
                dve.drain()
                dve.tensor_scalar(rest[:, :], rest[:, :], SIN_MAX, -SIN_MAX, ALU.min, ALU.max).then_inc(dve_step.sem, 1)
                dve.wait_ge(dve_step.sem, b_d + 1)
                dve.scalar_tensor_tensor(turns[:, :], rest[:, :], -1.0, rest[:, :], ALU.mult, ALU.min)
                dve.drain()
                dve.tensor_scalar(turns[:, :], turns[:, :], PI / 2, None, ALU.add).then_inc(dve_step.sem, 1)

            def scalar(act):
                act.wait_ge(dve_step.sem, b_d + 1)
                act.activation(sin[:, :], rest[:, :], ACT.Sin).then_inc(act_step.sem, 1)
                act.wait_ge(dve_step.sem, b_d + 2)
                act.activation(cos[:, :], turns[:, :], ACT.Sin).then_inc(act_step.sem, 1)
                act.wait_ge(act_step.sem, b_a + 1)
                act.activation(sin[:, :], sin[:, :], ACT.Copy, scale=const[:, a0 + freq + 1:a0 + freq + 2]).then_inc(act_step.sem, 1)
            act_step.n += 3
            dve_step.n += 2
            return {"vector": vector, "scalar": scalar}

        def rotate(x, tiles, swap, cos, sin):
            along, across = sq, y_part
            b_p, b_d, b_a, b_e, b_r = pe_step.n, dve_step.n, act_step.n, evacuated.n, rows_out.n

            def tensor(pe):
                pe.wait_ge(evacuated.sem, b_e)
                pe.wait_ge(rows_out.sem, b_r)
                for i, k in enumerate(tiles):
                    if b_d + i >= 4:
                        pe.wait_ge(dve_step.sem, b_d + i - 3 if i >= 4 else b_d)
                    pe.matmul(bank[4 + i % 4][:, :], swap, x[:, k, :], start=True, stop=True).then_inc(pe_step.sem, 1)

            def vector(dve):
                dve.wait_ge(act_step.sem, b_a)
                dve.drain()
                for i, k in enumerate(tiles):
                    dve.tensor_tensor(along[i % 2][:, :], x[:, k, :], cos[:, :], ALU.mult)
                    dve.wait_ge(pe_step.sem, b_p + i + 1)
                    dve.tensor_tensor(across[i % 2][:, :], bank[4 + i % 4][:, :], sin[:, :], ALU.mult).then_inc(dve_step.sem, 1)
                    dve.drain()
                    dve.tensor_tensor(x[:, k, :], along[i % 2][:, :], across[i % 2][:, :], ALU.add)
            pe_step.n += len(tiles)
            dve_step.n += len(tiles)
            return {"tensor": tensor, "vector": vector}

        def attention(name, pairs_n, q, k_of, v_of, static, space, finish_unit, key_bias=None):
            PER = 2 * TT
            U = 2 * PER
            turns_n = pairs_n // 2
            with ExitStack() as ctx:
                q_st, k_st = ([[x[:, n + r, :] for x in space] for r in range(2)] for n in (0, 2))
                v_st, probs_t = ([[x[:, n + r, :].rearrange("p (j d) -> p j d", d=P) for x in space] for r in range(2)] for n in (4, 6))
                probs = [sb(ctx, f"{name}_probs{r}", [P, S]) for r in range(2)]
                neg_max = [sb(ctx, f"{name}_neg_max{r}", [P, 1]) for r in range(2)]
                row_sum = [sb(ctx, f"{name}_row_sum{r}", [P, 1]) for r in range(4)]
                inv_sum = [sb(ctx, f"{name}_inv_sum{r}", [P, 1]) for r in range(2)]
                b_st, b_s, b_m, b_p = staged.n, scores_ready.n, max_ready.n, probs_ready.n
                b_hi = high_staged.n
                b_t, b_th, b_c, b_o, b_d = probs_turned.n, probs_high.n, probs_copied.n, out_ready.n, out_done.n
                once = 2 if static else 0
                each = 1 if static else 3

                def stagings(c, p):
                    out = [(q_st[p], q[:, bass.ds(c * 2 + p, 1), :])]
                    if not static:
                        out += [(k_st[p], k_of(c, p)), (v_st[p], v_of(c, p))]
                    return out

                def shaped(x, like):
                    return x[:, None, :] if len(x.shape) < len(like.shape) else x[:, :, :] if len(x.shape) == 3 else x[:, :]

                def stage_high(act, c, p):
                    act.wait_ge(out_ready.sem, b_o + c * U + (p * PER - PER))
                    act.wait_ge(staged.sem, b_st + once + c * (2 * each) + (p * each - each))
                    for st, src in stagings(c, p):
                        act.activation(shaped(st[0], src), src, ACT.Copy).then_inc(high_staged.sem, 1)

                with nc.Block() as block:
                    @block.gpsimd
                    def _(pool):
                        if static:
                            for n, (st, src) in enumerate(((k_st[0], k_of(0, 0)), (v_st[0], v_of(0, 0)))):
                                pool.wait_ge(high_staged.sem, b_hi + n + 1)
                                pool.tensor_tensor(shaped(st[1], src), src, shaped(st[0], src).bitcast(F32),
                                                   ALU.subtract).then_inc(staged.sem, 1)
                        with pool.Fori(0, turns_n) as c:
                            for p in range(2):
                                for n, (st, src) in enumerate(stagings(c, p)):
                                    pool.wait_ge(high_staged.sem, b_hi + once + c * (2 * each) + (p * each + n + 1))
                                    pool.tensor_tensor(shaped(st[1], src), src, shaped(st[0], src).bitcast(F32),
                                                       ALU.subtract).then_inc(staged.sem, 1)

                    @block.tensor
                    def _(pe):
                        with pe.Fori(0, turns_n) as c:
                            def score(u):
                                p, e, i = u // PER, u // TT % 2, u % TT
                                n = (i + 1) * P
                                if u % PER == 0:
                                    pe.wait_ge(staged.sem, b_st + once + c * (2 * each) + (p * each + each))
                                pe.wait_ge(probs_ready.sem, b_p + c * U + (u - 1))
                                out, rows = bank[u % 2], slice(64 * e, 64 * e + 64)
                                keys = k_st[0 if static else p]
                                three_products(pe, out[:, 0:n], [x[rows, i * P:n] for x in q_st[p]],
                                               [x[rows, 0:n] for x in keys], True, False)
                                if key_bias is not None:
                                    sel, parts = key_bias
                                    pe.matmul(out[:, 0:n], sel[:, bass.ds(c * (4 * P) + (2 * p + e) * P, P)], parts[:, 0:n],
                                              start=False, stop=False)
                                pe.matmul(out[:, i * P:n], ident_b[:, :], bias_b[:, :], start=False,
                                          stop=True).then_inc(scores_ready.sem, 1)

                            def turn(u):
                                i = u % TT
                                pe.wait_ge(probs_ready.sem, b_p + c * U + (u + 1))
                                pe.wait_ge(probs_copied.sem, b_c + c * U + (u - 1))
                                for j in range(i + 1):
                                    last = pe.transpose(bank[2 + u % 2][:, j * P:(j + 1) * P], probs[u % 2][:, j * P:(j + 1) * P], ident)
                                last.then_inc(probs_turned.sem, 1)

                            def values(u):
                                p, e, i = u // PER, u // TT % 2, u % TT
                                pe.wait_ge(probs_copied.sem, b_c + c * U + (u + 1))
                                pe.wait_ge(out_done.sem, b_d + c * U + (u - 1))
                                vals = v_st[0 if static else p]
                                for j in range(i + 1):
                                    last = three_products(pe, bank[4 + u % 2][:, 0:HD], [x[:, j, :] for x in probs_t[u % 2]],
                                                          [x[:, j, e * HD:(e + 1) * HD] for x in vals], j == 0, j == i)
                                last.then_inc(out_ready.sem, 1)
                            for step in range(U + 2):
                                if step < U:
                                    score(step)
                                if 1 <= step <= U:
                                    turn(step - 1)
                                if step >= 2:
                                    values(step - 2)

                    @block.vector
                    def _(dve):
                        with dve.Fori(0, turns_n) as c:
                            def maximum(u):
                                n = (u % TT + 1) * P
                                dve.wait_ge(scores_ready.sem, b_s + c * U + (u + 1))
                                dve.wait_ge(probs_ready.sem, b_p + c * U + (u - 1))
                                dve.tensor_reduce(neg_max[u % 2][:, :], bank[u % 2][:, 0:n], AX_X, ALU.max, negate=True).then_inc(max_ready.sem, 1)

                            def low(u):
                                n = (u % TT + 1) * P
                                dve.wait_ge(probs_high.sem, b_th + c * U + (u + 1))
                                dve.tensor_tensor(probs_t[u % 2][1][:, 0:u % TT + 1, :],
                                                  bank[2 + u % 2][:, 0:n].rearrange("p (j t) -> p j t", t=P),
                                                  probs_t[u % 2][0][:, 0:u % TT + 1, :].bitcast(F32), ALU.subtract).then_inc(probs_copied.sem, 1)

                            def take(u):
                                p, e, i = u // PER, u // TT % 2, u % TT
                                dve.wait_ge(out_ready.sem, b_o + c * U + (u + 1))
                                dve.reciprocal(inv_sum[u % 2][:, :], row_sum[u % 4][:, :])
                                dve.drain()
                                finish_unit(dve, c, p, e, i, bank[4 + u % 2][:, 0:HD], inv_sum[u % 2][:, :]).then_inc(out_done.sem, 1)
                            for step in range(U + 2):
                                if step < U:
                                    maximum(step)
                                if 1 <= step <= U:
                                    low(step - 1)
                                if step >= 2:
                                    take(step - 2)

                    @block.scalar
                    def _(act):
                        if static:
                            act.activation(k_st[0][0][:, :], k_of(0, 0), ACT.Copy).then_inc(high_staged.sem, 1)
                            act.activation(v_st[0][0][:, :, :], v_of(0, 0), ACT.Copy).then_inc(high_staged.sem, 1)
                        with act.Fori(0, turns_n) as c:
                            def exponential(u):
                                n = (u % TT + 1) * P
                                act.wait_ge(max_ready.sem, b_m + c * U + (u + 1))
                                act.wait_ge(probs_turned.sem, b_t + c * U + (u - 1))
                                act.wait_ge(out_done.sem, b_d + c * U + (u - 3))
                                act.activation(probs[u % 2][:, 0:n], bank[u % 2][:, 0:n], ACT.Exp, bias=neg_max[u % 2][:, :],
                                               accum_out=row_sum[u % 4][:, :]).then_inc(probs_ready.sem, 1)

                            def copy(u):
                                i = u % TT
                                act.wait_ge(probs_turned.sem, b_t + c * U + (u + 1))
                                act.wait_ge(out_ready.sem, b_o + c * U + (u - 1))
                                act.activation(probs_t[u % 2][0][:, 0:i + 1, :],
                                               bank[2 + u % 2][:, 0:(i + 1) * P].rearrange("p (j t) -> p j t", t=P),
                                               ACT.Copy).then_inc(probs_high.sem, 1)
                            stage_high(act, c, 0)
                            for step in range(U + 1):
                                if step == 3:
                                    stage_high(act, c, 1)
                                if step < U:
                                    exponential(step)
                                if step >= 1:
                                    copy(step - 1)
                staged.n += once + pairs_n * each
                high_staged.n += once + pairs_n * each
                for t in (scores_ready, max_ready, probs_ready, probs_turned, probs_high, probs_copied, out_ready, out_done):
                    t.n += turns_n * U

        def linear_attention(name, heads, dk, q, k, v, dv, scale, take, wts, decay_of=None, gates=None):
            turns_n = heads // 2
            per = P // dk
            with ExitStack() as ctx:
                k_st, q_st = sq, y_part
                dec = sb(ctx, f"{name}_dec", [P, TT, S]) if gates else None
                m_row = [sb(ctx, f"{name}_m_row{e}", [P, S]) for e in range(2)] if gates else None
                b_st, b_s, b_w, b_o, b_d = staged.n, scores_ready.n, weighted.n, out_ready.n, out_done.n
                b_g, b_e, b_k = gap_ready.n, decay_ready.n, kept.n
                b_r = [t.n for t in bias_row_in]
                U = 2 * TT
                n_st = 2 if per == 2 else 4
                with nc.Block() as block:
                    if gates:
                        @block.sync
                        def _(sp):
                            with sp.Fori(0, turns_n) as c:
                                for e in range(2):
                                    sp.wait_ge(gap_ready.sem, b_g + c * U + (e * TT - TT))
                                    sp.dma_start(m_row[e][:, :], gates[0][bass.ds(c * 2 + e, 1), :].broadcast_to([P, S]))\
                                        .then_inc(bias_row_in[e].sem, 16)

                        @block.scalar
                        def _(act):
                            with act.Fori(0, turns_n) as c:
                                for u in range(U):
                                    j = u % TT
                                    act.wait_ge(gap_ready.sem, b_g + c * U + (u + 1))
                                    act.activation(dec[:, j, j * P:S], dec[:, j, j * P:S], ACT.Exp).then_inc(decay_ready.sem, 1)

                    @block.gpsimd
                    def _(pool):
                        with pool.Fori(0, turns_n) as c:
                            pool.wait_ge(scores_ready.sem, b_s + c * U)
                            for e in range(n_st // 2):
                                x = c if per == 2 else c * 2 + e
                                pool.tensor_copy(k_st[e][:, None, :], k[:, bass.ds(x, 1), :]).then_inc(staged.sem, 1)
                                pool.tensor_copy(q_st[e][:, None, :], q[:, bass.ds(x, 1), :]).then_inc(staged.sem, 1)
                            if gates:
                                for u in range(U):
                                    j = u % TT
                                    pool.wait_ge(decay_ready.sem, b_e + c * U + (u + 1))
                                    pool.tensor_tensor(dec[:, j, j * P:(j + 1) * P], dec[:, j, j * P:(j + 1) * P],
                                                       cst("causal_keep"), ALU.mult).then_inc(kept.sem, 1)

                    @block.tensor
                    def _(pe):
                        with pe.Fori(0, turns_n) as c:
                            pe.wait_ge(staged.sem, b_st + (c + 1) * n_st)
                            for u in range(U):
                                e, j = u // TT, u % TT
                                pe.wait_ge(weighted.sem, b_w + c * U + (u - 3))
                                if per == 2:
                                    kk, qq = k_st[0][64 * e:64 * e + 64, :], q_st[0][64 * e:64 * e + 64, :]
                                else:
                                    kk, qq = k_st[e][:, :], q_st[e][:, :]
                                pe.matmul(bank[j][:, j * P:S], kk[:, j * P:(j + 1) * P], qq[:, j * P:S],
                                          start=True, stop=True).then_inc(scores_ready.sem, 1)
                            for u in range(U):
                                e, i = u // TT, u % TT
                                pe.wait_ge(weighted.sem, b_w + c * U + (e * TT + i + 1))
                                pe.wait_ge(out_done.sem, b_d + c * U + (u - 1))
                                for j in range(i + 1):
                                    last = pe.matmul(bank[4 + u % 2][:, 0:dv], wts[e][:, j, i * P:(i + 1) * P], v(c, e, j),
                                                     start=j == 0, stop=j == i)
                                last.then_inc(out_ready.sem, 1)

                    @block.vector
                    def _(dve):
                        with dve.Fori(0, turns_n) as c:
                            def gap(u):
                                e, j = u // TT, u % TT
                                if j == 0:
                                    dve.wait_ge(bias_row_in[e].sem, b_r[e] + (c + 1) * 16)
                                dve.wait_ge(weighted.sem, b_w + c * U + (u - 3))
                                dve.tensor_scalar(dec[:, j, j * P:S], m_row[e][:, j * P:S], gates[1][:, j, bass.ds(c * 2 + e, 1)],
                                                  0.0, ALU.add, ALU.min).then_inc(gap_ready.sem, 1)

                            def weigh(u):
                                e, j = u // TT, u % TT
                                n = S - j * P
                                dve.wait_ge(scores_ready.sem, b_s + c * U + (u + 1))
                                if gates:
                                    dve.wait_ge(kept.sem, b_k + c * U + (u + 1))
                                    d = dec[:, j, j * P:S]
                                else:
                                    d = decay_of(c * 2 + e)[:, :, 0:n]
                                if j == 0:
                                    dve.wait_ge(out_ready.sem, b_o + c * U + (e * TT - TT))
                                o, s = wts[e][:, j, j * P:S], bank[j][:, j * P:S]
                                if not gates:
                                    o, s = o[:, None, :], s[:, None, :]
                                dve.scalar_tensor_tensor(o, s, scale, d, ALU.mult, ALU.mult).then_inc(weighted.sem, 1)

                            if gates:
                                for u in range(TT):
                                    gap(u)
                            for u in range(U):
                                weigh(u)
                                if gates and u + TT < U:
                                    gap(u + TT)
                            for u in range(U):
                                e, i = u // TT, u % TT
                                dve.wait_ge(out_ready.sem, b_o + c * U + (u + 1))
                                take(dve, c, e, i, bank[4 + u % 2][:, 0:dv]).then_inc(out_done.sem, 1)
                staged.n += turns_n * n_st
                for t in (scores_ready, weighted, out_ready, out_done):
                    t.n += turns_n * U
                if gates:
                    for t in (gap_ready, decay_ready, kept):
                        t.n += turns_n * U
                    for t in bias_row_in:
                        t.n += 16 * turns_n

        def head_norm(name, h, heads, gate, sq_h):
            with ExitStack() as ctx:
                ss = sb(ctx, f"{name}_hss", [P, TT, heads])
                b_a, b_d = act_step.n, dve_step.n
                with nc.Block(no_gpsimd_drain=True) as block:
                    @block.scalar
                    def _(act):
                        for t in range(TT):
                            act.activation(sq_h[:, t, :, :], h[:, t, :, :], ACT.Square).then_inc(act_step.sem, 1)
                        act.wait_ge(dve_step.sem, b_d + 1)
                        act.activation(ss[:, :, :], ss[:, :, :], ACT.Sqrt, scale=1.0 / P, bias=EPS).then_inc(act_step.sem, 1)

                    @block.vector
                    def _(dve):
                        for t in range(TT):
                            dve.wait_ge(act_step.sem, b_a + t + 1)
                            dve.tensor_reduce(ss[:, t, :], sq_h[:, t, :, :], AX_X, ALU.add)
                        dve.drain()
                        dve.engine_nop().then_inc(dve_step.sem, 1)
                        dve.wait_ge(act_step.sem, b_a + TT + 1)
                        dve.reciprocal(ss[:, :, :], ss[:, :, :])
                        dve.drain()
                        for t in range(TT):
                            for n in range(heads):
                                dve.scalar_tensor_tensor(h[:, t, n, :], h[:, t, n, :], ss[:, t, n:n + 1], gate[:, t, n, :],
                                                         ALU.mult, ALU.mult)
                act_step.n += TT + 1
                dve_step.n += 1

        def compressed_loads(pe_rows, w1, w2):
            b_in = [t.n for t in inputs_in]

            def sync(sp):
                for s, n in enumerate(("cmp_pos_k", "cmp_pos_v")):
                    sp.dma_start(pe_rows[:, s, :], io[n][0].rearrange("(j l) d -> j (l d)", l=2)).then_inc(inputs_in[0].sem, 16)
                for s, n in enumerate(("cmp_k_w1", "cmp_v_w1")):
                    sp.dma_start(w1[s][:, :, :], io[n][0].rearrange("(j p) n -> p j n", p=P)).then_inc(inputs_in[1 + s].sem, 16)
                for s, n in enumerate(("cmp_k_w2", "cmp_v_w2")):
                    sp.dma_start(w2[:, s, :, :], io[n][0].rearrange("(t p) d -> p t d", p=P)).then_inc(inputs_in[3].sem, 16)
            for t, n in zip(inputs_in, (2, 1, 1, 2)):
                t.n += 16 * n
            return {"sync": sync}, b_in

        def compressed(ctx, loaded, pe_rows, w1, w2, qk, vg, gate, o):
            pe_t = sb(ctx, "pe_t", [P, 2, CB // 2])
            blk = sb(ctx, "cmp_blk", [P, 2, CB // 2, KV, CB])
            hid_k = sb(ctx, "cmp_hid_k", [P, 2, KV, CB])
            hid_v = sb(ctx, "cmp_hid_v", [P, 2, KV, 4, CB])
            k_cmp = sb(ctx, "k_cmp", [P, CB])
            v_blk = sb(ctx, "cmp_v_blk", [P, KV, 4, HD])
            sc = sb(ctx, "cmp_sc", [P, KV, TT, 4, CB])
            mx = sb(ctx, "cmp_max", [P, KV, TT, 4])
            coef = sb(ctx, "cmp_coef", [P, KV, TT, 4])
            probs_t = sb(ctx, "cmp_probs_t", [P, KV, S])
            p0, d0, a0, g0 = pe_step.n, dve_step.n, act_step.n, pool_step.n
            with nc.Block() as block:
                @block.gpsimd
                def _(pool):
                    pool.memset(blk[:, :, :, :, NC:CB], 0.0).then_inc(pool_step.sem, 1)
                    pool.memset(v_blk[:, :, :, :], 0.0).then_inc(pool_step.sem, 1)

                @block.tensor
                def _(pe):
                    pe.wait_ge(inputs_in[0].sem, loaded[0] + 32)
                    for s in range(2):
                        pe.transpose(bank[0][:, s * 16:(s + 1) * 16], pe_rows[:, s, :], ident[0:16, 0:16])
                    pe.matmul(bank[1][:, :], cst("swap_ret"), qk[:, 4, :], start=True, stop=True)
                    pe.matmul(bank[2][:, :], cst("swap_ret"), qk[:, 5, :], start=True, stop=True).then_inc(pe_step.sem, 1)
                    pe.wait_ge(pool_step.sem, g0 + 1)
                    for s in range(2):
                        pe.wait_ge(inputs_in[1 + s].sem, loaded[1 + s] + 16)
                        pe.wait_ge(dve_step.sem, d0 + s + 1)
                        for t in range(2):
                            for j in range(CB // 2):
                                last = pe.matmul(bank[3 + 2 * s + t][:, 0:KV * CB], w1[s][:, j, t * P:(t + 1) * P],
                                                 blk[:, s, j, :, :].rearrange("p g c -> p (g c)"), start=j == 0, stop=j == CB // 2 - 1)
                        last.then_inc(pe_step.sem, 1)
                    pe.wait_ge(inputs_in[3].sem, loaded[3] + 32)
                    pe.wait_ge(act_step.sem, a0 + 1)
                    for g in range(KV):
                        for t in range(2):
                            last = pe.matmul(bank[0][64 * g:64 * g + 64, 0:CB], w2[:, 0, t, :], hid_k[:, t, g, :], start=t == 0, stop=t == 1)
                    last.then_inc(pe_step.sem, 1)
                    pe.wait_ge(act_step.sem, a0 + 2)
                    for g in range(KV):
                        for t in range(2):
                            last = pe.matmul(bank[1][:, g * HD:(g + 1) * HD], hid_v[:, t, g, :, :].rearrange("p h c -> p (h c)"),
                                             w2[:, 1, t, :], start=t == 0, stop=t == 1)
                    last.then_inc(pe_step.sem, 1)
                    pe.wait_ge(dve_step.sem, d0 + 3)
                    for g in range(KV):
                        for i in range(TT):
                            for h in range(4):
                                at_col = (i * 4 + h) * CB
                                last = pe.matmul(bank[(2, 7)[g]][:, at_col:at_col + CB], qk[64 * g:64 * g + 64, h, i * P:(i + 1) * P],
                                                 k_cmp[64 * g:64 * g + 64, :], start=True, stop=True)
                        last.then_inc(pe_step.sem, 1)
                    for g in range(KV):
                        pe.wait_ge(dve_step.sem, d0 + 7 + g)
                        for i in range(TT):
                            last = pe.transpose(bank[3 + g][:, i * P:(i + 1) * P], sc[:, g, i, :, :].rearrange("p h c -> p (h c)"), ident)
                        last.then_inc(pe_step.sem, 1)
                    pe.wait_ge(dve_step.sem, d0 + 10)
                    for i in range(TT):
                        for g in range(KV):
                            last = pe.matmul(bank[4 + i][:, g * 256:(g + 1) * 256], probs_t[:, g, i * P:(i + 1) * P],
                                             v_blk[:, g, :, :].rearrange("p h d -> p (h d)"), start=True, stop=True)
                        last.then_inc(pe_step.sem, 1)

                @block.scalar
                def _(act):
                    act.activation(gate[:, :, :], vg[:, :, 256:280], ACT.Sigmoid)
                    act.wait_ge(pe_step.sem, p0 + 2)
                    for t in range(2):
                        last = act.activation(hid_k[:, t, :, :], bank[3 + t][:, 0:KV * CB].rearrange("p (g c) -> p g c", c=CB), ACT.Silu)
                    last.then_inc(act_step.sem, 1)
                    act.wait_ge(pe_step.sem, p0 + 3)
                    for t in range(2):
                        for h in range(4):
                            last = act.activation(hid_v[:, t, :, h, :], bank[5 + t][:, 0:KV * CB].rearrange("p (g c) -> p g c", c=CB), ACT.Silu)
                    last.then_inc(act_step.sem, 1)
                    for g in range(KV):
                        act.wait_ge(dve_step.sem, d0 + 5 + g)
                        act.activation(sc[:, g, :, :, :], sc[:, g, :, :, :], ACT.Exp).then_inc(act_step.sem, 1)

                @block.vector
                def _(dve):
                    dve.wait_ge(pe_step.sem, p0 + 1)
                    dve.tensor_copy(pe_t[:, :, :], bank[0][:, 0:CB].rearrange("p (s j) -> p s j", s=2))
                    dve.drain()
                    for s in range(2):
                        for g in range(KV):
                            for h in range(2):
                                half = slice(64 * h, 64 * h + 64)
                                src = qk[half, 4 + s, :] if g == h else bank[1 + s][half, :]
                                for r in range(2):
                                    x = src[:, 16 * r:16 * r + 16 * NC].rearrange("p (c j l) -> p j c l", j=8, l=2)[:, :, :, h]
                                    last = dve.tensor_tensor(blk[half, s, 8 * r:8 * r + 8, g, 0:NC], x,
                                                             pe_t[half, s, 8 * r:8 * r + 8, None].broadcast_to([64, 8, NC]), ALU.add)
                        last.then_inc(dve_step.sem, 1)
                    dve.wait_ge(pe_step.sem, p0 + 4)
                    dve.tensor_copy(k_cmp[:, :], bank[0][:, 0:CB]).then_inc(dve_step.sem, 1)
                    dve.wait_ge(pe_step.sem, p0 + 5)
                    dve.wait_ge(pool_step.sem, g0 + 2)
                    for g in range(KV):
                        for h in range(4):
                            last = dve.tensor_copy(v_blk[32 * h:32 * h + 32, g, h, :], bank[1][32 * h:32 * h + 32, g * HD:(g + 1) * HD])
                    last.then_inc(dve_step.sem, 1)
                    bias = cst("cmp_bias").rearrange("p (i c) -> p i c", c=CB)[:, :, None, :].broadcast_to([P, TT, 4, CB])
                    for g in range(KV):
                        dve.wait_ge(pe_step.sem, p0 + 6 + g)
                        s4 = bank[(2, 7)[g]][:, :].rearrange("p (i h c) -> p i h c", h=4, c=CB)
                        dve.tensor_tensor(sc[:, g, :, :, :], s4, bias, ALU.add)
                        dve.drain()
                        dve.tensor_reduce(mx[:, g, :, :], sc[:, g, :, :, :], AX_X, ALU.max)
                        dve.drain()
                        dve.tensor_tensor(sc[:, g, :, :, :], sc[:, g, :, :, :], mx[:, g, :, :, None].broadcast_to([P, TT, 4, CB]),
                                          ALU.subtract).then_inc(dve_step.sem, 1)
                    for g in range(KV):
                        dve.wait_ge(act_step.sem, a0 + 3 + g)
                        dve.tensor_reduce(mx[:, g, :, :], sc[:, g, :, :, :], AX_X, ALU.add)
                        dve.drain()
                        dve.reciprocal(mx[:, g, :, :], mx[:, g, :, :])
                        dve.tensor_tensor(coef[:, g, :, :], gate[:, :, :].rearrange("p i (e c b) -> p i e c b", e=2, b=3)[:, :, g, :, 0],
                                          cst("cmp_any")[:, :, None].broadcast_to([P, TT, 4]), ALU.mult)
                        dve.drain()
                        dve.tensor_tensor(coef[:, g, :, :], coef[:, g, :, :], mx[:, g, :, :], ALU.mult)
                        dve.drain()
                        dve.tensor_tensor(sc[:, g, :, :, :], sc[:, g, :, :, :], coef[:, g, :, :, None].broadcast_to([P, TT, 4, CB]),
                                          ALU.mult).then_inc(dve_step.sem, 1)
                    for g in range(KV):
                        dve.wait_ge(pe_step.sem, p0 + 8 + g)
                        dve.tensor_copy(probs_t[:, g, :], bank[3 + g][:, :]).then_inc(dve_step.sem, 1)
                    for i in range(TT):
                        dve.wait_ge(pe_step.sem, p0 + 10 + i)
                        dve.tensor_copy(o[:, i, :], bank[4 + i][:, :])
            pe_step.n += 13
            dve_step.n += 10
            act_step.n += 4
            pool_step.n += 2

        def nsa(cos_r, sin_r, o):
            with ExitStack() as mid:
                qk = sb(mid, "nsa_qk", [P, 8, S])
                vg = sb(mid, "nsa_vg", [P, TT, 280])
                gate = sb(mid, "nsa_gate", [P, TT, GATES])
                with ExitStack() as inner:
                    pe_rows = sb(inner, "pe_rows", [CB // 2, 2, P])
                    w1 = [sb(inner, f"cmp_w1_{s}", [P, CB // 2, CH]) for s in range(2)]
                    w2 = sb(inner, "cmp_w2", [P, 2, 2, HD])
                    with ExitStack() as deep:
                        cos, sin = sb(deep, "nsa_cos", [P, S]), sb(deep, "nsa_sin", [P, S])

                        def take_rows(dve, g, t):
                            return dve.tensor_copy(vg[:, t, :], bank[4 + t][:, 0:280])
                        pos_i = sb(deep, "pos_i", [P, S], I32)
                        work = [sb(deep, f"rope_{n}", [P, S]) for n in ("ang", "turns", "rest")]
                        first = [positions_load(pos_i), sums(xT), inverse_root()]
                        stage, ready = normalise(0)
                        first.append(stage)
                        first.append(dense("q", two_chunks(a_tiles), copy_to(qk, float(HD) ** -0.5), tile_ready=ready))
                        first.append(rope_tables(work, pos_i, 0, cos, sin))
                        first.append(dense("kcvc", two_chunks(a_tiles), copy_to(qk[:, 4:8, :])))
                        stage, loaded = compressed_loads(pe_rows, w1, w2)
                        first.append(stage)
                        first.append(rotate(qk, (0, 1, 2, 3, 4, 6, 7), cst("swap_nsa"), cos, sin))
                        first.append(dense_rows("vg", evac_dve=take_rows))
                        first.append(rope_tables(work, pos_i, 2, cos_r, sin_r))
                        run(*first)
                    with ExitStack() as deep:
                        compressed(deep, loaded, pe_rows, w1, w2, qk, vg, gate, o)
                coef = sb(mid, "nsa_coef", [P, 1])
                space = [sb(mid, f"nsa_space_{n}", [P, KT, S], F32R) for n in ("hi", "lo")]

                def branch(b):
                    def finish_unit(dve, c, p, e, i, out, inv_sum):
                        g = gate[:, i, :].rearrange("p (e c b) -> p e c b", e=2, b=3)[:, e, bass.ds(c * 2 + p, 1), b:b + 1]
                        dve.tensor_tensor(coef[:, :, None], inv_sum[:, :, None], g, ALU.mult)
                        dve.drain()
                        dst = o[:, i, :].rearrange("p (e c d) -> p e c d", e=2, d=HD)[:, e, bass.ds(c * 2 + p, 1), :]
                        return dve.scalar_tensor_tensor(dst, out[:, None, :], coef[:, :], dst, ALU.mult, ALU.add)
                    return finish_unit
                attention("slc", HQ // 2, qk, lambda c, p: qk[:, 6, :], lambda c, p: vg[:, :, 0:P], True, space, branch(1))
                attention("win", HQ // 2, qk, lambda c, p: qk[:, 7, :], lambda c, p: vg[:, :, P:2 * P], True, space, branch(2))

        def retention(cos, sin, spare, h_hi, h_lo):
            with ExitStack() as ctx:
                qk = sb(ctx, "ret_qk", [P, 8, S])
                vg = sb(ctx, "ret_vg", [P, TT, 2, RH * RD])
                h = qk[:, 0:RH, :].rearrange("p n (t d) -> p t n d", d=RD)
                wts = [spare, sb(ctx, "ret_wts", [P, TT, S])]
                decay = sb(ctx, "ret_decay", [P, RH, S])
                b_in = inputs_in[0].n
                inputs_in[0].n += 16

                def decay_load(sp):
                    sp.dma_start(decay[:, :, :], io["decay"]).then_inc(inputs_in[0].sem, 16)

                def rows_dve(dve, g, t):
                    return dve.tensor_copy(vg[:, t, bass.ds(g, 1), :], bank[4 + t][:, None, :])
                with ExitStack() as inner:
                    run(dense("rqk", two_chunks(a_tiles), copy_to(qk)), {"sync": decay_load},
                        rotate(qk, range(4), cst("swap_ret"), cos, sin),
                        dense_rows("rvg", evac_dve=rows_dve),
                        rotate(qk, range(4, 8), cst("swap_ret"), cos, sin))
                with nc.Block() as block:
                    @block.sync
                    def _(sp):
                        sp.wait_ge(inputs_in[0].sem, b_in + 16)

                    @block.scalar
                    def _(act):
                        act.activation(vg[:, :, 1, :], vg[:, :, 1, :], ACT.Silu)

                def take(dve, c, e, i, out):
                    return dve.tensor_copy(h[:, i, bass.ds(c * 2 + e, 1), :], out[:, None, :])
                linear_attention("ret", RH, RD, qk[:, 0:4, :], qk[:, 4:8, :],
                                 lambda c, e, j: vg[:, j, 0, bass.ds(c * 256 + e * P, P)], RD, float(RD) ** -0.5,
                                 take, wts, decay_of=lambda x: decay[:, bass.ds(x, 1), :])
                head_norm("ret", h, RH, vg[:, :, 1, :].rearrange("p t (n d) -> p t n d", d=RD),
                          wts[0][:, :, :].rearrange("p t (n d) -> p t n d", d=RD))
                to_features(lambda t, k: h[:, t, k, :], 4, h_hi, h_lo, 4)

        def mixing(h_hi, h_lo):
            with ExitStack() as ctx:
                mix = sb(ctx, "mix", [P, 1, S])
                mix_hi = sb(ctx, "mix_hi", [P, KT, S], F32R)
                mix_lo = sb(ctx, "mix_lo", [P, KT, S], F32R)
                sig = sb(ctx, "mix_sig", [P, 2, S])
                half_mix = sb(ctx, "half_mix", [P, 2, S])
                h_tiles = [(h_hi[:, k, :], h_lo[:, k, :]) for k in range(KT)]
                mix_tiles = [(mix_hi[:, k, :], mix_lo[:, k, :]) for k in range(KT)]
                chunks = [two_chunks(a_tiles)[0], [[(k * 256 + c * P, h_tiles[4 * c + k]) for k in range(4)] for c in range(2)]]
                b_mix = mixed.n
                chunk = lambda b, m: (b - 1) // 2 if isinstance(b, int) else m["i"]

                def early_act(act, b, slot, m):
                    if slot != m["slot"]:
                        return
                    act.wait_ge(products_done.sem, m["prod"] + b + 1)
                    act.wait_ge(evacuated.sem, m["evac"] + b)
                    for c in range(2):
                        ins = act.activation(sig[:, c, :], bank[2 * slot + c][:, :], ACT.Sigmoid)
                    ins.then_inc(evacuated.sem, 1)

                def early_dve(dve, b, slot, m):
                    if slot == m["slot"]:
                        return
                    dve.wait_ge(products_done.sem, m["prod"] + b + 1)
                    dve.wait_ge(evacuated.sem, m["evac"] + b)
                    for c in range(2):
                        ins = dve.tensor_tensor(half_mix[:, c, :], bank[2 * slot + c][:, :], sig[:, c, :], ALU.mult)
                    ins.then_inc(evacuated.sem, 1)
                    dve.drain()
                    dve.tensor_tensor(mix[:, :, :], half_mix[:, 0:1, :], half_mix[:, 1:2, :], ALU.add).then_inc(mixed.sem, 1)

                def late_act(act, b, slot, m):
                    if slot != m["slot"]:
                        ch = chunk(b, m)
                        act.wait_ge(mixed.sem, b_mix + ch * 3 + 1)
                        act.activation(mix_hi[:, bass.ds(ch, 1), :], mix[:, :, :], ACT.Copy).then_inc(mixed.sem, 1)

                def late_dve(dve, b, slot, m):
                    if slot != m["slot"]:
                        ch = chunk(b, m)
                        dve.wait_ge(mixed.sem, b_mix + ch * 3 + 2)
                        dve.tensor_tensor(mix_lo[:, bass.ds(ch, 1), :], mix[:, :, :], mix_hi[:, bass.ds(ch, 1), :].bitcast(F32),
                                          ALU.subtract).then_inc(mixed.sem, 1)
                sq_act, sq_dve = sums_on_the_way(xT)
                first = dense("mix", chunks, early_dve, late_dve, early_act, late_act)
                mixed.n += 3 * KT
                run(first, dense("out1", two_chunks(mix_tiles), add_to(xT), sq_dve, none, sq_act,
                                 tile_ready=lambda k: (mixed.sem, b_mix + 3 * k + 3)))

        def mlp():
            with ExitStack() as ctx:
                h_hi = sb(ctx, "mlp_hi", [P, KT, S], F32R)
                h_lo = sb(ctx, "mlp_lo", [P, KT, S], F32R)
                pos = [sb(ctx, f"mlp_pos{r}", [P, 2, S]) for r in range(2)]
                pos_sq = [sb(ctx, f"mlp_pos_sq{r}", [P, 2, S]) for r in range(2)]
                h_tiles = [(h_hi[:, k, :], h_lo[:, k, :]) for k in range(KT)]

                def early_act(act, b, slot, m):
                    act.wait_ge(products_done.sem, m["prod"] + b + 1)
                    act.wait_ge(hid_ready.sem, m["hid"] + b - 1)
                    for c in range(2):
                        ins = act.activation(pos[slot][:, c, :], bank[2 * slot + c][:, :], ACT.Relu)
                    ins.then_inc(evacuated.sem, 1)

                def early_dve(dve, b, slot, m):
                    dve.wait_ge(evacuated.sem, m["evac"] + b + 1)
                    dve.tensor_tensor(pos_sq[slot][:, :, :], pos[slot][:, :, :], pos[slot][:, :, :], ALU.mult)

                def late_act(act, b, slot, m):
                    act.wait_ge(evacuated.sem, m["evac"] + b + 1)
                    act.activation(h_hi[:, bass.ds(b * 2, 2), :], pos[slot][:, :, :], ACT.Square).then_inc(part_ready.sem, 1)

                def late_dve(dve, b, slot, m):
                    dve.wait_ge(part_ready.sem, m["part"] + b + 1)
                    dve.drain()
                    dve.tensor_tensor(h_lo[:, bass.ds(b * 2, 2), :], pos_sq[slot][:, :, :], h_hi[:, bass.ds(b * 2, 2), :].bitcast(F32),
                                      ALU.subtract).then_inc(hid_ready.sem, 1)
                stages = [inverse_root()]
                stage, ready = normalise(1)
                stages.append(stage)
                for g in range(4):
                    b_hid = hid_ready.n
                    stages.append(dense(f"up{g}", two_chunks(a_tiles), early_dve, late_dve, early_act, late_act,
                                        tile_ready=ready if g == 0 else None))
                    part_ready.n += 4
                    hid_ready.n += 4
                    sq_act, sq_dve = sums_on_the_way(xT) if g == 3 else (none, none)
                    stages.append(dense(f"down{g}", two_chunks(h_tiles), add_to(xT), sq_dve, none, sq_act,
                                        tile_ready=(lambda b_hid: lambda k: (hid_ready.sem, b_hid + k // 2 + 1))(b_hid)))
                    if g == 3:
                        squared.n += KT
                        summed.n += KT
                stages += [inverse_root(), update(2)]
                run(*stages)

        def first_block():
            with ExitStack() as ctx:
                cos_r, sin_r = sb(ctx, "ret_cos", [P, S]), sb(ctx, "ret_sin", [P, S])
                o = sb(ctx, "nsa_o", [P, TT, HQ * HD])
                nsa(cos_r, sin_r, o)
                h_hi = sb(ctx, "cat_hi", [P, KT, S], F32R)
                h_lo = sb(ctx, "cat_lo", [P, KT, S], F32R)
                to_features(lambda t, k: o[:, t, k * P:(k + 1) * P], 4, h_hi, h_lo, 0)
                retention(cos_r, sin_r, o, h_hi, h_lo)
                mixing(h_hi, h_lo)
                squared.n += KT
                summed.n += KT
            mlp()

        def log_sigmoid(act, dve, x, t1, t2, b_a, b_d, part):
            if part == "dve":
                dve.scalar_tensor_tensor(t1, x, -1.0, x, ALU.mult, ALU.min).then_inc(dve_step.sem, 1)
                dve.tensor_scalar(t2, x, 0.0, None, ALU.min)
                dve.drain()
                dve.wait_ge(act_step.sem, b_a + 1)
                dve.tensor_tensor(x, t2, t1, ALU.subtract)
                dve.drain()
            else:
                act.wait_ge(dve_step.sem, b_d + 1)
                act.activation(t1, t1, ACT.Exp)
                act.drain()
                act.activation(t1, t1, ACT.Ln, bias=1.0).then_inc(act_step.sem, 1)

        def mlstm():
            with ExitStack() as ctx:
                h = sb(ctx, "ml_h", [P, TT, MH, MV])
                with ExitStack() as inner:
                    qk = sb(inner, "ml_qk", [P, 8, S])
                    v = sb(inner, "ml_v", [P, TT, MH, MV + 1])
                    og = sb(inner, "ml_og", [P, TT, MH, MV])
                    a_col = sb(inner, "ml_a_col", [P, TT, MH])
                    e_col = sb(inner, "ml_e_col", [P, TT, MH])
                    with ExitStack() as tmp:
                        bias = sb(tmp, "ml_bias", [MH, 2])
                        lf, ig, t1, t2 = (sb(tmp, f"ml_{n}", [MH, S]) for n in ("lf", "ig", "t1", "t2"))
                        fsum, mrun, one = (sb(tmp, f"ml_{n}", [MH, S]) for n in ("fsum", "mrun", "one"))
                        b_in = inputs_in[0].n
                        inputs_in[0].n += 32

                        def bias_load(sp):
                            sp.dma_start(bias[:, 0:1], io["mlstm_b_gate_2"][0, 0:MH].rearrange("(h a) -> h a", a=1)).then_inc(inputs_in[0].sem, 16)
                            sp.dma_start(bias[:, 1:2], io["mlstm_b_gate_2"][0, MH:2 * MH].rearrange("(h a) -> h a", a=1)).then_inc(inputs_in[0].sem, 16)

                        def gate_rows(dve, b, slot, m):
                            dve.wait_ge(products_done.sem, m["prod"] + b + 1)
                            dve.tensor_copy(ig[:, :], bank[2 * slot][0:MH, :])
                            dve.tensor_copy(lf[:, :], bank[2 * slot][32:32 + MH, :]).then_inc(evacuated.sem, 1)

                        def v_rows(dve, g, t):
                            return dve.tensor_copy(v[:, t, bass.ds(g * 4, 4), 0:MV], bank[4 + t][:, :].rearrange("p (h d) -> p h d", d=MV))

                        def o_rows(act, g, t):
                            return act.activation(og[:, t, bass.ds(g * 4, 4), :], bank[4 + t][:, :].rearrange("p (h d) -> p h d", d=MV), ACT.Sigmoid)
                        stage, ready = normalise(3)
                        stages = [{"sync": bias_load}, inverse_root(), stage]
                        stages.append(dense("mg", [[[(k * P, a_tiles[k]) for k in range(KT)]]], gate_rows, tile_ready=ready))
                        b_a, b_d, b_p, b_st, b_pool = act_step.n, dve_step.n, pe_step.n, rows_stored.n, pool_step.n

                        def gate_pool(pool):
                            pool.memset(v[:, :, :, MV:MV + 1], 1.0)

                        def gate_vector(dve):
                            dve.memset(one[:, :], 1.0)
                            dve.wait_ge(inputs_in[0].sem, b_in + 32)
                            dve.drain()
                            dve.tensor_scalar(ig[:, :], ig[:, :], bias[:, 0:1], None, ALU.add)
                            dve.tensor_scalar(lf[:, :], lf[:, :], bias[:, 1:2], None, ALU.add)
                            dve.drain()
                            log_sigmoid(None, dve, lf[:, :], t1[:, :], t2[:, :], b_a, b_d, "dve")
                            dve.tensor_tensor_scan(fsum[:, :], one[:, :], lf[:, :], 0.0, ALU.mult, ALU.add)
                            dve.drain()
                            dve.tensor_tensor(ig[:, :], ig[:, :], fsum[:, :], ALU.subtract)
                            dve.drain()
                            dve.tensor_tensor_scan(mrun[:, :], one[:, :], ig[:, :], 0.0, ALU.mult, ALU.max)
                            dve.drain()
                            dve.tensor_scalar(t2[:, :], mrun[:, :], -1.0, None, ALU.mult)
                            dve.tensor_tensor(t1[:, :], fsum[:, :], mrun[:, :], ALU.add)
                            dve.drain()
                            dve.engine_nop().then_inc(dve_step.sem, 1)

                        def gate_scalar(act):
                            log_sigmoid(act, None, lf[:, :], t1[:, :], t2[:, :], b_a, b_d, "act")
                            act.wait_ge(dve_step.sem, b_d + 2)
                            act.activation(t1[:, :], t1[:, :], ACT.Exp, scale=-1.0).then_inc(act_step.sem, 1)
                        stages.append({"gpsimd": gate_pool, "vector": gate_vector, "scalar": gate_scalar})
                        act_step.n += 2
                        dve_step.n += 2
                        stages.append(dense("mqk", two_chunks(a_tiles), copy_to(qk)))

                        def turn_tensor(pe):
                            pe.wait_ge(dve_step.sem, b_d + 2)
                            for t in range(TT):
                                pe.transpose(bank[4][:, t * MH:(t + 1) * MH], ig[:, t * P:(t + 1) * P], ident[0:MH, 0:MH])
                            pe.wait_ge(act_step.sem, b_a + 2)
                            for t in range(TT):
                                last = pe.transpose(bank[5][:, t * MH:(t + 1) * MH], t1[:, t * P:(t + 1) * P], ident[0:MH, 0:MH])
                            last.then_inc(pe_step.sem, 1)

                        def turn_vector(dve):
                            dve.wait_ge(pe_step.sem, b_p + 1)
                            dve.tensor_copy(a_col[:, :, :], bank[4][:, 0:TT * MH].rearrange("p (t h) -> p t h", h=MH))
                            dve.tensor_copy(e_col[:, :, :], bank[5][:, 0:TT * MH].rearrange("p (t h) -> p t h", h=MH)).then_inc(dve_step.sem, 1)

                        def row_store(sp):
                            sp.wait_ge(dve_step.sem, b_d + 2)
                            sp.dma_start(io["row_scratch"][0:MH, :], t2[:, :]).then_inc(rows_stored.sem, 16)
                        stages.append({"tensor": turn_tensor, "vector": turn_vector, "sync": row_store})
                        pe_step.n += 1
                        dve_step.n += 1
                        stages.append(dense_rows("mv", evac_dve=v_rows))
                        stages.append(dense_rows("mo", evac_act=o_rows))
                        rows_stored.n += 16
                        stages.append({"sync": lambda sp: sp.wait_ge(rows_stored.sem, b_st + 16)})
                        run(*stages)
                    with ExitStack() as tmp:
                        dens = [sb(tmp, f"ml_den{r}", [P, 1]) for r in range(2)]

                        def take(dve, c, e, i, out):
                            den = dens[i % 2]
                            dve.scalar_tensor_tensor(den[:, :], out[:, MV:MV + 1], -1.0, e_col[:, i, bass.ds(c * 2 + e, 1)], ALU.mult, ALU.max)
                            dve.drain()
                            dve.tensor_tensor(den[:, :], out[:, MV:MV + 1], den[:, :], ALU.max)
                            dve.drain()
                            dve.reciprocal(den[:, :], den[:, :])
                            dve.drain()
                            return dve.tensor_scalar(h[:, i, bass.ds(c * 2 + e, 1), :], out[:, None, 0:MV], den[:, :], None, ALU.mult)
                        wts = [sb(tmp, f"ml_wts{e}", [P, TT, S]) for e in range(2)]
                        linear_attention("ml", MH, MK, qk[:, 0:4, :], qk[:, 4:8, :],
                                         lambda c, e, j: v[:, j, bass.ds(c * 2 + e, 1), :], MV + 1, float(MK) ** -0.5, take, wts,
                                         gates=(io["row_scratch"], a_col))
                    head_norm("ml", h, MH, og, qk[:, :, :].rearrange("p (t n) (m d) -> p t (n m) d", t=TT, d=MV))
                to_features(lambda t, k: h[:, t, k, :], KT, a_hi, a_lo, weight=12)
            post_norm_dense("mout", 5, a_tiles)

        def post_norm_dense(name, vec, xs):
            with ExitStack() as ctx:
                y = sb(ctx, f"{name}_y", [P, KT, S])
                sq_act, sq_dve = sums_on_the_way(y)
                stages = [dense(name, two_chunks(xs), copy_to(y), sq_dve, none, sq_act)]
                squared.n += KT
                summed.n += KT
                stages += [inverse_root(), update(vec, src=y)]
                run(*stages)

        def ffn(l):
            with ExitStack() as ctx:
                y = sb(ctx, f"ffn{l}_y", [P, KT, S])
                h_hi = sb(ctx, f"ffn{l}_hi", [P, KT, S], F32R)
                h_lo = sb(ctx, f"ffn{l}_lo", [P, KT, S], F32R)
                u = [sb(ctx, f"ffn{l}_u{r}", [P, 2, S + 2]) for r in range(2)]
                z = [sb(ctx, f"ffn{l}_z{r}", [P, 2, S]) for r in range(2)]
                h_tiles = [(h_hi[:, k, :], h_lo[:, k, :]) for k in range(KT)]
                b_pool = pool_step.n

                def margins(pool):
                    for r in range(2):
                        pool.memset(u[r][:, :, 0:2], 0.0).then_inc(pool_step.sem, 1)
                pool_step.n += 2
                stage, ready = normalise(7 + l)
                stages = [{"gpsimd": margins, "vector": lambda dve: dve.wait_ge(pool_step.sem, b_pool + 2)}, inverse_root(), stage]
                for g, (f0, n) in enumerate(FG):
                    def tap(j, b, c, f0=f0):
                        return conv[:, 2 * l + j // 2, bass.ds(b + (44 * (j % 2) + FT * c + f0), 1)]

                    def early_act(act, b, slot, m):
                        act.wait_ge(products_done.sem, m["prod"] + b + 1)
                        act.wait_ge(part_used.sem, m["pused"] + 2 * b - 2)
                        for c in range(2):
                            ins = act.activation(u[slot][:, c, 2:S + 2], bank[2 * slot + c][:, :], ACT.Copy)
                        ins.then_inc(evacuated.sem, 1)

                    def late_act(act, b, slot, m):
                        act.wait_ge(part_used.sem, m["pused"] + 2 * b + 1)
                        act.activation(z[slot][:, 0, :], z[slot][:, 0, :], ACT.Gelu_apprx_tanh).then_inc(gelu_ready.sem, 1)
                        act.wait_ge(hid_ready.sem, m["hid"] + 2 * b + 1)
                        act.activation(h_hi[:, bass.ds(b, 1), :], z[slot][:, 0:1, :], ACT.Copy).then_inc(part_ready.sem, 1)

                    def early_dve(dve, b, slot, m, tap=tap):
                        dve.wait_ge(evacuated.sem, m["evac"] + b + 1)
                        for c in range(2):
                            dve.tensor_scalar(z[slot][:, c, :], u[slot][:, c, 2:S + 2], tap(2, b, c), tap(3, b, c), ALU.mult, ALU.add)
                        dve.drain()
                        for c in range(2):
                            dve.scalar_tensor_tensor(z[slot][:, c, :], u[slot][:, c, 1:S + 1], tap(1, b, c), z[slot][:, c, :], ALU.mult, ALU.add)
                        dve.drain()
                        for c in range(2):
                            dve.scalar_tensor_tensor(z[slot][:, c, :], u[slot][:, c, 0:S], tap(0, b, c), z[slot][:, c, :],
                                                     ALU.mult, ALU.add).then_inc(part_used.sem, 1)

                    def late_dve(dve, b, slot, m):
                        dve.wait_ge(part_used.sem, m["pused"] + 2 * b + 2)
                        dve.wait_ge(gelu_ready.sem, m["gelu"] + b + 1)
                        dve.tensor_tensor(z[slot][:, 0, :], z[slot][:, 0, :], z[slot][:, 1, :], ALU.mult).then_inc(hid_ready.sem, 1)
                        dve.wait_ge(hid_ready.sem, m["hid"] + 2 * b + 1)
                        dve.wait_ge(part_ready.sem, m["part"] + b + 1)
                        dve.tensor_tensor(h_lo[:, bass.ds(b, 1), :], z[slot][:, 0:1, :], h_hi[:, bass.ds(b, 1), :].bitcast(F32),
                                          ALU.subtract).then_inc(hid_ready.sem, 1)
                    b_hid = hid_ready.n
                    stages.append(dense(f"fu{l}{g}", two_chunks(a_tiles), early_dve, late_dve, early_act, late_act,
                                        tile_ready=ready if g == 0 else None))
                    part_used.n += 2 * n
                    hid_ready.n += 2 * n
                    part_ready.n += n
                    gelu_ready.n += n
                    final = g == len(FG) - 1
                    sq_act, sq_dve = sums_on_the_way(y) if final else (none, none)
                    stages.append(dense(f"fd{l}{g}", two_chunks(h_tiles[:n]), copy_to(y) if g == 0 else add_to(y), sq_dve, none, sq_act,
                                        tile_ready=(lambda b_hid: lambda k: (hid_ready.sem, b_hid + 2 * k + 2))(b_hid)))
                    if final:
                        squared.n += KT
                        summed.n += KT
                stages += [inverse_root(), update(9 + l, src=y, with_sums=l == 0)]
                run(*stages)

        def fox():
            with ExitStack() as ctx:
                g = sb(ctx, "fx_g", [P, TT, FH * FD])
                with ExitStack() as inner:
                    kT = sb(inner, "fx_k", [P, 8, S])
                    qT = sb(inner, "fx_q", [P, 8, S])
                    v = sb(inner, "fx_v", [P, TT, FH * FD])
                    parts = sb(inner, "fx_parts", [P, S], BF16)
                    sel = sb(inner, "fx_sel", [P, FH * P], BF16)
                    with ExitStack() as tmp:
                        bias = sb(tmp, "fx_bias", [FH, 1])
                        lf, t1, t2, one = (sb(tmp, f"fx_{n}", [FH, S]) for n in ("lf", "t1", "t2", "one"))
                        b_in = inputs_in[0].n
                        inputs_in[0].n += 16

                        def bias_load(sp):
                            sp.dma_start(bias[:, :], io["kv_b_f_2"].rearrange("(h a) -> h a", a=1)).then_inc(inputs_in[0].sem, 16)

                        def v_rows(dve, grp, t):
                            return dve.tensor_copy(v[:, t, bass.ds(grp * 512, 512)], bank[4 + t][:, :])

                        def f_rows(dve, b, slot, m):
                            dve.wait_ge(products_done.sem, m["prod"] + b + 1)
                            dve.tensor_copy(lf[:, :], bank[2 * slot][0:FH, :]).then_inc(evacuated.sem, 1)
                        stage, ready = normalise(11)
                        stages = [{"sync": bias_load}, inverse_root(), stage]
                        stages.append(dense("ff", [[[(k * P, a_tiles[k]) for k in range(KT)]]], f_rows, tile_ready=ready))
                        b_a, b_d, b_pool = act_step.n, dve_step.n, pool_step.n

                        def gate_pool(pool):
                            pool.memset(parts[:, :], 0.0).then_inc(pool_step.sem, 1)
                            pool.memset(sel[:, :], 0.0).then_inc(pool_step.sem, 1)

                        def gate_vector(dve):
                            dve.memset(one[:, :], 1.0)
                            dve.wait_ge(inputs_in[0].sem, b_in + 16)
                            dve.drain()
                            dve.tensor_scalar(lf[:, :], lf[:, :], bias[:, 0:1], None, ALU.add)
                            dve.drain()
                            log_sigmoid(None, dve, lf[:, :], t1[:, :], t2[:, :], b_a, b_d, "dve")
                            dve.tensor_tensor_scan(t2[:, :], one[:, :], lf[:, :], 0.0, ALU.mult, ALU.add)
                            dve.drain()
                            dve.tensor_scalar(t1[:, :], t2[:, :], -1.0, None, ALU.mult)
                            dve.wait_ge(pool_step.sem, b_pool + 2)
                            dve.drain()
                            for j in range(3):
                                rows = slice(32 * j, 32 * j + FH)
                                dve.tensor_copy(parts[rows, :], t1[:, :])
                                dve.tensor_copy(sel[rows, :].rearrange("p (h q) -> p h q", q=P), ident[0:FH, 0:FH, None].broadcast_to([FH, FH, P]))
                                dve.drain()
                                if j < 2:
                                    dve.tensor_copy(t2[:, :], parts[rows, :])
                                    dve.drain()
                                    dve.tensor_tensor(t1[:, :], t1[:, :], t2[:, :], ALU.subtract)
                                    dve.drain()

                        def gate_scalar(act):
                            log_sigmoid(act, None, lf[:, :], t1[:, :], t2[:, :], b_a, b_d, "act")
                        stages.append({"gpsimd": gate_pool, "vector": gate_vector, "scalar": gate_scalar})
                        act_step.n += 1
                        dve_step.n += 1
                        pool_step.n += 2
                        stages.append(dense("fk", two_chunks(a_tiles), copy_to(kT)))
                        stages.append(dense_rows("fv", evac_dve=v_rows))

                        def g_rows(act, grp, t):
                            return act.activation(g[:, t, bass.ds(grp * 512, 512)], bank[4 + t][:, :], ACT.Sigmoid)
                        stage, ready = normalise(4)
                        stages.append(stage)
                        stages.append(dense("fq", two_chunks(a_tiles), copy_to(qT, float(FD) ** -0.5), tile_ready=ready))
                        stages.append(dense_rows("fg", evac_act=g_rows))
                        run(*stages)

                    def finish_unit(dve, c, p, e, i, out, inv_sum):
                        dst = g[:, i, bass.ds(c * (2 * P) + p * P + e * FD, FD)]
                        return dve.scalar_tensor_tensor(dst, out, inv_sum, dst, ALU.mult, ALU.mult)
                    attention("fox", FH // 2, qT, lambda c, p: kT[:, bass.ds(c * 2 + p, 1), :],
                              lambda c, p: v[:, :, bass.ds(c * (2 * P) + p * P, P)], False, (a_hi, a_lo), finish_unit, key_bias=(sel, parts))
                to_features(lambda t, k: g[:, t, k * P:(k + 1) * P], KT, a_hi, a_lo)
            post_norm_dense("fout", 6, a_tiles)

        def store():
            with ExitStack() as ctx:
                rows = sb(ctx, "out_rows", [P, TT, D])
                b_t, b_o = turned.n, turned_out.n
                with nc.Block() as block:
                    @block.tensor
                    def _(pe):
                        for t in range(TT):
                            for h in range(2):
                                n = 2 * t + h
                                if n >= 4:
                                    pe.wait_ge(turned_out.sem, b_o + n - 3)
                                for k in range(4):
                                    last = pe.transpose(bank[n % 4][:, k * P:(k + 1) * P], xT[:, 4 * h + k, t * P:(t + 1) * P], ident)
                                last.then_inc(turned.sem, 1)

                    @block.vector
                    def _(dve):
                        for n in range(2 * TT):
                            dve.wait_ge(turned.sem, b_t + n + 1)
                            dve.tensor_copy(rows[:, n // 2, (n % 2) * 512:(n % 2 + 1) * 512], bank[n % 4][:, :]).then_inc(turned_out.sem, 1)

                    @block.sync
                    def _(sp):
                        for t in range(TT):
                            sp.wait_ge(turned_out.sem, b_o + 2 * t + 2)
                            sp.dma_start(io["out"][0, t * P:(t + 1) * P, :], rows[:, t, :]).then_inc(stored.sem, 16)
                        sp.wait_ge(stored.sem, 16 * TT)

        setup()
        first_block()
        mlstm()
        ffn(0)
        fox()
        ffn(1)
        store()


_INS = ["x", "positions", "norm_mix", "w_in", "cmp_pos_k", "cmp_pos_v", "cmp_k_w1", "cmp_k_w2", "cmp_v_w1", "cmp_v_w2",
        "w_proj_a", "w_proj_b", "w_out", "norm_mlp", "w_up", "w_down", "norm_final", "norm_mix_pre_2", "norm_mix_post_2",
        "norm_ffn_pre_2", "norm_ffn_post_2", "mlstm_w_in_2", "mlstm_b_gate_2", "mlstm_norm_2", "mlstm_w_out_2", "kv_norm_2",
        "kv_w_2", "kv_b_f_2", "fox_w_qg_2", "fox_w_out_2", "ffn_w_up_2", "ffn_conv_w_2", "ffn_conv_b_2", "ffn_w_down_2"]


def kernel(**inputs):
    import concourse.bacc as _bacc
    from concourse.bass_utils import run_bass_kernel_spmd as _run

    nc = _bacc.Bacc("TRN2", target_bir_lowering=False, num_devices=1)
    packed, at, decay = shape_constants()
    arrays, io = {}, {}

    def give(name, a):
        arrays[f"in_{name}"] = a
        io[name] = nc.dram_tensor(f"in_{name}", a.shape, mybir.dt.from_np(a.dtype), kind="ExternalInput").ap()

    for name in _INS:
        give(name, np.ascontiguousarray(inputs[name]))
    give("const", packed)
    give("decay", decay)
    io["row_scratch"] = nc.dram_tensor("row_scratch", (FH, S), F32, kind="Internal").ap()
    io["out"] = nc.dram_tensor("out_x", (1, S, D), F32, kind="ExternalOutput").ap()
    build(nc, io, at)
    r = _run(nc, [arrays], core_ids=[0])
    return r.results[0]["out_x"]
```

```python
from contextlib import ExitStack

import numpy as np

import concourse.bass as bass
from concourse import mybir

F32, F32R = mybir.dt.float32, mybir.dt.float32r
BF16, I32 = mybir.dt.bfloat16, mybir.dt.int32
ACT = mybir.ActivationFunctionType
ALU = mybir.AluOpType
AX_X = mybir.AxisListType.X

P = 128
S = 512
D = 1024
KT = D // P
TT = S // P
SLOT = KT * 256
EPS = 1e-6
NEG = -1e30

HD, HQ, KV = 64, 8, 2
RH, RD = 4, 128
CB, CS, CH = 32, 16, 256
NC = (S - CB) // CS + 1
MLP_H = 4 * D
COLS = np.cumsum([0, HQ * HD] + [KV * HD] * 6 + [3 * HQ] + [RH * RD] * 4 + [D, D]).tolist()
(C_Q, C_KC, C_VC, C_KS, C_VS, C_KW, C_VW, C_G, C_RQ, C_RK, C_RV, C_RG, C_GA, C_GB) = COLS[:14]
GATES = 3 * HQ
MH, MK, MV = 8, 64, 128
FH, FD = 16, 64
FF = 2816
FT = FF // P

PI = float(np.pi)
TWO_PI_HI = 6.28125
TWO_PI_LO = 2 * np.pi - TWO_PI_HI
ROUND = 12582912.0
SIN_MAX = 3.1415925

VECS = ["norm_mix", "norm_mlp", "norm_final", "norm_mix_pre_2", "norm_mix_post_2",
        "norm_ffn_pre_2", "norm_ffn_post_2", "kv_norm_2", "mlstm_norm_2"]

GAINS = 13 * KT


class Tally:

    def __init__(self, sem):
        self.sem = sem
        self.n = 0


def shape_constants():
    p = np.arange(P)
    c = {}
    c["ident"] = np.eye(P)
    c["causal_bias"] = np.where(p[None, :] <= p[:, None], 0.0, NEG)
    c["causal_keep"] = np.where(p[:, None] <= p[None, :], 1.0, 0.0)
    half, rot = 8, 16
    d = p % HD
    partner = np.where(d < half, p + half, np.where(d < rot, p - half, p))
    c["swap_nsa"] = (p[:, None] == partner[None, :])
    c["swap_ret"] = (p[:, None] == ((p + RD // 2) % RD)[None, :])
    inv = np.exp(np.float32(-np.log(500000.0)) * np.arange(half, dtype=np.float32) * np.float32(2.0) / np.float32(rot))
    invr = np.exp(np.float32(-np.log(10000.0)) * np.arange(RD // 2, dtype=np.float32) * np.float32(2.0) / np.float32(RD))
    angles = np.zeros((P, 4))
    angles[:, 0] = np.where(d < rot, inv[d % half], 0.0)
    angles[:, 1] = np.where(d < half, -1.0, 1.0)
    angles[:, 2] = invr[p % (RD // 2)]
    angles[:, 3] = np.where(p < RD // 2, -1.0, 1.0)
    c["angles"] = angles
    t = p[:, None] + P * np.arange(TT)[None, :]
    end = CS * np.arange(CB) + CB - 1
    ok = (end[None, None, :] <= t[:, :, None]) & (np.arange(CB) < NC)[None, None, :]
    c["cmp_bias"] = np.where(ok, 0.0, NEG).reshape(P, TT * CB)
    c["cmp_any"] = ok.any(-1)
    packed = np.concatenate([np.asarray(v, np.float32) for v in c.values()], 1)
    at, off = {}, 0
    for k, v in c.items():
        at[k] = (off, off + v.shape[1])
        off += v.shape[1]
    log_g = np.log(1.0 - np.exp2(-5.0 - np.arange(RH)))
    rel = np.arange(S)[None, :] - p[:, None]
    decay = np.where(rel[:, None, :] >= 0, np.exp(log_g[None, :, None] * np.maximum(rel, 0)[:, None, :]), 0.0)
    return packed, at, np.ascontiguousarray(decay.astype(np.float32))


class Weights:

    def __init__(self, blocks, forms):
        self.blocks = blocks
        self.forms = forms

    def form(self, b):
        return self.forms[b % len(self.forms)]


def build(nc, io, at):
    top = ExitStack()
    with top:
        def sb(ctx, name, shape, dt=F32):
            return ctx.enter_context(nc.sbuf_tensor(name, shape, dt))

        def tally(name):
            return Tally(top.enter_context(nc.semaphore(name)))

        raw = [sb(top, f"w_raw{r}", [P, SLOT]) for r in range(2)]
        w_hi = [sb(top, f"w_hi{r}", [P, SLOT], F32R) for r in range(2)]
        w_lo = [sb(top, f"w_lo{r}", [P, SLOT], F32R) for r in range(2)]
        xT = sb(top, "xT", [P, KT, S])
        a_hi = sb(top, "a_hi", [P, KT, S], F32R)
        a_lo = sb(top, "a_lo", [P, KT, S], F32R)
        width = io["const"].shape[1]
        const = sb(top, "const_sb", [P, width])
        ident_b = sb(top, "ident_b", [P, P], BF16)
        bias_b = sb(top, "bias_b", [P, P], BF16)
        mean_of = sb(top, "mean_of", [P, P])
        inv_col = sb(top, "inv_col", [P, TT])
        sq = [sb(top, f"sq{r}", [P, S]) for r in range(2)]
        total = sb(top, "total", [P, S])
        inv = sb(top, "inv", [P, S])
        y_part = [sb(top, f"y_part{r}", [P, S]) for r in range(2)]
        gains = sb(top, "gains", [P, GAINS])
        conv = sb(top, "conv", [P, 4, 88])
        bank = [top.enter_context(nc.psum_tensor(f"bank{i}", [P, 512], F32)) for i in range(8)]

        def cst(name):
            return const[:, at[name][0]:at[name][1]]

        ident = cst("ident")

        raw_loaded = [tally(f"raw_loaded{r}") for r in range(2)]
        hi_ready, lo_ready = tally("hi_ready"), tally("lo_ready")
        products_done, evacuated = tally("products_done"), tally("evacuated")
        rows_done, rows_out = tally("rows_done"), tally("rows_out")
        part_ready, part_used = tally("part_ready"), tally("part_used")
        gelu_ready = tally("gelu_ready")
        hid_ready = tally("hid_ready")
        inputs_in = [tally(f"inputs_in{i}") for i in range(4)]
        squared, summed, mean_ready, mixed = (tally(n) for n in ("squared", "summed", "mean_ready", "mixed"))
        positions_in, high_staged, den_ready = (tally(n) for n in ("positions_in", "high_staged", "den_ready"))
        scaled, updated, pool_updated, split_hi_done, split_lo_done = (tally(n) for n in ("scaled", "updated", "pool_updated", "split_hi_done", "split_lo_done"))
        turned, turned_out, turned_hi = tally("turned"), tally("turned_out"), tally("turned_hi")
        keys_staged = tally("keys_staged")
        staged, scores_ready, max_ready, probs_ready = (tally(n) for n in ("staged", "scores_ready", "max_ready", "probs_ready"))
        probs_turned, probs_copied, out_ready, out_done = (tally(n) for n in ("probs_turned", "probs_copied", "out_ready", "out_done"))
        bias_row_in = [tally(f"bias_row_in{r}") for r in range(2)]
        bias_row_used = tally("bias_row_used")
        logits_ready = tally("logits_ready")
        gap_ready, decay_ready, kept, weighted = (tally(n) for n in ("gap_ready", "decay_ready", "kept", "weighted"))
        act_step, dve_step, pe_step, pool_step = (tally(n) for n in ("act_step", "dve_step", "pe_step", "pool_step"))
        rows_stored = tally("rows_stored")
        stored = tally("stored")
        POOL_TILES = 3
        LEAD = 32
        led = [products_done, evacuated, rows_done, rows_out, part_ready, part_used, hi_ready, lo_ready, scores_ready,
               max_ready, probs_ready, probs_turned, probs_copied, out_ready, out_done, staged, keys_staged, bias_row_used,
               logits_ready, gap_ready, decay_ready, kept, weighted, gelu_ready, hid_ready,
               squared, summed, mixed, high_staged, den_ready]

        stream = {"slot": 0}

        def slot_view(ring, r, form):
            tiles, width, _ = form
            return ring[r][:, 0:tiles * width].rearrange("p (t n) -> p t n", t=tiles)

        def load(eng, spec, b, slot, q):
            dst = slot_view(raw, slot, spec.forms[q])
            for col, ncol, src, *rows in spec.forms[q][2]:
                eng.dma_start(dst[rows[0] if rows else slice(0, P), :, col:col + ncol], src(b)).then_inc(raw_loaded[slot].sem, 16)

        def prefetch(eng, spec):
            for b in range(min(2, spec.blocks)):
                slot = (stream["slot"] + b) % 2
                load(eng, spec, b, slot, b % len(spec.forms))

        def loads(eng, spec, nxt, m):
            def one(b, q):
                eng.wait_ge(lo_ready.sem, m["lo"] + b - 1)
                load(eng, spec, b, (m["slot"] + q) % 2, q % len(spec.forms))
            if spec.blocks > 4:
                with eng.Fori(1, spec.blocks // 2) as i:
                    one(i * 2, 0)
                    one(i * 2 + 1, 1)
            else:
                for b in range(2, spec.blocks):
                    one(b, b % 2)
            if nxt is not None:
                for b in range(min(2, nxt.blocks)):
                    e = spec.blocks + b
                    eng.wait_ge(lo_ready.sem, m["lo"] + e - 1)
                    load(eng, nxt, b, (m["slot"] + e) % 2, b % len(nxt.forms))

        def hi_part(act, spec, nxt, b, q, m):
            beyond = isinstance(b, int) and b == spec.blocks
            if beyond and nxt is None:
                return
            slot, form = (m["slot"] + q) % 2, (nxt.forms[0] if beyond else spec.forms[q % len(spec.forms)])
            n = form[0] * form[1]
            before = m["raw"][slot]
            if beyond:
                before += sum(16 * len(spec.form(x)[2]) for x in range(q, spec.blocks, 2))
                turn = 1
            else:
                turn = b // 2 + 1 if isinstance(b, int) else m["i"] + 2
            act.wait_ge(raw_loaded[slot].sem, before + 16 * len(form[2]) * turn)
            act.wait_ge(products_done.sem, m["prod"] + b - 1)
            act.activation(w_hi[slot][:, 0:n], raw[slot][:, 0:n], ACT.Copy).then_inc(hi_ready.sem, 1)

        def lo_part(dve, spec, nxt, b, q, m):
            beyond = isinstance(b, int) and b == spec.blocks
            if beyond and nxt is None:
                return
            slot, form = (m["slot"] + q) % 2, (nxt.forms[0] if beyond else spec.forms[q % len(spec.forms)])
            n = form[0] * form[1]
            dve.wait_ge(hi_ready.sem, m["hi"] + b + 1)
            dve.tensor_tensor(w_lo[slot][:, 0:n], raw[slot][:, 0:n], w_hi[slot][:, 0:n].bitcast(F32),
                              ALU.subtract).then_inc(lo_ready.sem, 1)

        def marks():
            return {"slot": stream["slot"], "raw": [t.n for t in raw_loaded], "hi": hi_ready.n, "lo": lo_ready.n,
                    "prod": products_done.n, "evac": evacuated.n, "rows": rows_done.n, "rowsout": rows_out.n,
                    "part": part_ready.n, "pused": part_used.n, "gelu": gelu_ready.n, "hid": hid_ready.n,
                    "sq": squared.n, "sum": summed.n, "mixed": mixed.n, "i": 0}

        def finish(spec):
            for b in range(spec.blocks):
                slot = (stream["slot"] + b) % 2
                raw_loaded[slot].n += 16 * len(spec.form(b)[2])
            stream["slot"] = (stream["slot"] + spec.blocks) % 2
            for t in (hi_ready, lo_ready, products_done):
                t.n += spec.blocks

        def none(eng, b, slot, m):
            pass

        def split_between(eng, spec, nxt, m, part, early, late):
            part(eng, spec, nxt, 1, 1, m)
            n, first = spec.blocks, 0
            slot = lambda q: (m["slot"] + q) % 2
            if n > 4:
                with eng.Fori(0, n // 2 - 1) as i:
                    m["i"] = i
                    for q in range(2):
                        early(eng, i * 2 + q, slot(q), m)
                        part(eng, spec, nxt, i * 2 + (q + 2), q, m)
                        late(eng, i * 2 + q, slot(q), m)
                first = n - 2
            for b in range(first, n):
                early(eng, b, slot(b % 2), m)
                if n > 1 and b + 2 <= n:
                    part(eng, spec, nxt, b + 2, b % 2, m)
                late(eng, b, slot(b % 2), m)

        def three_products(pe, out, w, x, first, last):
            pe.matmul(out, w[0], x[0], start=first, stop=False)
            pe.matmul(out, w[0], x[1], start=False, stop=False)
            return pe.matmul(out, w[1], x[0], start=False, stop=last)

        def run(*stages):
            uses = {e for s in stages for e in s}
            with nc.Block(no_gpsimd_drain="gpsimd" not in uses) as block:
                if "sync" in uses:
                    @block.sync
                    def _(sp):
                        for s in stages:
                            if "sync" in s:
                                s["sync"](sp)

                if "scalar" in uses:
                    @block.scalar
                    def _(act):
                        for s in stages:
                            if "scalar" in s:
                                s["scalar"](act)

                if "vector" in uses:
                    @block.vector
                    def _(dve):
                        for s in stages:
                            if "vector" in s:
                                s["vector"](dve)

                if "gpsimd" in uses:
                    @block.gpsimd
                    def _(pool):
                        for s in stages:
                            if "gpsimd" in s:
                                s["gpsimd"](pool)

                if "tensor" in uses:
                    @block.tensor
                    def _(pe):
                        for s in stages:
                            if "tensor" in s:
                                s["tensor"](pe)

        def dense(name, chunks, early_dve=none, late_dve=none, early_act=none, late_act=none, tile_ready=None):
            spec, nxt, m = specs[name], after(name), marks()

            def sync(sp):
                loads(sp, spec, nxt, m)

            def scalar(act):
                split_between(act, spec, nxt, m, hi_part, early_act, late_act)

            def vector(dve):
                split_between(dve, spec, nxt, m, lo_part, early_dve, late_dve)

            def tensor(pe):
                def use(b, q):
                    slot = (m["slot"] + q) % 2
                    pe.wait_ge(lo_ready.sem, m["lo"] + b + 1)
                    pe.wait_ge(evacuated.sem, m["evac"] + b - 1)
                    sets = chunks[q % len(chunks)]
                    terms = [(c, k) for c in range(len(sets)) for k in range(len(sets[c]))]
                    if tile_ready is not None and q == 0:
                        terms = [(c, k) for k in range(len(sets[0])) for c in range(len(sets))]
                    for c, k in terms:
                        if tile_ready is not None and q == 0 and c == 0:
                            pe.wait_ge(*tile_ready(k))
                        col, x = sets[c][k]
                        w = [ring[slot][:, col:col + P] for ring in (w_hi, w_lo)]
                        last = three_products(pe, bank[2 * slot + c][:, :], w, x, k == 0, k == len(sets[c]) - 1)
                    last.then_inc(products_done.sem, 1)
                if spec.blocks <= 2:
                    for b in range(spec.blocks):
                        use(b, b)
                else:
                    with pe.Fori(0, spec.blocks // 2) as i:
                        use(i * 2, 0)
                        use(i * 2 + 1, 1)
            finish(spec)
            evacuated.n += spec.blocks
            return {"sync": sync, "scalar": scalar, "vector": vector, "tensor": tensor}

        def dense_rows(name, evac_dve=None, evac_act=None):
            spec, nxt, m = specs[name], after(name), marks()
            tiles, width, _ = spec.forms[0]

            def rows(fn):
                def early(eng, b, slot, m):
                    if fn is None or slot == m["slot"]:
                        return
                    g = (b - 1) // 2 if isinstance(b, int) else m["i"]
                    for t in range(TT):
                        eng.wait_ge(rows_done.sem, m["rows"] + g * TT + (t + 1))
                        fn(eng, g, t).then_inc(rows_out.sem, 1)
                return early

            def sync(sp):
                loads(sp, spec, nxt, m)

            def scalar(act):
                split_between(act, spec, nxt, m, hi_part, rows(evac_act), none)

            def vector(dve):
                split_between(dve, spec, nxt, m, lo_part, rows(evac_dve), none)

            def tensor(pe):
                m["i"] = 0

                def use(b, q):
                    slot = (m["slot"] + q) % 2
                    pe.wait_ge(lo_ready.sem, m["lo"] + b + 1)
                    g = b // 2 if isinstance(b, int) else m["i"]
                    for t in range(TT):
                        if q == 0:
                            pe.wait_ge(rows_out.sem, m["rowsout"] + g * TT + (t + 1 - TT))
                        for k in range(tiles):
                            x = [a[:, q * tiles + k, t * P:(t + 1) * P] for a in (a_hi, a_lo)]
                            w = [ring[slot][:, k * width:(k + 1) * width] for ring in (w_hi, w_lo)]
                            last = three_products(pe, bank[4 + t][:, 0:width], x, w, q == 0 and k == 0,
                                                  q == 1 and k == tiles - 1)
                        if q == 1:
                            last.then_inc(rows_done.sem, 1)
                    if q == 0:
                        last.then_inc(products_done.sem, 1)
                    else:
                        pe.drain().then_inc(products_done.sem, 1)
                if spec.blocks == 2:
                    use(0, 0)
                    use(1, 1)
                else:
                    with pe.Fori(0, spec.blocks // 2) as i:
                        m["i"] = i
                        use(i * 2, 0)
                        use(i * 2 + 1, 1)
            finish(spec)
            rows_done.n += TT * spec.blocks // 2
            rows_out.n += TT * spec.blocks // 2
            return {"sync": sync, "scalar": scalar, "vector": vector, "tensor": tensor}

        def view(w):
            return w.rearrange("(t p) n -> p t n", p=P)

        def cols(w, start, n=256, step=256, t0=0, t1=None):
            v = view(w)[:, t0:t1, :]
            return lambda b: v[:, :, bass.ds(b * step + start, n)]

        def plain(w, start, blocks, t0=0, tiles=KT):
            return Weights(blocks, [(tiles, 256, [(0, 256, cols(w, start, t0=t0, t1=t0 + tiles))])])

        def row_blocks(w, start, groups):
            forms = []
            for q in range(2):
                v = view(w)[:, q * KT // 2:(q + 1) * KT // 2, :]
                forms.append((KT // 2, 512, [(0, 512, (lambda v, q: lambda b: v[:, :, bass.ds((b - q) * 256 + start, 512)])(v, q))]))
            return Weights(2 * groups, forms)

        a_tiles = [(a_hi[:, k, :], a_lo[:, k, :]) for k in range(KT)]

        def two_chunks(xs):
            return [[[(k * 256 + c * P, x) for k, x in enumerate(xs)] for c in range(2)]]

        W_IN, W_IN2, KV_W = io["w_in"][0], io["mlstm_w_in_2"][0], io["kv_w_2"]
        v_in = view(W_IN)
        q_pieces = [(128 * j + 64 * g, 64, (lambda j, g: lambda b: v_in[:, :, bass.ds(b * 128 + (C_Q + 256 * g + 64 * j), 64)])(j, g))
                    for j in range(2) for g in range(2)]
        half = [v_in[:, q * 4:(q + 1) * 4, :] for q in range(2)]
        specs = {}
        specs["q"] = Weights(2, [(KT, 256, q_pieces)])
        specs["kcvc"] = Weights(2, [(KT, 256, [(0, 256, lambda b: v_in[:, :, C_KC:C_KC + 256])]),
                                    (KT, 256, [(0, 128, lambda b: v_in[:, :, C_KS:C_KS + 128]),
                                               (128, 128, lambda b: v_in[:, :, C_KW:C_KW + 128])])])
        specs["vg"] = Weights(2, [(4, 280, [(0, 128, (lambda q: lambda b: half[q][:, :, C_VS:C_VS + 128])(q)),
                                            (128, 152, (lambda q: lambda b: half[q][:, :, C_VW:C_VW + 152])(q))])
                                  for q in range(2)])
        specs["rqk"] = plain(W_IN, C_RQ, 4)
        specs["rvg"] = row_blocks(W_IN, C_RV, 2)
        v_proj_a = [io["w_proj_a"][0][256 * e:256 * e + 256, :].rearrange("(c d) n -> d c n", d=HD) for e in range(2)]
        specs["mix"] = Weights(16, [
            (KT, 256, [(0, 128, lambda b: v_in[:, :, bass.ds(b * 64 + C_GA, 128)]),
                       (128, 128, lambda b: v_in[:, :, bass.ds(b * 64 + C_GB, 128)])]),
            (4, 256, [(0, 128, (lambda e: lambda b: v_proj_a[e][:, :, bass.ds(b * 64 - 64, 128)])(e), slice(64 * e, 64 * e + 64))
                      for e in range(2)] + [
                      (128, 128, lambda b: view(io["w_proj_b"][0])[:, :, bass.ds(b * 64 - 64, 128)])])])
        specs["out1"] = plain(io["w_out"][0], 0, 4)
        order = ["q", "kcvc", "vg", "rqk", "rvg", "mix", "out1"]
        for g in range(4):
            specs[f"up{g}"] = plain(io["w_up"][0], g * D, 4)
            specs[f"down{g}"] = plain(io["w_down"][0], 0, 4, t0=g * KT)
            order += [f"up{g}", f"down{g}"]
        specs["mqk"] = plain(W_IN2, 0, 4)
        specs["mv"] = row_blocks(W_IN2, 1024, 2)
        specs["mo"] = row_blocks(W_IN2, 2048, 2)
        v_in2, v_kv = view(W_IN2), view(KV_W)
        specs["mg"] = Weights(1, [(KT, 128, [(0, 8, lambda b: v_in2[:, :, 3072:3080]), (8, 24, lambda b: v_in2[:, :, 0:24]),
                                             (32, 8, lambda b: v_in2[:, :, 3080:3088]), (40, 88, lambda b: v_in2[:, :, 24:112])])])
        specs["mout"] = plain(io["mlstm_w_out_2"][0], 0, 4)
        order += ["mg", "mqk", "mv", "mo", "mout"]
        FG = [(0, 8), (8, 8), (16, 6)]

        def ffn_specs(l):
            wu, wd = view(io["ffn_w_up_2"][l]), io["ffn_w_down_2"][l]
            for g, (f0, n) in enumerate(FG):
                specs[f"fu{l}{g}"] = Weights(n, [(KT, 256, [
                    (0, 128, (lambda f0: lambda b: wu[:, :, bass.ds(b * P + f0 * P, P)])(f0)),
                    (128, 128, (lambda f0: lambda b: wu[:, :, bass.ds(b * P + (FF + f0 * P), P)])(f0))])])
                specs[f"fd{l}{g}"] = plain(wd, 0, 4, t0=f0, tiles=n)
                order.extend([f"fu{l}{g}", f"fd{l}{g}"])

        ffn_specs(0)
        specs["fk"] = plain(KV_W, 0, 4)
        specs["fv"] = row_blocks(KV_W, D, 2)
        specs["ff"] = Weights(1, [(KT, 128, [(0, 16, lambda b: v_kv[:, :, 2048:2064]), (16, 112, lambda b: v_kv[:, :, 0:112])])])
        specs["fq"] = plain(io["fox_w_qg_2"][0], 0, 4)
        specs["fg"] = plain(io["fox_w_qg_2"][0], D, 4)
        specs["fout"] = plain(io["fox_w_out_2"][0], 0, 4)
        order += ["ff", "fk", "fv", "fq", "fg", "fout"]
        ffn_specs(1)

        def after(name):
            i = order.index(name)
            return specs[order[i + 1]] if i + 1 < len(order) else None

        def setup():
            with ExitStack() as ctx:
                x_rows = sb(ctx, "x_rows", [P, TT, D])
                gain_rows = sb(ctx, "gain_rows", [GAINS, P])
                conv_rows = sb(ctx, "conv_rows", [88, 4, P])
                with nc.Block() as block:
                    @block.sync
                    def _(sp):
                        sp.dma_start(x_rows[:, :, :], io["x"][0].rearrange("(t p) d -> p t d", p=P)).then_inc(inputs_in[0].sem, 16)
                        prefetch(sp, specs["q"])

                    @block.scalar
                    def _(act):
                        act.dma_start(const[:, :], io["const"]).then_inc(inputs_in[1].sem, 16)
                        row = 0
                        for name in VECS:
                            v = io[name]
                            n = v.shape[0] if len(v.shape) == 2 else 1
                            src = v.rearrange("l (t p) -> (l t) p", p=P) if len(v.shape) == 2 else v.rearrange("(t p) -> t p", p=P)
                            act.dma_start(gain_rows[row:row + n * KT, :], src).then_inc(inputs_in[2].sem, 16)
                            row += n * KT
                        for l in range(2):
                            w = io["ffn_conv_w_2"][l].rearrange("k (t p) -> (k t) p", p=P)
                            act.dma_start(conv_rows[:, 2 * l, :], w[0:88, :]).then_inc(inputs_in[3].sem, 16)
                            act.dma_start(conv_rows[0:44, 2 * l + 1, :], w[88:132, :]).then_inc(inputs_in[3].sem, 16)
                            act.dma_start(conv_rows[44:88, 2 * l + 1, :],
                                          io["ffn_conv_b_2"][l].rearrange("(t p) -> t p", p=P)).then_inc(inputs_in[3].sem, 16)
                        for k in range(KT):
                            act.wait_ge(turned_out.sem, k + 1)
                            if k >= 2:
                                act.wait_ge(summed.sem, LEAD + k - 1)
                            act.activation(sq[k % 2][:, :], xT[:, k, :], ACT.Square).then_inc(squared.sem, 1)
                        act.wait_ge(raw_loaded[0].sem, 16 * len(specs["q"].forms[0][2]))
                        act.activation(w_hi[0][:, :], raw[0][:, :], ACT.Copy).then_inc(hi_ready.sem, 1)

                    @block.gpsimd
                    def _(pool):
                        for t in led:
                            pool.sem_inc(t.sem, LEAD)
                        pool.memset(mean_of[:, :], 1.0 / D).then_inc(pool_step.sem, 1)

                    @block.tensor
                    def _(pe):
                        pe.wait_ge(inputs_in[0].sem, 16)
                        pe.wait_ge(inputs_in[1].sem, 16)
                        for k in range(KT):
                            if k >= 4:
                                pe.wait_ge(turned_out.sem, k - 3)
                            for t in range(TT):
                                last = pe.transpose(bank[k % 4][:, t * P:(t + 1) * P], x_rows[:, t, k * P:(k + 1) * P], ident)
                            last.then_inc(turned.sem, 1)
                        pe.wait_ge(inputs_in[2].sem, 16 * len(VECS))
                        pe.transpose(bank[4][:, 0:GAINS], gain_rows[:, :], ident[0:GAINS, 0:GAINS]).then_inc(turned.sem, 1)
                        pe.wait_ge(inputs_in[3].sem, 16 * 6)
                        for j in range(4):
                            last = pe.transpose(bank[5][:, j * 88:(j + 1) * 88], conv_rows[:, j, :], ident[0:88, 0:88])
                        last.then_inc(turned.sem, 1)

                    @block.vector
                    def _(dve):
                        dve.wait_ge(inputs_in[1].sem, 16)
                        dve.tensor_copy(ident_b[:, :], ident)
                        dve.tensor_copy(bias_b[:, :], cst("causal_bias"))
                        for k in range(KT):
                            dve.wait_ge(turned.sem, k + 1)
                            dve.tensor_copy(xT[:, k, :], bank[k % 4][:, :]).then_inc(turned_out.sem, 1)
                            if k >= 1:
                                add_square(dve, k - 1, LEAD, LEAD)
                        add_square(dve, KT - 1, LEAD, LEAD)
                        dve.wait_ge(turned.sem, KT + 1)
                        dve.tensor_copy(gains[:, :], bank[4][:, 0:GAINS])
                        dve.wait_ge(turned.sem, KT + 2)
                        dve.tensor_copy(conv[:, :, :], bank[5][:, 0:352].rearrange("p (a b) -> p a b", a=4))
                        dve.wait_ge(hi_ready.sem, LEAD + 1)
                        dve.tensor_tensor(w_lo[0][:, :], raw[0][:, :], w_hi[0][:, :].bitcast(F32), ALU.subtract).then_inc(lo_ready.sem, 1)
            turned.n += KT + 2
            turned_out.n += KT
            pool_step.n += 1
            for t, n in zip(inputs_in, (1, 1, len(VECS), 6)):
                t.n += 16 * n
            for t in led:
                t.n = LEAD
            squared.n += KT
            summed.n += KT

        def add_square(dve, k, b_sq, b_sum):
            dve.wait_ge(squared.sem, b_sq + k + 1)
            if k == 0:
                dve.tensor_copy(total[:, :], sq[0][:, :]).then_inc(summed.sem, 1)
            else:
                dve.wait_ge(summed.sem, b_sum + k)
                dve.tensor_tensor(total[:, :], total[:, :], sq[k % 2][:, :], ALU.add).then_inc(summed.sem, 1)

        def sums_on_the_way(src):
            def late_act(act, b, slot, m):
                act.wait_ge(evacuated.sem, m["evac"] + b + 1)
                for c in range(2):
                    k = 2 * b + c
                    if k >= 2:
                        act.wait_ge(summed.sem, m["sum"] + k - 1)
                    act.activation(sq[c][:, :], src[:, k, :], ACT.Square).then_inc(squared.sem, 1)

            def late_dve(dve, b, slot, m):
                for c in range(2):
                    add_square(dve, 2 * b + c, m["sq"], m["sum"])
            return late_act, late_dve

        def inverse_root():
            b_sum, b_mean = summed.n, mean_ready.n

            def tensor(pe):
                pe.wait_ge(summed.sem, b_sum)
                for t in range(TT):
                    last = pe.matmul(bank[7][:, t:t + 1], total[:, t * P:(t + 1) * P], mean_of[:, 0:1], start=True, stop=True)
                last.then_inc(mean_ready.sem, 1)
                pe.wait_ge(mean_ready.sem, b_mean + 3)
                for t in range(TT):
                    last = pe.matmul(bank[6][:, t * P:(t + 1) * P], inv_col[:, t:t + 1].broadcast_to([P, P]), ident, start=True, stop=True)
                last.then_inc(mean_ready.sem, 1)

            def scalar(act):
                act.wait_ge(mean_ready.sem, b_mean + 1)
                act.activation(inv_col[:, :], bank[7][:, 0:TT], ACT.Sqrt, bias=EPS).then_inc(mean_ready.sem, 1)

            def vector(dve):
                dve.wait_ge(mean_ready.sem, b_mean + 2)
                dve.reciprocal(inv_col[:, :], inv_col[:, :]).then_inc(mean_ready.sem, 1)
                dve.wait_ge(mean_ready.sem, b_mean + 4)
                dve.tensor_copy(inv[:, :], bank[6][:, :])
                dve.drain()
            mean_ready.n += 4
            return {"tensor": tensor, "scalar": scalar, "vector": vector}

        def inverse_root_of_mean():
            b_mean = mean_ready.n

            def scalar(act):
                act.wait_ge(mean_ready.sem, b_mean)
                act.activation(inv[:, :], bank[7][:, :], ACT.Sqrt, bias=EPS).then_inc(mean_ready.sem, 1)

            def vector(dve):
                dve.wait_ge(mean_ready.sem, b_mean + 1)
                dve.reciprocal(inv[:, :], inv[:, :])
                dve.drain()
            mean_ready.n += 1
            return {"scalar": scalar, "vector": vector}

        def gain(vec, k):
            return gains[:, vec * KT + k:vec * KT + k + 1]

        def normalise(vec):
            b_sc, b_hi, b_lo, b_pr = scaled.n, split_hi_done.n, split_lo_done.n, products_done.n

            def scalar(act):
                act.wait_ge(products_done.sem, b_pr)
                for k in range(KT):
                    act.wait_ge(scaled.sem, b_sc + k + 1)
                    act.activation(a_hi[:, k, :], y_part[k % 2][:, :], ACT.Copy).then_inc(split_hi_done.sem, 1)

            def vector(dve):
                def lo(k):
                    dve.wait_ge(split_hi_done.sem, b_hi + k + 1)
                    dve.tensor_tensor(a_lo[:, k, :], y_part[k % 2][:, :], a_hi[:, k, :].bitcast(F32),
                                      ALU.subtract).then_inc(split_lo_done.sem, 1)
                for k in range(KT):
                    if k >= 2:
                        dve.wait_ge(split_lo_done.sem, b_lo + k - 1)
                    dve.scalar_tensor_tensor(y_part[k % 2][:, :], xT[:, k, :], gain(vec, k), inv[:, :],
                                             ALU.mult, ALU.mult).then_inc(scaled.sem, 1)
                    if k >= 1:
                        lo(k - 1)
                lo(KT - 1)
            scaled.n += KT
            split_hi_done.n += KT
            split_lo_done.n += KT
            return {"scalar": scalar, "vector": vector}, lambda k: (split_lo_done.sem, b_lo + k + 1)

        def update(vec, src=None, with_mean=True):
            b_sc, b_up, b_sq, b_sum, b_pool, b_tiles = scaled.n, updated.n, squared.n, summed.n, pool_step.n, pool_updated.n
            ours = KT - (POOL_TILES if src is not None else 0)
            order = [(k, updated, b_up + k + 1) for k in range(ours)]
            for n, k in enumerate(range(ours, KT)):
                order.insert(3 * n + 2, (k, pool_updated, b_tiles + n + 1))

            def scalar(act):
                for n, (k, done, value) in enumerate(order):
                    act.wait_ge(done.sem, value)
                    if n >= 2:
                        act.wait_ge(summed.sem, b_sum + n - 1)
                    act.activation(sq[n % 2][:, :], xT[:, k, :], ACT.Square).then_inc(squared.sem, 1)

            def tensor(pe):
                for n in range(KT):
                    pe.wait_ge(squared.sem, b_sq + n + 1)
                    pe.matmul(bank[7][:, :], mean_of[:, :], sq[n % 2][:, :], start=n == 0,
                              stop=n == KT - 1).then_inc(mean_ready.sem if n == KT - 1 else summed.sem, 1)

            def gpsimd(pool):
                pool.wait_ge(summed.sem, b_sum)
                for k in range(ours, KT):
                    pool.tensor_scalar(src[:, k, :], src[:, k, :], gain(vec, k), None, ALU.mult).then_inc(pool_step.sem, 1)
                pool.wait_ge(scaled.sem, b_sc + 1)
                for n, k in enumerate(range(ours, KT)):
                    pool.wait_ge(pool_step.sem, b_pool + POOL_TILES + n)
                    pool.tensor_tensor(src[:, k, :], src[:, k, :], inv[:, :], ALU.mult).then_inc(pool_step.sem, 1)
                    pool.wait_ge(pool_step.sem, b_pool + POOL_TILES + n + 1)
                    pool.tensor_tensor(xT[:, k, :], xT[:, k, :], src[:, k, :], ALU.add).then_inc(pool_updated.sem, 1)

            def vector(dve):
                def add(k):
                    dve.wait_ge(scaled.sem, b_sc + k + 1)
                    dve.tensor_tensor(xT[:, k, :], xT[:, k, :], y_part[k % 2][:, :], ALU.add).then_inc(updated.sem, 1)
                for k in range(ours):
                    if src is None:
                        dve.scalar_tensor_tensor(xT[:, k, :], xT[:, k, :], gain(vec, k), inv[:, :],
                                                 ALU.mult, ALU.mult).then_inc(updated.sem, 1)
                        continue
                    if k >= 2:
                        dve.wait_ge(updated.sem, b_up + k - 1)
                    dve.scalar_tensor_tensor(y_part[k % 2][:, :], src[:, k, :], gain(vec, k), inv[:, :],
                                             ALU.mult, ALU.mult).then_inc(scaled.sem, 1)
                    if k >= 1:
                        add(k - 1)
                if src is not None:
                    add(ours - 1)
                dve.drain()
            updated.n += ours
            stage = {"vector": vector}
            if src is not None:
                scaled.n += ours
                pool_step.n += 2 * POOL_TILES
                pool_updated.n += POOL_TILES
                stage["gpsimd"] = gpsimd
            if with_mean:
                squared.n += KT
                summed.n += KT - 1
                mean_ready.n += 1
                stage.update(scalar=scalar, tensor=tensor)
            return stage

        def copy_to(dst, scale=None):
            def early(dve, b, slot, m):
                dve.wait_ge(products_done.sem, m["prod"] + b + 1)
                for c in range(2):
                    out, src = dst[:, bass.ds(b * 2 + c, 1), :], bank[2 * slot + c][:, None, :]
                    ins = dve.tensor_copy(out, src) if scale is None else dve.tensor_scalar(out, src, scale, None, ALU.mult)
                ins.then_inc(evacuated.sem, 1)
            return early

        def add_to(dst):
            def early(dve, b, slot, m):
                dve.wait_ge(products_done.sem, m["prod"] + b + 1)
                for c in range(2):
                    y = dst[:, bass.ds(b * 2 + c, 1), :]
                    ins = dve.tensor_tensor(y, bank[2 * slot + c][:, None, :], y, ALU.add)
                ins.then_inc(evacuated.sem, 1)
            return early

        def positions_load(pos_i):
            def sync(sp):
                sp.dma_start(pos_i[:, :], io["positions"][0:1, :].broadcast_to([P, S])).then_inc(positions_in.sem, 16)
            return {"sync": sync}

        def rope_tables(work, pos_i, freq, cos, sin):
            ang, turns, rest = work
            a0 = at["angles"][0]
            b_a, b_d = act_step.n, dve_step.n

            def vector(dve):
                dve.wait_ge(positions_in.sem, 16)
                if b_a:
                    dve.wait_ge(act_step.sem, b_a)
                dve.tensor_copy(ang[:, :], pos_i[:, :])
                dve.drain()
                dve.tensor_scalar(ang[:, :], ang[:, :], const[:, a0 + freq:a0 + freq + 1], None, ALU.mult)
                dve.drain()
                dve.tensor_scalar(turns[:, :], ang[:, :], 1.0 / (2 * PI), ROUND, ALU.mult, ALU.add)
                dve.drain()
                dve.tensor_scalar(turns[:, :], turns[:, :], ROUND, None, ALU.subtract)
                dve.drain()
                dve.scalar_tensor_tensor(rest[:, :], turns[:, :], -TWO_PI_HI, ang[:, :], ALU.mult, ALU.add)
                dve.drain()
                dve.scalar_tensor_tensor(rest[:, :], turns[:, :], -TWO_PI_LO, rest[:, :], ALU.mult, ALU.add)
                dve.drain()
                dve.tensor_scalar(rest[:, :], rest[:, :], SIN_MAX, -SIN_MAX, ALU.min, ALU.max).then_inc(dve_step.sem, 1)
                dve.wait_ge(dve_step.sem, b_d + 1)
                dve.scalar_tensor_tensor(turns[:, :], rest[:, :], -1.0, rest[:, :], ALU.mult, ALU.min)
                dve.drain()
                dve.tensor_scalar(turns[:, :], turns[:, :], PI / 2, None, ALU.add).then_inc(dve_step.sem, 1)

            def scalar(act):
                act.wait_ge(dve_step.sem, b_d + 1)
                act.activation(sin[:, :], rest[:, :], ACT.Sin).then_inc(act_step.sem, 1)
                act.wait_ge(dve_step.sem, b_d + 2)
                act.activation(cos[:, :], turns[:, :], ACT.Sin).then_inc(act_step.sem, 1)
                act.wait_ge(act_step.sem, b_a + 1)
                act.activation(sin[:, :], sin[:, :], ACT.Copy, scale=const[:, a0 + freq + 1:a0 + freq + 2]).then_inc(act_step.sem, 1)
            act_step.n += 3
            dve_step.n += 2
            return {"vector": vector, "scalar": scalar}

        def rotate(x, tiles, swap, cos, sin):
            along, across = sq, y_part
            b_p, b_d, b_a, b_e = pe_step.n, dve_step.n, act_step.n, evacuated.n

            def tensor(pe):
                pe.wait_ge(evacuated.sem, b_e)
                for i, k in enumerate(tiles):
                    if b_d + i >= 4:
                        pe.wait_ge(dve_step.sem, b_d + i - 3 if i >= 4 else b_d)
                    pe.matmul(bank[i % 4][:, :], swap, x[:, k, :], start=True, stop=True).then_inc(pe_step.sem, 1)

            def vector(dve):
                dve.wait_ge(act_step.sem, b_a)
                dve.drain()
                for i, k in enumerate(tiles):
                    dve.tensor_tensor(along[i % 2][:, :], x[:, k, :], cos[:, :], ALU.mult)
                    dve.wait_ge(pe_step.sem, b_p + i + 1)
                    dve.tensor_tensor(across[i % 2][:, :], bank[i % 4][:, :], sin[:, :], ALU.mult).then_inc(dve_step.sem, 1)
                    dve.drain()
                    dve.tensor_tensor(x[:, k, :], along[i % 2][:, :], across[i % 2][:, :], ALU.add)
            pe_step.n += len(tiles)
            dve_step.n += len(tiles)
            return {"tensor": tensor, "vector": vector}

        def attention(name, turns_n, q_of, k_of, v_of, static, space, factor, finish, together, key_bias=None):
            PER = 2 * TT
            U = 2 * PER
            HEADS = U // TT
            outs_n = 1 if together else 2
            with ExitStack() as ctx:
                q_st, k_st = ([[x[:, n + r, :] for x in space] for r in range(2)] for n in (0, 2))
                probs = sq + y_part
                v_st = [x[:, :].rearrange("p (j d) -> p j d", d=P) for x in (total, inv)]
                probs_t = [sb(ctx, f"{name}_probs_t{r}", [P, TT, S]) for r in range(2)]
                neg_max = [sb(ctx, f"{name}_neg_max{r}", [P, 1]) for r in range(4)]
                row_sum = [sb(ctx, f"{name}_row_sum{r}", [P, 1]) for r in range(4)]
                score_bank, turn_bank, out_bank = bank[0:4], bank[4:6], bank[6:8]
                b_st, b_s, b_m, b_p, b_hi = staged.n, scores_ready.n, max_ready.n, probs_ready.n, high_staged.n
                b_n, b_t, b_c, b_o, b_d = weighted.n, probs_turned.n, probs_copied.n, out_ready.n, out_done.n
                once = 2 if static else 0
                each = 1 if static else 2

                def stagings(c, p):
                    return [(q_st[p], q_of(c, p))] + ([] if static else [(k_st[p], k_of(c, p))])

                def shaped(x, like):
                    return x[:, None, :] if len(like.shape) == 3 else x[:, :]

                def over_turns(eng, lag, step):
                    def turn_of(c, first, last):
                        for s in range(lag if last else U):
                            def unit(lead):
                                if s >= lead:
                                    return None if last else (c, s - lead)
                                return None if first else (c - 1, s - lead + U)
                            step(c, s, unit)
                    turn_of(0, True, False)
                    with eng.Fori(1, turns_n - 1) as c:
                        turn_of(c, False, False)
                    turn_of(turns_n - 1, False, False)
                    turn_of(turns_n, False, True)

                def next_pair(c, s, unit, stage):
                    if s == 5 and unit(0):
                        stage(c, 1)
                    elif s == PER + 5 and unit(0) and not (isinstance(c, int) and c + 1 == turns_n):
                        stage(c + 1, 0)

                with nc.Block(no_gpsimd_drain=True) as block:
                    @block.tensor
                    def _(pe):
                        def score(c, u):
                            p, e, i = u // PER, u // TT % 2, u % TT
                            n = (i + 1) * P
                            if u % PER == 0:
                                pe.wait_ge(staged.sem, b_st + once + c * (2 * each) + (p * each + each))
                            pe.wait_ge(probs_ready.sem, b_p + c * U + (u - 3))
                            out, rows = score_bank[u % 4], slice(64 * e, 64 * e + 64)
                            three_products(pe, out[:, 0:n], [x[rows, i * P:n] for x in q_st[p]],
                                           [x[rows, 0:n] for x in k_st[p]], True, False)
                            if key_bias is not None:
                                sel, parts = key_bias
                                pe.matmul(out[:, 0:n], sel[:, bass.ds(c * (4 * P) + (2 * p + e) * P, P)], parts[:, 0:n],
                                          start=False, stop=False)
                            pe.matmul(out[:, i * P:n], ident_b[:, :], bias_b[:, :], start=False,
                                      stop=True).then_inc(scores_ready.sem, 1)

                        def turn(c, u):
                            pe.wait_ge(weighted.sem, b_n + c * U + (u + 1))
                            pe.wait_ge(probs_copied.sem, b_c + c * U + (u - 1))
                            for j in range(u % TT + 1):
                                last = pe.transpose(turn_bank[u % 2][:, j * P:(j + 1) * P], probs[u % 4][:, j * P:(j + 1) * P], ident)
                            last.then_inc(probs_turned.sem, 1)

                        def values(c, u):
                            p, e, h = u // PER, u // TT % 2, u // TT
                            pe.wait_ge(probs_copied.sem, b_c + c * U + (u + 1))
                            pe.wait_ge(out_done.sem, b_d + (c if together else c * 2 + (p - 1)))
                            rows = slice(64 * e, 64 * e + 64)
                            out = out_bank[e if together else p]
                            vals = v_of(0, p) if static else v_st[p]
                            for j in range(TT):
                                last = pe.matmul(out[rows, j * P:S], vals[:, j, rows], probs_t[h % 2][:, j, j * P:S],
                                                 start=j == 0 and not (together and p == 1),
                                                 stop=j == TT - 1 and not (together and p == 0))
                            last.then_inc(out_ready.sem, 1)

                        def step(c, s, unit):
                            for lead, part in ((0, score), (3, turn), (5, values)):
                                if unit(lead) and (part is not values or unit(lead)[1] % TT == TT - 1):
                                    part(*unit(lead))
                        over_turns(pe, 5, step)

                    @block.vector
                    def _(dve):
                        def low(st, src, value):
                            dve.wait_ge(high_staged.sem, value)
                            dve.tensor_tensor(shaped(st[1], src), src, shaped(st[0], src).bitcast(F32),
                                              ALU.subtract).then_inc(staged.sem, 1)

                        def stage_low(c, p):
                            for n, (st, src) in enumerate(stagings(c, p)):
                                low(st, src, b_hi + once + c * (2 * each) + (p * each + n + 1))

                        def maximum(c, u):
                            n = (u % TT + 1) * P
                            dve.wait_ge(scores_ready.sem, b_s + c * U + (u + 1))
                            dve.wait_ge(probs_ready.sem, b_p + c * U + (u - 3))
                            dve.tensor_reduce(neg_max[u % 4][:, :], score_bank[u % 4][:, 0:n], AX_X, ALU.max, negate=True).then_inc(max_ready.sem, 1)

                        def weigh(c, u):
                            p, e, i = u // PER, u // TT % 2, u % TT
                            n = (i + 1) * P
                            dve.wait_ge(probs_ready.sem, b_p + c * U + (u + 1))
                            dve.reciprocal(row_sum[u % 4][:, :], row_sum[u % 4][:, :])
                            dve.drain()
                            x = probs[u % 4][:, 0:n]
                            if factor is None:
                                ins = dve.tensor_scalar(x, x, row_sum[u % 4][:, :], None, ALU.mult)
                            else:
                                ins = dve.tensor_scalar(x, x, row_sum[u % 4][:, :], factor(c, p, e, i), ALU.mult, ALU.mult)
                            ins.then_inc(weighted.sem, 1)

                        def take(c, u):
                            p = u // PER
                            if together and p == 0:
                                return
                            dve.wait_ge(out_ready.sem, b_o + c * HEADS + 2 * (p + 1))
                            outs = [out_bank[e if together else p][64 * e:64 * e + 64, :] for e in range(2)]
                            finish(dve, c, p, outs).then_inc(out_done.sem, 1)

                        def step(c, s, unit):
                            for lead, part in ((0, maximum), (1, weigh), (6, take)):
                                if unit(lead) and (part is not take or unit(lead)[1] % PER == PER - 1):
                                    part(*unit(lead))
                            next_pair(c, s, unit, stage_low)
                        if static:
                            for p in range(2):
                                low(k_st[p], k_of(0, p), b_hi + p + 1)
                        stage_low(0, 0)
                        over_turns(dve, 6, step)

                    @block.scalar
                    def _(act):
                        def stage_high(c, p):
                            act.wait_ge(scores_ready.sem, b_s + c * U + (p * PER - PER))
                            act.wait_ge(staged.sem, b_st + once + c * (2 * each) + (p * each - each))
                            for st, src in stagings(c, p):
                                act.activation(shaped(st[0], src), src, ACT.Copy).then_inc(high_staged.sem, 1)
                            if not static:
                                act.wait_ge(out_ready.sem, b_o + c * HEADS + (2 * p - 2))
                                act.activation(v_st[p], v_of(c, p), ACT.Copy)

                        def exponential(c, u):
                            n = (u % TT + 1) * P
                            act.wait_ge(max_ready.sem, b_m + c * U + (u + 1))
                            act.wait_ge(probs_turned.sem, b_t + c * U + (u - 3))
                            act.activation(probs[u % 4][:, 0:n], score_bank[u % 4][:, 0:n], ACT.Exp, bias=neg_max[u % 4][:, :],
                                           accum_out=row_sum[u % 4][:, :]).then_inc(probs_ready.sem, 1)

                        def copy(c, u):
                            i, h = u % TT, u // TT
                            act.wait_ge(probs_turned.sem, b_t + c * U + (u + 1))
                            act.wait_ge(out_ready.sem, b_o + c * HEADS + (h - 1))
                            act.activation(probs_t[h % 2][:, 0:i + 1, i * P:(i + 1) * P],
                                           turn_bank[u % 2][:, 0:(i + 1) * P].rearrange("p (j t) -> p j t", t=P),
                                           ACT.Copy).then_inc(probs_copied.sem, 1)

                        def step(c, s, unit):
                            next_pair(c, s, unit, stage_high)
                            for lead, part in ((0, exponential), (3, copy)):
                                if unit(lead):
                                    part(*unit(lead))
                        if static:
                            for p in range(2):
                                act.activation(k_st[p][0], k_of(0, p), ACT.Copy).then_inc(high_staged.sem, 1)
                        stage_high(0, 0)
                        over_turns(act, 3, step)
                staged.n += once + turns_n * 2 * each
                high_staged.n += once + turns_n * 2 * each
                for t in (scores_ready, max_ready, probs_ready, weighted, probs_turned, probs_copied):
                    t.n += turns_n * U
                out_ready.n += turns_n * HEADS
                out_done.n += turns_n * outs_n

        def split_tiles(src, hi, lo, tiles):
            b_hi, b_lo = split_hi_done.n, split_lo_done.n

            def scalar(act):
                for k in range(tiles):
                    act.activation(hi[:, k, :], src[:, k, :], ACT.Copy).then_inc(split_hi_done.sem, 1)

            def vector(dve):
                for k in range(tiles):
                    dve.wait_ge(split_hi_done.sem, b_hi + k + 1)
                    dve.tensor_tensor(lo[:, k, :], src[:, k, :], hi[:, k, :].bitcast(F32), ALU.subtract).then_inc(split_lo_done.sem, 1)
            split_hi_done.n += tiles
            split_lo_done.n += tiles
            return {"scalar": scalar, "vector": vector}, lambda k: (split_lo_done.sem, b_lo + k + 1)

        def linear_attention(name, heads, dk, q, k, v, dv, scale, wts, put, put_waits=None, decay_of=None, gates=None):
            turns_n = heads // 2
            per = P // dk
            H = TT
            U = 2 * H
            with ExitStack() as ctx:
                k_st, q_st = sq, y_part
                dec = sb(ctx, f"{name}_dec", [P, TT, S]) if gates else None
                m_row = [sb(ctx, f"{name}_m_row{e}", [P, S]) for e in range(2)] if gates else None
                out_bank = bank[4:8]
                b_st, b_s, b_w, b_o, b_d = staged.n, scores_ready.n, weighted.n, out_ready.n, out_done.n
                b_g, b_e, b_k, b_n = gap_ready.n, decay_ready.n, kept.n, den_ready.n
                b_r = [t.n for t in bias_row_in]
                n_st = 2 if per == 2 else 4

                def over_heads(eng, lag, step):
                    step(0, 0, None)
                    step(0, 1, (0, 0))
                    if turns_n > 2:
                        with eng.Fori(1, turns_n - 1) as c:
                            step(c, 0, (c - 1, 1))
                            step(c, 1, (c, 0))
                    step(turns_n - 1, 0, (turns_n - 2, 1))
                    step(turns_n - 1, 1, (turns_n - 1, 0))
                    if lag:
                        step(None, None, (turns_n - 1, 1))

                def following(c, e):
                    if e == 0:
                        return c, 1
                    return None if isinstance(c, int) and c + 1 == turns_n else (c + 1, 0)

                with nc.Block(no_gpsimd_drain=not gates) as block:
                    if gates:
                        @block.sync
                        def _(sp):
                            with sp.Fori(0, turns_n) as c:
                                for e in range(2):
                                    sp.wait_ge(gap_ready.sem, b_g + c * U + (e * H - H))
                                    sp.dma_start(m_row[e][:, :], gates[0][bass.ds(c * 2 + e, 1), :].broadcast_to([P, S]))\
                                        .then_inc(bias_row_in[e].sem, 16)

                        @block.gpsimd
                        def _(pool):
                            with pool.Fori(0, turns_n) as c:
                                for u in range(U):
                                    j = u % H
                                    pool.wait_ge(decay_ready.sem, b_e + c * U + (u + 1))
                                    pool.tensor_tensor(dec[:, j, j * P:(j + 1) * P], dec[:, j, j * P:(j + 1) * P],
                                                       cst("causal_keep"), ALU.mult).then_inc(kept.sem, 1)

                    @block.tensor
                    def _(pe):
                        def scores(c, e):
                            if per == 1 or e == 0:
                                pe.wait_ge(staged.sem, b_st + c * n_st + (e * 2 + 2))
                            for j in range(H):
                                pe.wait_ge(weighted.sem, b_w + c * U + (e * H + j + 1 - H))
                                if per == 2:
                                    kk, qq = k_st[0][64 * e:64 * e + 64, :], q_st[0][64 * e:64 * e + 64, :]
                                else:
                                    kk, qq = k_st[e][:, :], q_st[e][:, :]
                                pe.matmul(bank[j][:, j * P:S], kk[:, j * P:(j + 1) * P], qq[:, j * P:S],
                                          start=True, stop=True).then_inc(scores_ready.sem, 1)

                        def values(c, e):
                            for i in range(H):
                                pe.wait_ge(weighted.sem, b_w + c * U + (e * H + i + 1))
                                pe.wait_ge(out_done.sem, b_d + c * U + (e * H + i + 1 - H))
                                for j in range(i + 1):
                                    last = pe.matmul(out_bank[i][:, 0:dv], wts[e][:, j, i * P:(i + 1) * P], v(c, e, j),
                                                     start=j == 0, stop=j == i)
                                last.then_inc(out_ready.sem, 1)

                        def step(c, e, back):
                            if c is not None:
                                scores(c, e)
                            if back:
                                values(*back)
                        over_heads(pe, 1, step)

                    @block.vector
                    def _(dve):
                        def gap(c, e, j):
                            if j == 0:
                                dve.wait_ge(bias_row_in[e].sem, b_r[e] + (c + 1) * 16)
                            dve.wait_ge(weighted.sem, b_w + c * U + (e * H + j + 1 - H))
                            dve.tensor_scalar(dec[:, j, j * P:S], m_row[e][:, j * P:S], gates[1][:, j, bass.ds(c * 2 + e, 1)],
                                              0.0, ALU.add, ALU.min).then_inc(gap_ready.sem, 1)

                        def weigh(c, e, j):
                            u, n = e * H + j, S - j * P
                            dve.wait_ge(scores_ready.sem, b_s + c * U + (u + 1))
                            if gates:
                                dve.wait_ge(kept.sem, b_k + c * U + (u + 1))
                                d = dec[:, j, j * P:S]
                            else:
                                d = decay_of(c * 2 + e)[:, :, 0:n]
                            if j == 0:
                                dve.wait_ge(out_ready.sem, b_o + c * U + (e * H - H))
                            o, s = wts[e][:, j, j * P:S], bank[j][:, j * P:S]
                            if not gates:
                                o, s = o[:, None, :], s[:, None, :]
                            dve.scalar_tensor_tensor(o, s, scale, d, ALU.mult, ALU.mult).then_inc(weighted.sem, 1)

                        def step(c, e, back):
                            if c is not None:
                                nxt = following(c, e)
                                for j in range(H):
                                    weigh(c, e, j)
                                    if gates and nxt:
                                        gap(*nxt, j)
                            if back and put_waits:
                                dve.wait_ge(out_ready.sem, b_o + back[0] * U + (back[1] * H + H))
                                put_waits(dve, *back, out_bank).then_inc(den_ready.sem, 1)
                        if gates:
                            for j in range(H):
                                gap(0, 0, j)
                        over_heads(dve, 1 if put_waits else 0, step)

                    @block.scalar
                    def _(act):
                        def stage(c, e):
                            act.wait_ge(scores_ready.sem, b_s + c * U + (0 if per == 2 else e * H - H))
                            x = c if per == 2 else c * 2 + e
                            act.activation(k_st[e][:, None, :], k[:, bass.ds(x, 1), :], ACT.Copy).then_inc(staged.sem, 1)
                            act.activation(q_st[e][:, None, :], q[:, bass.ds(x, 1), :], ACT.Copy).then_inc(staged.sem, 1)

                        def decay(c, e):
                            for j in range(H):
                                act.wait_ge(gap_ready.sem, b_g + c * U + (e * H + j + 1))
                                act.activation(dec[:, j, j * P:S], dec[:, j, j * P:S], ACT.Exp).then_inc(decay_ready.sem, 1)

                        def step(c, e, back):
                            if c is not None:
                                nxt = following(c, e)
                                if gates and nxt:
                                    decay(*nxt)
                                if (per == 1 or e == 1) and following(c, 1):
                                    stage(c + 1, 0 if per == 2 else e)
                            if back:
                                for i in range(H):
                                    if put_waits:
                                        act.wait_ge(den_ready.sem, b_n + back[0] * 2 + (back[1] + 1))
                                    act.wait_ge(out_ready.sem, b_o + back[0] * U + (back[1] * H + i + 1))
                                    put(act, *back, i, out_bank[i][:, 0:dv]).then_inc(out_done.sem, 1)
                        for e in range(1 if per == 2 else 2):
                            stage(0, e)
                        if gates:
                            decay(0, 0)
                        over_heads(act, 1, step)
                staged.n += turns_n * n_st
                for t in (scores_ready, weighted, out_ready, out_done):
                    t.n += turns_n * U
                if put_waits:
                    den_ready.n += heads
                if gates:
                    for t in (gap_ready, decay_ready, kept):
                        t.n += turns_n * U
                    for t in bias_row_in:
                        t.n += 16 * turns_n

        def head_norm(h, heads, gate, sq_h, hi, lo, first=0, weight=None):
            ss = total[:, 0:TT * heads].rearrange("p (t n) -> p t n", t=TT)
            b_a, b_d, b_t, b_h, b_o = act_step.n, dve_step.n, turned.n, turned_hi.n, turned_out.n
            with nc.Block(no_gpsimd_drain=True) as block:
                @block.tensor
                def _(pe):
                    for n in range(heads):
                        if n >= 4:
                            pe.wait_ge(turned_out.sem, b_o + n - 3)
                        pe.wait_ge(dve_step.sem, b_d + 1 + n + 1)
                        for t in range(TT):
                            last = pe.transpose(bank[n % 4][:, t * P:(t + 1) * P], h[:, t, n, :], ident)
                        last.then_inc(turned.sem, 1)

                @block.scalar
                def _(act):
                    for t in range(TT):
                        act.activation(sq_h[:, t, :, :], h[:, t, :, :], ACT.Square).then_inc(act_step.sem, 1)
                    act.wait_ge(dve_step.sem, b_d + 1)
                    act.activation(ss[:, :, :], ss[:, :, :], ACT.Sqrt, scale=1.0 / P, bias=EPS).then_inc(act_step.sem, 1)
                    for n in range(heads):
                        act.wait_ge(turned.sem, b_t + n + 1)
                        act.activation(hi[:, first + n, :], bank[n % 4][:, :], ACT.Copy,
                                       scale=1.0 if weight is None else gain(weight, n)).then_inc(turned_hi.sem, 1)

                @block.vector
                def _(dve):
                    def low(n):
                        dve.wait_ge(turned_hi.sem, b_h + n + 1)
                        high = hi[:, first + n, :].bitcast(F32)
                        if weight is None:
                            ins = dve.tensor_tensor(lo[:, first + n, :], bank[n % 4][:, :], high, ALU.subtract)
                        else:
                            ins = dve.scalar_tensor_tensor(lo[:, first + n, :], bank[n % 4][:, :], gain(weight, n), high,
                                                           ALU.mult, ALU.subtract)
                        ins.then_inc(turned_out.sem, 1)
                    for t in range(TT):
                        dve.wait_ge(act_step.sem, b_a + t + 1)
                        dve.tensor_reduce(ss[:, t, :], sq_h[:, t, :, :], AX_X, ALU.add)
                    dve.drain()
                    dve.engine_nop().then_inc(dve_step.sem, 1)
                    dve.wait_ge(act_step.sem, b_a + TT + 1)
                    dve.reciprocal(ss[:, :, :], ss[:, :, :])
                    dve.drain()
                    for n in range(heads):
                        for t in range(TT):
                            ins = dve.scalar_tensor_tensor(h[:, t, n, :], h[:, t, n, :], ss[:, t, n:n + 1], gate[:, t, n, :],
                                                           ALU.mult, ALU.mult)
                        ins.then_inc(dve_step.sem, 1)
                        if n >= 2:
                            low(n - 2)
                    low(heads - 2)
                    low(heads - 1)
            act_step.n += TT + 1
            dve_step.n += 1 + heads
            for t in (turned, turned_hi, turned_out):
                t.n += heads

        def compressed_loads(pe_rows, w1, w2):
            b_in = [t.n for t in inputs_in]

            def sync(sp):
                for s, n in enumerate(("cmp_pos_k", "cmp_pos_v")):
                    sp.dma_start(pe_rows[:, s, :], io[n][0].rearrange("(j l) d -> j (l d)", l=2)).then_inc(inputs_in[0].sem, 16)
                for s, n in enumerate(("cmp_k_w1", "cmp_v_w1")):
                    sp.dma_start(w1[s][:, :, :], io[n][0].rearrange("(j p) n -> p j n", p=P)).then_inc(inputs_in[1 + s].sem, 16)
                for s, n in enumerate(("cmp_k_w2", "cmp_v_w2")):
                    sp.dma_start(w2[:, s, :, :], io[n][0].rearrange("(t p) d -> p t d", p=P)).then_inc(inputs_in[3].sem, 16)
            for t, n in zip(inputs_in, (2, 1, 1, 2)):
                t.n += 16 * n
            return {"sync": sync}, b_in

        def compressed(ctx, loaded, pe_rows, w1, w2, qk, vg, gate, o):
            pe_t = sb(ctx, "pe_t", [P, 2, CB // 2])
            blk = sb(ctx, "cmp_blk", [P, 2, CB // 2, KV, CB])
            hid = sb(ctx, "cmp_hid", [KV * CB, 2, CH])
            hid_k = sb(ctx, "cmp_hid_k", [P, 2, KV, CB])
            hid_v = sb(ctx, "cmp_hid_v", [P, 2, KV, 4, CB])
            k_cmp = sb(ctx, "k_cmp", [P, CB])
            v_blk = sb(ctx, "cmp_v_blk", [P, KV, 4, HD])
            sc = sb(ctx, "cmp_sc", [P, KV, TT, 4, CB])
            mx = sb(ctx, "cmp_max", [P, KV, TT, 4])
            coef = sb(ctx, "cmp_coef", [P, KV, TT, 4])
            probs_t = sb(ctx, "cmp_probs_t", [P, KV, S])
            p0, d0, a0, g0 = pe_step.n, dve_step.n, act_step.n, pool_step.n
            with nc.Block() as block:
                @block.gpsimd
                def _(pool):
                    pool.memset(blk[:, :, :, :, NC:CB], 0.0).then_inc(pool_step.sem, 1)
                    pool.memset(v_blk[:, :, :, :], 0.0).then_inc(pool_step.sem, 1)

                @block.tensor
                def _(pe):
                    pe.wait_ge(inputs_in[0].sem, loaded[0] + 32)
                    for s in range(2):
                        pe.transpose(bank[0][:, s * 16:(s + 1) * 16], pe_rows[:, s, :], ident[0:16, 0:16])
                    pe.matmul(bank[1][:, :], cst("swap_ret"), qk[:, 4, :], start=True, stop=True)
                    pe.matmul(bank[2][:, :], cst("swap_ret"), qk[:, 5, :], start=True, stop=True).then_inc(pe_step.sem, 1)
                    pe.wait_ge(pool_step.sem, g0 + 1)
                    for s in range(2):
                        pe.wait_ge(inputs_in[1 + s].sem, loaded[1 + s] + 16)
                        pe.wait_ge(dve_step.sem, d0 + s + 1)
                        for j in range(CB // 2):
                            last = pe.matmul(bank[3 + s][0:KV * CB, 0:CH], blk[:, s, j, :, :].rearrange("p g c -> p (g c)"), w1[s][:, j, :],
                                             start=j == 0, stop=j == CB // 2 - 1)
                        last.then_inc(pe_step.sem, 1)
                    for s in range(2):
                        pe.wait_ge(act_step.sem, a0 + s + 1)
                        for t in range(2):
                            last = pe.transpose(bank[5 + s][:, t * 64:(t + 1) * 64], hid[:, s, t * P:(t + 1) * P], ident[0:64, 0:64])
                        last.then_inc(pe_step.sem, 1)
                    pe.wait_ge(inputs_in[3].sem, loaded[3] + 32)
                    pe.wait_ge(act_step.sem, a0 + 3)
                    for g in range(KV):
                        for t in range(2):
                            last = pe.matmul(bank[0][64 * g:64 * g + 64, 0:CB], w2[:, 0, t, :], hid_k[:, t, g, :], start=t == 0, stop=t == 1)
                    last.then_inc(pe_step.sem, 1)
                    pe.wait_ge(act_step.sem, a0 + 4)
                    for g in range(KV):
                        for t in range(2):
                            last = pe.matmul(bank[1][:, g * HD:(g + 1) * HD], hid_v[:, t, g, :, :].rearrange("p h c -> p (h c)"),
                                             w2[:, 1, t, :], start=t == 0, stop=t == 1)
                    last.then_inc(pe_step.sem, 1)
                    pe.wait_ge(dve_step.sem, d0 + 3)
                    for g in range(KV):
                        for i in range(TT):
                            for h in range(4):
                                at_col = (i * 4 + h) * CB
                                last = pe.matmul(bank[(2, 7)[g]][:, at_col:at_col + CB], qk[64 * g:64 * g + 64, h, i * P:(i + 1) * P],
                                                 k_cmp[64 * g:64 * g + 64, :], start=True, stop=True)
                        last.then_inc(pe_step.sem, 1)
                    for g in range(KV):
                        pe.wait_ge(dve_step.sem, d0 + 7 + g)
                        for i in range(TT):
                            last = pe.transpose(bank[3 + g][:, i * P:(i + 1) * P], sc[:, g, i, :, :].rearrange("p h c -> p (h c)"), ident)
                        last.then_inc(pe_step.sem, 1)
                    pe.wait_ge(dve_step.sem, d0 + 10)
                    for h in range(4):
                        for g in range(KV):
                            last = pe.matmul(bank[4 + h][64 * g:64 * g + 64, :], v_blk[:, g, h, :], probs_t[:, g, :], start=True, stop=True)
                        last.then_inc(pe_step.sem, 1)

                @block.scalar
                def _(act):
                    act.activation(gate[:, :, :], vg[:, :, 256:280], ACT.Sigmoid)
                    for s in range(2):
                        act.wait_ge(pe_step.sem, p0 + 2 + s)
                        act.activation(hid[:, s, :], bank[3 + s][0:KV * CB, 0:CH], ACT.Silu).then_inc(act_step.sem, 1)
                    act.wait_ge(pe_step.sem, p0 + 4)
                    act.activation(hid_k[:, :, :, :], bank[5][:, 0:P].rearrange("p (t g c) -> p t g c", t=2, c=CB), ACT.Copy).then_inc(act_step.sem, 1)
                    act.wait_ge(pe_step.sem, p0 + 5)
                    for h in range(4):
                        last = act.activation(hid_v[:, :, :, h, :], bank[6][:, 0:P].rearrange("p (t g c) -> p t g c", t=2, c=CB), ACT.Copy)
                    last.then_inc(act_step.sem, 1)
                    for g in range(KV):
                        act.wait_ge(dve_step.sem, d0 + 5 + g)
                        act.activation(sc[:, g, :, :, :], sc[:, g, :, :, :], ACT.Exp).then_inc(act_step.sem, 1)

                @block.vector
                def _(dve):
                    dve.wait_ge(pe_step.sem, p0 + 1)
                    dve.tensor_copy(pe_t[:, :, :], bank[0][:, 0:CB].rearrange("p (s j) -> p s j", s=2))
                    dve.drain()
                    for s in range(2):
                        for g in range(KV):
                            for h in range(2):
                                half = slice(64 * h, 64 * h + 64)
                                src = qk[half, 4 + s, :] if g == h else bank[1 + s][half, :]
                                for r in range(2):
                                    x = src[:, 16 * r:16 * r + 16 * NC].rearrange("p (c j l) -> p j c l", j=8, l=2)[:, :, :, h]
                                    last = dve.tensor_tensor(blk[half, s, 8 * r:8 * r + 8, g, 0:NC], x,
                                                             pe_t[half, s, 8 * r:8 * r + 8, None].broadcast_to([64, 8, NC]), ALU.add)
                        last.then_inc(dve_step.sem, 1)
                    dve.wait_ge(pe_step.sem, p0 + 6)
                    dve.tensor_copy(k_cmp[:, :], bank[0][:, 0:CB]).then_inc(dve_step.sem, 1)
                    dve.wait_ge(pe_step.sem, p0 + 7)
                    dve.wait_ge(pool_step.sem, g0 + 2)
                    for g in range(KV):
                        for h in range(4):
                            last = dve.tensor_copy(v_blk[32 * h:32 * h + 32, g, h, :], bank[1][32 * h:32 * h + 32, g * HD:(g + 1) * HD])
                    last.then_inc(dve_step.sem, 1)
                    bias = cst("cmp_bias").rearrange("p (i c) -> p i c", c=CB)[:, :, None, :].broadcast_to([P, TT, 4, CB])
                    for g in range(KV):
                        dve.wait_ge(pe_step.sem, p0 + 8 + g)
                        s4 = bank[(2, 7)[g]][:, :].rearrange("p (i h c) -> p i h c", h=4, c=CB)
                        dve.tensor_tensor(sc[:, g, :, :, :], s4, bias, ALU.add)
                        dve.drain()
                        dve.tensor_reduce(mx[:, g, :, :], sc[:, g, :, :, :], AX_X, ALU.max)
                        dve.drain()
                        dve.tensor_tensor(sc[:, g, :, :, :], sc[:, g, :, :, :], mx[:, g, :, :, None].broadcast_to([P, TT, 4, CB]),
                                          ALU.subtract).then_inc(dve_step.sem, 1)
                    for g in range(KV):
                        dve.wait_ge(act_step.sem, a0 + 5 + g)
                        dve.tensor_reduce(mx[:, g, :, :], sc[:, g, :, :, :], AX_X, ALU.add)
                        dve.drain()
                        dve.reciprocal(mx[:, g, :, :], mx[:, g, :, :])
                        dve.tensor_tensor(coef[:, g, :, :], gate[:, :, :].rearrange("p i (e c b) -> p i e c b", e=2, b=3)[:, :, g, :, 0],
                                          cst("cmp_any")[:, :, None].broadcast_to([P, TT, 4]), ALU.mult)
                        dve.drain()
                        dve.tensor_tensor(coef[:, g, :, :], coef[:, g, :, :], mx[:, g, :, :], ALU.mult)
                        dve.drain()
                        dve.tensor_tensor(sc[:, g, :, :, :], sc[:, g, :, :, :], coef[:, g, :, :, None].broadcast_to([P, TT, 4, CB]),
                                          ALU.mult).then_inc(dve_step.sem, 1)
                    for g in range(KV):
                        dve.wait_ge(pe_step.sem, p0 + 10 + g)
                        dve.tensor_copy(probs_t[:, g, :], bank[3 + g][:, :]).then_inc(dve_step.sem, 1)
                    for h in range(4):
                        dve.wait_ge(pe_step.sem, p0 + 12 + h)
                        dve.tensor_copy(o[:, h, :], bank[4 + h][:, :])
            pe_step.n += 15
            dve_step.n += 10
            act_step.n += 6
            pool_step.n += 2

        def nsa(pos_i, o):
            with ExitStack() as mid:
                qk = sb(mid, "nsa_qk", [P, 8, S])
                vg = sb(mid, "nsa_vg", [P, TT, 280])
                gate = sb(mid, "nsa_gate", [P, TT, GATES])
                with ExitStack() as inner:
                    pe_rows = sb(inner, "pe_rows", [CB // 2, 2, P])
                    w1 = [sb(inner, f"cmp_w1_{s}", [P, CB // 2, CH]) for s in range(2)]
                    w2 = sb(inner, "cmp_w2", [P, 2, 2, HD])
                    with ExitStack() as deep:
                        cos, sin = sb(deep, "nsa_cos", [P, S]), sb(deep, "nsa_sin", [P, S])

                        def take_rows(dve, g, t):
                            return dve.tensor_copy(vg[:, t, :], bank[4 + t][:, 0:280])
                        work = [sb(deep, f"rope_{n}", [P, S]) for n in ("ang", "turns", "rest")]
                        first = [positions_load(pos_i), inverse_root()]
                        stage, ready = normalise(0)
                        first.append(stage)
                        first.append(dense("q", two_chunks(a_tiles), copy_to(qk, float(HD) ** -0.5), tile_ready=ready))
                        first.append(rope_tables(work, pos_i, 0, cos, sin))
                        first.append(dense("kcvc", two_chunks(a_tiles), copy_to(qk[:, 4:8, :])))
                        stage, loaded = compressed_loads(pe_rows, w1, w2)
                        first.append(stage)
                        first.append(rotate(qk, (0, 1, 2, 3, 4, 6, 7), cst("swap_nsa"), cos, sin))
                        first.append(dense_rows("vg", evac_dve=take_rows))
                        run(*first)
                    with ExitStack() as deep:
                        compressed(deep, loaded, pe_rows, w1, w2, qk, vg, gate, o)
                space = [sb(mid, f"nsa_space_{n}", [P, 4, S], F32R) for n in ("hi", "lo")]

                def factor(c, p, e, i):
                    return gate[:, i, bass.ds(c * 3 + (3 * 4 * e + p + 1), 1)]

                def finish(dve, c, p, outs):
                    for e in range(2):
                        half = slice(64 * e, 64 * e + 64)
                        dst = o[half, bass.ds(c, 1), :]
                        ins = dve.tensor_tensor(dst, outs[e][:, None, :], dst, ALU.add)
                    return ins
                attention("nsa", HQ // 2, lambda c, p: qk[:, bass.ds(c, 1), :], lambda c, p: qk[:, 6 + p, :],
                          lambda c, p: vg[:, :, p * P:(p + 1) * P], True, space, factor, finish, True)

        def retention(pos_i, cos, sin, spare, h_hi, h_lo):
            with ExitStack() as ctx:
                qk = sb(ctx, "ret_qk", [P, 8, S])
                vg = sb(ctx, "ret_vg", [P, TT, 2, RH * RD])
                h = qk[:, 0:RH, :].rearrange("p n (t d) -> p t n d", d=RD)
                wts = [spare, sb(ctx, "ret_wts", [P, TT, S])]
                decay = sb(ctx, "ret_decay", [P, RH, S])
                b_in = inputs_in[0].n
                inputs_in[0].n += 16

                def decay_load(sp):
                    sp.dma_start(decay[:, :, :], io["decay"]).then_inc(inputs_in[0].sem, 16)

                def rows_dve(dve, g, t):
                    return dve.tensor_copy(vg[:, t, bass.ds(g, 1), :], bank[4 + t][:, None, :])
                with ExitStack() as inner:
                    work = [wts[1][:, n, :] for n in range(3)]
                    run(split_tiles(spare, h_hi, h_lo, 4)[0], dense("rqk", two_chunks(a_tiles), copy_to(qk)), {"sync": decay_load},
                        rope_tables(work, pos_i, 2, cos, sin),
                        rotate(qk, range(4), cst("swap_ret"), cos, sin),
                        dense_rows("rvg", evac_dve=rows_dve),
                        rotate(qk, range(4, 8), cst("swap_ret"), cos, sin))
                with nc.Block() as block:
                    @block.sync
                    def _(sp):
                        sp.wait_ge(inputs_in[0].sem, b_in + 16)

                    @block.scalar
                    def _(act):
                        act.activation(vg[:, :, 1, :], vg[:, :, 1, :], ACT.Silu)

                def put(act, c, e, i, out):
                    return act.activation(h[:, i, bass.ds(c * 2 + e, 1), :], out[:, None, :], ACT.Copy)
                linear_attention("ret", RH, RD, qk[:, 0:4, :], qk[:, 4:8, :],
                                 lambda c, e, j: vg[:, j, 0, bass.ds(c * 256 + e * P, P)], RD, float(RD) ** -0.5, wts, put,
                                 decay_of=lambda x: decay[:, bass.ds(x, 1), :])
                head_norm(h, RH, vg[:, :, 1, :].rearrange("p t (n d) -> p t n d", d=RD),
                          wts[0][:, :, :].rearrange("p t (n d) -> p t n d", d=RD), h_hi, h_lo, first=4)

        def mixing(h_hi, h_lo):
            with ExitStack() as ctx:
                mix = sb(ctx, "mix", [P, 1, S])
                mix_hi = sb(ctx, "mix_hi", [P, KT, S], F32R)
                mix_lo = sb(ctx, "mix_lo", [P, KT, S], F32R)
                sig = sb(ctx, "mix_sig", [P, 2, S])
                half_mix = sb(ctx, "half_mix", [P, 2, S])
                h_tiles = [(h_hi[:, k, :], h_lo[:, k, :]) for k in range(KT)]
                mix_tiles = [(mix_hi[:, k, :], mix_lo[:, k, :]) for k in range(KT)]
                chunks = [two_chunks(a_tiles)[0], [[(k * 256 + c * P, h_tiles[4 * c + k]) for k in range(4)] for c in range(2)]]
                b_mix = mixed.n
                chunk = lambda b, m: (b - 1) // 2 if isinstance(b, int) else m["i"]

                def early_dve(dve, b, slot, m):
                    if slot == m["slot"]:
                        return
                    dve.wait_ge(products_done.sem, m["prod"] + b + 1)
                    dve.wait_ge(evacuated.sem, m["evac"] + b)
                    for c in range(2):
                        ins = dve.tensor_tensor(half_mix[:, c, :], bank[2 * slot + c][:, :], sig[:, c, :], ALU.mult)
                    ins.then_inc(evacuated.sem, 1)
                    dve.drain()
                    dve.tensor_tensor(mix[:, :, :], half_mix[:, 0:1, :], half_mix[:, 1:2, :], ALU.add).then_inc(mixed.sem, 1)

                def late_act(act, b, slot, m):
                    if slot == m["slot"]:
                        act.wait_ge(products_done.sem, m["prod"] + b + 1)
                        act.wait_ge(evacuated.sem, m["evac"] + b)
                        for c in range(2):
                            ins = act.activation(sig[:, c, :], bank[2 * slot + c][:, :], ACT.Sigmoid)
                        ins.then_inc(evacuated.sem, 1)
                    else:
                        ch = chunk(b, m)
                        act.wait_ge(mixed.sem, b_mix + ch * 3 + 1)
                        act.activation(mix_hi[:, bass.ds(ch, 1), :], mix[:, :, :], ACT.Copy).then_inc(mixed.sem, 1)

                def late_dve(dve, b, slot, m):
                    if slot != m["slot"]:
                        ch = chunk(b, m)
                        dve.wait_ge(mixed.sem, b_mix + ch * 3 + 2)
                        dve.tensor_tensor(mix_lo[:, bass.ds(ch, 1), :], mix[:, :, :], mix_hi[:, bass.ds(ch, 1), :].bitcast(F32),
                                          ALU.subtract).then_inc(mixed.sem, 1)
                sq_act, sq_dve = sums_on_the_way(xT)
                first = dense("mix", chunks, early_dve, late_dve, none, late_act)
                mixed.n += 3 * KT
                run(first, dense("out1", two_chunks(mix_tiles), add_to(xT), sq_dve, none, sq_act,
                                 tile_ready=lambda k: (mixed.sem, b_mix + 3 * k + 3)))

        def mlp():
            with ExitStack() as ctx:
                h_hi = sb(ctx, "mlp_hi", [P, KT, S], F32R)
                h_lo = sb(ctx, "mlp_lo", [P, KT, S], F32R)
                pos = [sb(ctx, f"mlp_pos{r}", [P, 2, S]) for r in range(2)]
                pos_sq = [sb(ctx, f"mlp_pos_sq{r}", [P, 2, S]) for r in range(2)]
                h_tiles = [(h_hi[:, k, :], h_lo[:, k, :]) for k in range(KT)]

                def early_act(act, b, slot, m):
                    act.wait_ge(products_done.sem, m["prod"] + b + 1)
                    act.wait_ge(hid_ready.sem, m["hid"] + b - 1)
                    for c in range(2):
                        ins = act.activation(pos[slot][:, c, :], bank[2 * slot + c][:, :], ACT.Relu)
                    ins.then_inc(evacuated.sem, 1)

                def early_dve(dve, b, slot, m):
                    dve.wait_ge(evacuated.sem, m["evac"] + b + 1)
                    dve.tensor_tensor(pos_sq[slot][:, :, :], pos[slot][:, :, :], pos[slot][:, :, :], ALU.mult)

                def late_act(act, b, slot, m):
                    act.wait_ge(evacuated.sem, m["evac"] + b + 1)
                    act.activation(h_hi[:, bass.ds(b * 2, 2), :], pos[slot][:, :, :], ACT.Square).then_inc(part_ready.sem, 1)

                def late_dve(dve, b, slot, m):
                    dve.wait_ge(part_ready.sem, m["part"] + b + 1)
                    dve.drain()
                    dve.tensor_tensor(h_lo[:, bass.ds(b * 2, 2), :], pos_sq[slot][:, :, :], h_hi[:, bass.ds(b * 2, 2), :].bitcast(F32),
                                      ALU.subtract).then_inc(hid_ready.sem, 1)
                stages = [inverse_root()]
                stage, ready = normalise(1)
                stages.append(stage)
                for g in range(4):
                    b_hid = hid_ready.n
                    stages.append(dense(f"up{g}", two_chunks(a_tiles), early_dve, late_dve, early_act, late_act,
                                        tile_ready=ready if g == 0 else None))
                    part_ready.n += 4
                    hid_ready.n += 4
                    sq_act, sq_dve = sums_on_the_way(xT) if g == 3 else (none, none)
                    stages.append(dense(f"down{g}", two_chunks(h_tiles), add_to(xT), sq_dve, none, sq_act,
                                        tile_ready=(lambda b_hid: lambda k: (hid_ready.sem, b_hid + k // 2 + 1))(b_hid)))
                    if g == 3:
                        squared.n += KT
                        summed.n += KT
                stages += [inverse_root(), update(2)]
                run(*stages)

        def first_block():
            with ExitStack() as ctx:
                pos_i = sb(ctx, "pos_i", [P, S], I32)
                cos_r, sin_r = sb(ctx, "ret_cos", [P, S]), sb(ctx, "ret_sin", [P, S])
                o = sb(ctx, "nsa_o", [P, 4, S])
                nsa(pos_i, o)
                h_hi = sb(ctx, "cat_hi", [P, KT, S], F32R)
                h_lo = sb(ctx, "cat_lo", [P, KT, S], F32R)
                retention(pos_i, cos_r, sin_r, o, h_hi, h_lo)
                mixing(h_hi, h_lo)
                squared.n += KT
                summed.n += KT
            mlp()

        def log_sigmoid(act, dve, x, t1, t2, b_a, b_d, part):
            if part == "dve":
                dve.scalar_tensor_tensor(t1, x, -1.0, x, ALU.mult, ALU.min).then_inc(dve_step.sem, 1)
                dve.tensor_scalar(t2, x, 0.0, None, ALU.min)
                dve.drain()
                dve.wait_ge(act_step.sem, b_a + 1)
                dve.tensor_tensor(x, t2, t1, ALU.subtract)
                dve.drain()
            else:
                act.wait_ge(dve_step.sem, b_d + 1)
                act.activation(t1, t1, ACT.Exp)
                act.drain()
                act.activation(t1, t1, ACT.Ln, bias=1.0).then_inc(act_step.sem, 1)

        def mlstm():
            with ExitStack() as ctx:
                h = sb(ctx, "ml_h", [P, TT, MH, MV])
                with ExitStack() as inner:
                    qk = sb(inner, "ml_qk", [P, 8, S])
                    v = sb(inner, "ml_v", [P, TT, MH, MV + 1])
                    og = sb(inner, "ml_og", [P, TT, MH, MV])
                    a_col = sb(inner, "ml_a_col", [P, TT, MH])
                    e_col = sb(inner, "ml_e_col", [P, TT, MH])
                    with ExitStack() as tmp:
                        bias = sb(tmp, "ml_bias", [MH, 2])
                        lf, ig, t1, t2 = (sb(tmp, f"ml_{n}", [MH, S]) for n in ("lf", "ig", "t1", "t2"))
                        fsum, mrun, one = (sb(tmp, f"ml_{n}", [MH, S]) for n in ("fsum", "mrun", "one"))
                        b_in = inputs_in[0].n
                        inputs_in[0].n += 32

                        def bias_load(sp):
                            sp.dma_start(bias[:, 0:1], io["mlstm_b_gate_2"][0, 0:MH].rearrange("(h a) -> h a", a=1)).then_inc(inputs_in[0].sem, 16)
                            sp.dma_start(bias[:, 1:2], io["mlstm_b_gate_2"][0, MH:2 * MH].rearrange("(h a) -> h a", a=1)).then_inc(inputs_in[0].sem, 16)

                        def gate_rows(dve, b, slot, m):
                            dve.wait_ge(products_done.sem, m["prod"] + b + 1)
                            dve.tensor_copy(ig[:, :], bank[2 * slot][0:MH, :])
                            dve.tensor_copy(lf[:, :], bank[2 * slot][32:32 + MH, :]).then_inc(evacuated.sem, 1)

                        def v_rows(dve, g, t):
                            return dve.tensor_copy(v[:, t, bass.ds(g * 4, 4), 0:MV], bank[4 + t][:, :].rearrange("p (h d) -> p h d", d=MV))

                        def o_rows(act, g, t):
                            return act.activation(og[:, t, bass.ds(g * 4, 4), :], bank[4 + t][:, :].rearrange("p (h d) -> p h d", d=MV), ACT.Sigmoid)
                        stage, ready = normalise(3)
                        stages = [{"sync": bias_load}, inverse_root_of_mean(), stage]
                        stages.append(dense("mg", [[[(k * P, a_tiles[k]) for k in range(KT)]]], gate_rows, tile_ready=ready))
                        b_a, b_d, b_p, b_st, b_pool = act_step.n, dve_step.n, pe_step.n, rows_stored.n, pool_step.n

                        def gate_pool(pool):
                            pool.memset(v[:, :, :, MV:MV + 1], 1.0)

                        def gate_vector(dve):
                            dve.memset(one[:, :], 1.0)
                            dve.wait_ge(inputs_in[0].sem, b_in + 32)
                            dve.drain()
                            dve.tensor_scalar(ig[:, :], ig[:, :], bias[:, 0:1], None, ALU.add)
                            dve.tensor_scalar(lf[:, :], lf[:, :], bias[:, 1:2], None, ALU.add)
                            dve.drain()
                            log_sigmoid(None, dve, lf[:, :], t1[:, :], t2[:, :], b_a, b_d, "dve")
                            dve.tensor_tensor_scan(fsum[:, :], one[:, :], lf[:, :], 0.0, ALU.mult, ALU.add)
                            dve.drain()
                            dve.tensor_tensor(ig[:, :], ig[:, :], fsum[:, :], ALU.subtract)
                            dve.drain()
                            dve.tensor_tensor_scan(mrun[:, :], one[:, :], ig[:, :], 0.0, ALU.mult, ALU.max)
                            dve.drain()
                            dve.tensor_scalar(t2[:, :], mrun[:, :], -1.0, None, ALU.mult)
                            dve.tensor_tensor(t1[:, :], fsum[:, :], mrun[:, :], ALU.add)
                            dve.drain()
                            dve.engine_nop().then_inc(dve_step.sem, 1)

                        def gate_scalar(act):
                            log_sigmoid(act, None, lf[:, :], t1[:, :], t2[:, :], b_a, b_d, "act")
                            act.wait_ge(dve_step.sem, b_d + 2)
                            act.activation(t1[:, :], t1[:, :], ACT.Exp, scale=-1.0).then_inc(act_step.sem, 1)
                        stages.append({"gpsimd": gate_pool, "vector": gate_vector, "scalar": gate_scalar})
                        act_step.n += 2
                        dve_step.n += 2
                        stages.append(dense("mqk", two_chunks(a_tiles), copy_to(qk)))

                        b_e = evacuated.n

                        def turn_tensor(pe):
                            pe.wait_ge(dve_step.sem, b_d + 2)
                            pe.wait_ge(evacuated.sem, b_e)
                            for t in range(TT):
                                pe.transpose(bank[0][:, t * MH:(t + 1) * MH], ig[:, t * P:(t + 1) * P], ident[0:MH, 0:MH])
                            pe.wait_ge(act_step.sem, b_a + 2)
                            for t in range(TT):
                                last = pe.transpose(bank[1][:, t * MH:(t + 1) * MH], t1[:, t * P:(t + 1) * P], ident[0:MH, 0:MH])
                            last.then_inc(pe_step.sem, 1)

                        def turn_vector(dve):
                            dve.wait_ge(pe_step.sem, b_p + 1)
                            dve.tensor_copy(a_col[:, :, :], bank[0][:, 0:TT * MH].rearrange("p (t h) -> p t h", h=MH))
                            dve.tensor_copy(e_col[:, :, :], bank[1][:, 0:TT * MH].rearrange("p (t h) -> p t h", h=MH)).then_inc(dve_step.sem, 1)

                        def row_store(sp):
                            sp.wait_ge(dve_step.sem, b_d + 2)
                            sp.dma_start(io["row_scratch"][0:MH, :], t2[:, :]).then_inc(rows_stored.sem, 16)
                        stages.append({"tensor": turn_tensor, "vector": turn_vector, "sync": row_store})
                        pe_step.n += 1
                        dve_step.n += 1
                        stages.append(dense_rows("mv", evac_dve=v_rows))
                        stages.append(dense_rows("mo", evac_act=o_rows))
                        rows_stored.n += 16
                        stages.append({"sync": lambda sp: sp.wait_ge(rows_stored.sem, b_st + 16)})
                        run(*stages)
                    with ExitStack() as tmp:
                        dens = [sb(tmp, f"ml_den{r}", [P, TT]) for r in range(2)]

                        def denominators(dve, c, e, outs):
                            den = dens[e]
                            for i in range(TT):
                                dve.scalar_tensor_tensor(den[:, i:i + 1], outs[i][:, MV:MV + 1], -1.0, e_col[:, i, bass.ds(c * 2 + e, 1)],
                                                         ALU.mult, ALU.max)
                            dve.drain()
                            for i in range(TT):
                                dve.tensor_tensor(den[:, i:i + 1], outs[i][:, MV:MV + 1], den[:, i:i + 1], ALU.max)
                            dve.drain()
                            return dve.reciprocal(den[:, :], den[:, :])

                        def put(act, c, e, i, out):
                            return act.activation(h[:, i, bass.ds(c * 2 + e, 1), :], out[:, None, 0:MV], ACT.Copy, scale=dens[e][:, i:i + 1])
                        wts = [sb(tmp, f"ml_wts{e}", [P, TT, S]) for e in range(2)]
                        linear_attention("ml", MH, MK, qk[:, 0:4, :], qk[:, 4:8, :],
                                         lambda c, e, j: v[:, j, bass.ds(c * 2 + e, 1), :], MV + 1, float(MK) ** -0.5, wts, put,
                                         denominators, gates=(io["row_scratch"], a_col))
                    head_norm(h, MH, og, qk[:, :, :].rearrange("p (t n) (m d) -> p t (n m) d", t=TT, d=MV), a_hi, a_lo, weight=12)
            post_norm_dense("mout", 5, a_tiles)

        def post_norm_dense(name, vec, xs, src=None):
            with ExitStack() as ctx:
                y = sb(ctx, f"{name}_y", [P, KT, S])
                sq_act, sq_dve = sums_on_the_way(y)
                stages, ready = [], None
                if src is not None:
                    stage, ready = split_tiles(src, a_hi, a_lo, KT)
                    stages.append(stage)
                stages.append(dense(name, two_chunks(xs), copy_to(y), sq_dve, none, sq_act, tile_ready=ready))
                squared.n += KT
                summed.n += KT
                stages += [inverse_root(), update(vec, src=y)]
                run(*stages)

        def ffn(l):
            with ExitStack() as ctx:
                y = sb(ctx, f"ffn{l}_y", [P, KT, S])
                h_hi = sb(ctx, f"ffn{l}_hi", [P, KT, S], F32R)
                h_lo = sb(ctx, f"ffn{l}_lo", [P, KT, S], F32R)
                u = [sb(ctx, f"ffn{l}_u{r}", [P, 2, S + 2]) for r in range(2)]
                z = [sb(ctx, f"ffn{l}_z{r}", [P, 2, S]) for r in range(2)]
                h_tiles = [(h_hi[:, k, :], h_lo[:, k, :]) for k in range(KT)]
                b_pool = pool_step.n

                def margins(pool):
                    for r in range(2):
                        pool.memset(u[r][:, :, 0:2], 0.0).then_inc(pool_step.sem, 1)
                pool_step.n += 2
                stage, ready = normalise(7 + l)
                stages = [{"gpsimd": margins, "vector": lambda dve: dve.wait_ge(pool_step.sem, b_pool + 2)}, inverse_root_of_mean(), stage]
                for g, (f0, n) in enumerate(FG):
                    def tap(j, b, c, f0=f0):
                        return conv[:, 2 * l + j // 2, bass.ds(b + (44 * (j % 2) + FT * c + f0), 1)]

                    def early_act(act, b, slot, m):
                        act.wait_ge(products_done.sem, m["prod"] + b + 1)
                        act.wait_ge(part_used.sem, m["pused"] + 2 * b - 2)
                        for c in range(2):
                            ins = act.activation(u[slot][:, c, 2:S + 2], bank[2 * slot + c][:, :], ACT.Copy)
                        ins.then_inc(evacuated.sem, 1)

                    def late_act(act, b, slot, m):
                        act.wait_ge(part_used.sem, m["pused"] + 2 * b + 1)
                        act.activation(z[slot][:, 0, :], z[slot][:, 0, :], ACT.Gelu_apprx_tanh).then_inc(gelu_ready.sem, 1)
                        act.wait_ge(hid_ready.sem, m["hid"] + 2 * b + 1)
                        act.activation(h_hi[:, bass.ds(b, 1), :], z[slot][:, 0:1, :], ACT.Copy).then_inc(part_ready.sem, 1)

                    def early_dve(dve, b, slot, m, tap=tap):
                        dve.wait_ge(evacuated.sem, m["evac"] + b + 1)
                        for c in range(2):
                            dve.tensor_scalar(z[slot][:, c, :], u[slot][:, c, 2:S + 2], tap(2, b, c), tap(3, b, c), ALU.mult, ALU.add)
                        dve.drain()
                        for c in range(2):
                            dve.scalar_tensor_tensor(z[slot][:, c, :], u[slot][:, c, 1:S + 1], tap(1, b, c), z[slot][:, c, :], ALU.mult, ALU.add)
                        dve.drain()
                        for c in range(2):
                            dve.scalar_tensor_tensor(z[slot][:, c, :], u[slot][:, c, 0:S], tap(0, b, c), z[slot][:, c, :],
                                                     ALU.mult, ALU.add).then_inc(part_used.sem, 1)

                    def late_dve(dve, b, slot, m):
                        dve.wait_ge(part_used.sem, m["pused"] + 2 * b + 2)
                        dve.wait_ge(gelu_ready.sem, m["gelu"] + b + 1)
                        dve.tensor_tensor(z[slot][:, 0, :], z[slot][:, 0, :], z[slot][:, 1, :], ALU.mult).then_inc(hid_ready.sem, 1)
                        dve.wait_ge(hid_ready.sem, m["hid"] + 2 * b + 1)
                        dve.wait_ge(part_ready.sem, m["part"] + b + 1)
                        dve.tensor_tensor(h_lo[:, bass.ds(b, 1), :], z[slot][:, 0:1, :], h_hi[:, bass.ds(b, 1), :].bitcast(F32),
                                          ALU.subtract).then_inc(hid_ready.sem, 1)
                    b_hid = hid_ready.n
                    stages.append(dense(f"fu{l}{g}", two_chunks(a_tiles), early_dve, late_dve, early_act, late_act,
                                        tile_ready=ready if g == 0 else None))
                    part_used.n += 2 * n
                    hid_ready.n += 2 * n
                    part_ready.n += n
                    gelu_ready.n += n
                    final = g == len(FG) - 1
                    sq_act, sq_dve = sums_on_the_way(y) if final else (none, none)
                    stages.append(dense(f"fd{l}{g}", two_chunks(h_tiles[:n]), copy_to(y) if g == 0 else add_to(y), sq_dve, none, sq_act,
                                        tile_ready=(lambda b_hid: lambda k: (hid_ready.sem, b_hid + 2 * k + 2))(b_hid)))
                    if final:
                        squared.n += KT
                        summed.n += KT
                stages += [inverse_root(), update(9 + l, src=y, with_mean=l == 0)]
                run(*stages)

        def fox():
            with ExitStack() as ctx:
                gT = sb(ctx, "fx_g", [P, KT, S])
                with ExitStack() as inner:
                    kT = sb(inner, "fx_k", [P, 8, S])
                    qT = sb(inner, "fx_q", [P, 8, S])
                    v = sb(inner, "fx_v", [P, TT, FH * FD])
                    parts = sb(inner, "fx_parts", [P, S], BF16)
                    sel = sb(inner, "fx_sel", [P, FH * P], BF16)
                    with ExitStack() as tmp:
                        bias = sb(tmp, "fx_bias", [FH, 1])
                        lf, t1, t2, one = (sb(tmp, f"fx_{n}", [FH, S]) for n in ("lf", "t1", "t2", "one"))
                        b_in = inputs_in[0].n
                        inputs_in[0].n += 16

                        def bias_load(sp):
                            sp.dma_start(bias[:, :], io["kv_b_f_2"].rearrange("(h a) -> h a", a=1)).then_inc(inputs_in[0].sem, 16)

                        def v_rows(dve, grp, t):
                            return dve.tensor_copy(v[:, t, bass.ds(grp * 512, 512)], bank[4 + t][:, :])

                        def f_rows(dve, b, slot, m):
                            dve.wait_ge(products_done.sem, m["prod"] + b + 1)
                            dve.tensor_copy(lf[:, :], bank[2 * slot][0:FH, :]).then_inc(evacuated.sem, 1)
                        stage, ready = normalise(11)
                        stages = [{"sync": bias_load}, inverse_root_of_mean(), stage]
                        stages.append(dense("ff", [[[(k * P, a_tiles[k]) for k in range(KT)]]], f_rows, tile_ready=ready))
                        b_a, b_d, b_pool = act_step.n, dve_step.n, pool_step.n

                        def gate_pool(pool):
                            pool.memset(parts[:, :], 0.0).then_inc(pool_step.sem, 1)
                            pool.memset(sel[:, :], 0.0).then_inc(pool_step.sem, 1)
                            pool.wait_ge(pool_step.sem, b_pool + 2)
                            for j in range(3):
                                pool.tensor_copy(sel[32 * j:32 * j + FH, :].rearrange("p (h q) -> p h q", q=P),
                                                 ident[0:FH, 0:FH, None].broadcast_to([FH, FH, P]))

                        def gate_vector(dve):
                            dve.memset(one[:, :], 1.0)
                            dve.wait_ge(inputs_in[0].sem, b_in + 16)
                            dve.drain()
                            dve.tensor_scalar(lf[:, :], lf[:, :], bias[:, 0:1], None, ALU.add)
                            dve.drain()
                            log_sigmoid(None, dve, lf[:, :], t1[:, :], t2[:, :], b_a, b_d, "dve")
                            dve.tensor_tensor_scan(t2[:, :], one[:, :], lf[:, :], 0.0, ALU.mult, ALU.add)
                            dve.drain()
                            dve.tensor_scalar(t1[:, :], t2[:, :], -1.0, None, ALU.mult)
                            dve.wait_ge(pool_step.sem, b_pool + 1)
                            dve.drain()
                            for j in range(3):
                                rows = slice(32 * j, 32 * j + FH)
                                dve.tensor_copy(parts[rows, :], t1[:, :])
                                dve.drain()
                                if j < 2:
                                    dve.tensor_copy(t2[:, :], parts[rows, :])
                                    dve.drain()
                                    dve.tensor_tensor(t1[:, :], t1[:, :], t2[:, :], ALU.subtract)
                                    dve.drain()

                        def gate_scalar(act):
                            log_sigmoid(act, None, lf[:, :], t1[:, :], t2[:, :], b_a, b_d, "act")
                        stages.append({"gpsimd": gate_pool, "vector": gate_vector, "scalar": gate_scalar})
                        act_step.n += 1
                        dve_step.n += 1
                        pool_step.n += 2
                        stages.append(dense("fk", two_chunks(a_tiles), copy_to(kT)))
                        stages.append(dense_rows("fv", evac_dve=v_rows))

                        def gates(act, b, slot, m):
                            act.wait_ge(products_done.sem, m["prod"] + b + 1)
                            for c in range(2):
                                ins = act.activation(gT[:, bass.ds(b * 2 + c, 1), :], bank[2 * slot + c][:, None, :], ACT.Sigmoid)
                            ins.then_inc(evacuated.sem, 1)
                        stage, ready = normalise(4)
                        stages.append(stage)
                        stages.append(dense("fq", two_chunks(a_tiles), copy_to(qT, float(FD) ** -0.5), tile_ready=ready))
                        stages.append(dense("fg", two_chunks(a_tiles), early_act=gates))
                        run(*stages)

                    def finish(dve, c, p, outs):
                        pair = gT[:, bass.ds(c * 2 + p, 1), :]
                        return dve.tensor_tensor(pair, bank[6 + p][:, None, :], pair, ALU.mult)
                    attention("fox", FH // 4, lambda c, p: qT[:, bass.ds(c * 2 + p, 1), :], lambda c, p: kT[:, bass.ds(c * 2 + p, 1), :],
                              lambda c, p: v[:, :, bass.ds(c * (2 * P) + p * P, P)], False, (a_hi, a_lo), None, finish, False,
                              key_bias=(sel, parts))
                post_norm_dense("fout", 6, a_tiles, gT)

        def store():
            with ExitStack() as ctx:
                rows = sb(ctx, "out_rows", [P, TT, D])
                b_t, b_o = turned.n, turned_out.n
                with nc.Block() as block:
                    @block.tensor
                    def _(pe):
                        for t in range(TT):
                            for h in range(2):
                                n = 2 * t + h
                                if n >= 4:
                                    pe.wait_ge(turned_out.sem, b_o + n - 3)
                                for k in range(4):
                                    last = pe.transpose(bank[n % 4][:, k * P:(k + 1) * P], xT[:, 4 * h + k, t * P:(t + 1) * P], ident)
                                last.then_inc(turned.sem, 1)

                    @block.vector
                    def _(dve):
                        for n in range(2 * TT):
                            dve.wait_ge(turned.sem, b_t + n + 1)
                            dve.tensor_copy(rows[:, n // 2, (n % 2) * 512:(n % 2 + 1) * 512], bank[n % 4][:, :]).then_inc(turned_out.sem, 1)

                    @block.sync
                    def _(sp):
                        for t in range(TT):
                            sp.wait_ge(turned_out.sem, b_o + 2 * t + 2)
                            sp.dma_start(io["out"][0, t * P:(t + 1) * P, :], rows[:, t, :]).then_inc(stored.sem, 16)
                        sp.wait_ge(stored.sem, 16 * TT)

        setup()
        first_block()
        mlstm()
        ffn(0)
        fox()
        ffn(1)
        store()


_INS = ["x", "positions", "norm_mix", "w_in", "cmp_pos_k", "cmp_pos_v", "cmp_k_w1", "cmp_k_w2", "cmp_v_w1", "cmp_v_w2",
        "w_proj_a", "w_proj_b", "w_out", "norm_mlp", "w_up", "w_down", "norm_final", "norm_mix_pre_2", "norm_mix_post_2",
        "norm_ffn_pre_2", "norm_ffn_post_2", "mlstm_w_in_2", "mlstm_b_gate_2", "mlstm_norm_2", "mlstm_w_out_2", "kv_norm_2",
        "kv_w_2", "kv_b_f_2", "fox_w_qg_2", "fox_w_out_2", "ffn_w_up_2", "ffn_conv_w_2", "ffn_conv_b_2", "ffn_w_down_2"]


def kernel(**inputs):
    import concourse.bacc as _bacc
    from concourse.bass_utils import run_bass_kernel_spmd as _run

    nc = _bacc.Bacc("TRN2", target_bir_lowering=False, num_devices=1)
    packed, at, decay = shape_constants()
    arrays, io = {}, {}

    def give(name, a):
        arrays[f"in_{name}"] = a
        io[name] = nc.dram_tensor(f"in_{name}", a.shape, mybir.dt.from_np(a.dtype), kind="ExternalInput").ap()

    for name in _INS:
        give(name, np.ascontiguousarray(inputs[name]))
    give("const", packed)
    give("decay", decay)
    io["row_scratch"] = nc.dram_tensor("row_scratch", (FH, S), F32, kind="Internal").ap()
    io["out"] = nc.dram_tensor("out_x", (1, S, D), F32, kind="ExternalOutput").ap()
    build(nc, io, at)
    r = _run(nc, [arrays], core_ids=[0])
    return r.results[0]["out_x"]
```
